# Optimizing a Trainium2 kernel written in Bass

```python
import math
import jax, jax.numpy as jnp
from jax import lax
import numpy as np

D_MODEL = 1024
BATCH = 1
SEQ = 256
DEPTH = 1

MLSTM_HEADS = 4
MLSTM_WIDTH = D_MODEL
MLSTM_HEAD_DIM = MLSTM_WIDTH // MLSTM_HEADS
MLSTM_CHUNK = 64
CONV_WIDTH = 4
ATTN_PATTERNS = ((128, 1), (512, 4), (2048, 16))
ATTN_GROUP_HEADS = 4
ATTN_HEAD_DIM = 128
ATTN_HEADS = ATTN_GROUP_HEADS * len(ATTN_PATTERNS)
ATTN_WIDTH = ATTN_HEADS * ATTN_HEAD_DIM
ATTN_OUT_WIDTH = ATTN_GROUP_HEADS * ATTN_HEAD_DIM
ATTN_BLOCK = 128
ALIBI_MAX_BIAS = 8.0
N_EXPERTS = 16
N_EXPERT_GROUPS = 4
EXPERTS_PER_GROUP = N_EXPERTS // N_EXPERT_GROUPS
TOP_K = 2
D_FF_EXPERT = 512
IN_SPLITS = (MLSTM_WIDTH, MLSTM_WIDTH, MLSTM_WIDTH, MLSTM_WIDTH, 2 * MLSTM_HEADS,
             ATTN_WIDTH, ATTN_WIDTH, ATTN_WIDTH, D_MODEL, D_MODEL)
IN_COLS = sum(IN_SPLITS)
EPS = 1e-6

kernel_name = "hybrid_mlstm_dilated_alibi_moe_block"

def rms_norm(x, g):
    xf = x.astype(jnp.float32)
    y = xf * lax.rsqrt(jnp.mean(xf * xf, axis=-1, keepdims=True) + EPS)
    return (y * g.astype(jnp.float32)).astype(x.dtype)

def modulate(h, shift, scale):
    return h * (1.0 + scale[:, None, :]) + shift[:, None, :]

def causal_depthwise_conv(x, w):
    k_w, ch = w.shape
    return lax.conv_general_dilated(
        x, w[:, None, :].astype(x.dtype), window_strides=(1,), padding=[(k_w - 1, 0)],
        dimension_numbers=("NWC", "WIO", "NWC"), feature_group_count=ch)

def mlstm_chunkwise(q, k, v, i_pre, f_pre):
    B, S, H, Dh = q.shape
    L = MLSTM_CHUNK
    NC = S // L
    f32 = jnp.float32

    def to_chunks(t):
        return t.astype(f32).reshape(B, NC, L, H, Dh).transpose(1, 0, 3, 2, 4)

    def gates_to_chunks(t):
        return t.astype(f32).reshape(B, NC, L, H).transpose(1, 0, 3, 2)

    qc = to_chunks(q) * (Dh ** -0.5)
    kc = to_chunks(k)
    vc = to_chunks(v)
    lic = gates_to_chunks(i_pre)
    lfc = jax.nn.log_sigmoid(gates_to_chunks(f_pre))
    causal = jnp.tril(jnp.ones((L, L), dtype=bool))

    def step(carry, inp):
        C, n, m = carry
        qb, kb, vb, li, lf = inp
        b = jnp.cumsum(lf, axis=-1)
        dmat = jnp.where(causal, b[..., :, None] - b[..., None, :] + li[..., None, :], -jnp.inf)
        inter = b + m[..., None]
        m_t = jnp.maximum(inter, jnp.max(dmat, axis=-1))
        w = jnp.exp(dmat - m_t[..., None])
        a_inter = jnp.exp(inter - m_t)
        s = jnp.einsum("bhtd,bhsd->bhts", qb, kb) * w
        num = jnp.einsum("bhts,bhsd->bhtd", s, vb) + a_inter[..., None] * jnp.einsum("bhtd,bhde->bhte", qb, C)
        den = jnp.sum(s, axis=-1) + a_inter * jnp.einsum("bhtd,bhd->bht", qb, n)
        h = num / jnp.maximum(jnp.abs(den), jnp.exp(-m_t))[..., None]
        b_last = b[..., -1]
        g = b_last[..., None] - b + li
        m_new = jnp.maximum(b_last + m, jnp.max(g, axis=-1))
        ws = jnp.exp(g - m_new[..., None])
        decay = jnp.exp(b_last + m - m_new)
        kw = kb * ws[..., None]
        C_new = decay[..., None, None] * C + jnp.einsum("bhsd,bhse->bhde", kw, vb)
        n_new = decay[..., None] * n + jnp.sum(kw, axis=2)
        return (C_new, n_new, m_new), h

    init = (jnp.zeros((B, H, Dh, Dh), f32), jnp.zeros((B, H, Dh), f32), jnp.zeros((B, H), f32))
    _, h = lax.scan(step, init, (qc, kc, vc, lic, lfc))
    return h.transpose(1, 0, 3, 2, 4).reshape(B, S, H, Dh)

def dilated_window_attention(q, k, v, window, dilation, slopes):
    B, S, H, Dh = q.shape
    d = dilation
    n_back = window // d
    Lsub = S // d
    blk = ATTN_BLOCK
    nb = -(-Lsub // blk)
    Lp = nb * blk
    f32 = jnp.float32

    def to_blocks(t):
        t = t.astype(f32).reshape(B, Lsub, d, H, Dh)
        t = jnp.pad(t, ((0, 0), (0, Lp - Lsub), (0, 0), (0, 0), (0, 0)))
        return t.reshape(B, nb, blk, d, H, Dh)

    qb = to_blocks(q)
    kb = to_blocks(k)
    vb = to_blocks(v)
    pad_prev = ((0, 0), (1, 0), (0, 0), (0, 0), (0, 0), (0, 0))
    kk = jnp.concatenate([jnp.pad(kb, pad_prev)[:, :-1], kb], axis=2)
    vv = jnp.concatenate([jnp.pad(vb, pad_prev)[:, :-1], vb], axis=2)
    scores = jnp.einsum("bnqrhd,bnkrhd->bnrhqk", qb, kk) * (Dh ** -0.5)

    qi = jnp.arange(blk)[:, None]
    kj = jnp.arange(2 * blk)[None, :]
    dist = blk + qi - kj
    key_pos = jnp.arange(nb)[:, None] * blk - blk + jnp.arange(2 * blk)[None, :]
    valid = ((dist >= 0) & (dist <= n_back))[None] & (key_pos >= 0)[:, None, :]
    valid = valid[:, None, None]
    alibi = -slopes.astype(f32)[:, None, None] * (dist * d).astype(f32)[None]
    scores = jnp.where(valid, scores + alibi, -jnp.inf)
    lse = jax.nn.logsumexp(scores, axis=-1)
    p = jnp.exp(scores - lse[..., None])
    out = jnp.einsum("bnrhqk,bnkrhd->bnqrhd", p, vv)
    out = out.reshape(B, Lp, d, H, Dh)[:, :Lsub].reshape(B, S, H, Dh)
    lse = lse.transpose(0, 1, 4, 2, 3).reshape(B, Lp, d, H)[:, :Lsub].reshape(B, S, H)
    return out, lse

def mixer(u, w_in, conv_w, gate_b, norm_g, w_branch_m, w_branch_a, w_out):
    B, S, _ = u.shape
    proj = u @ w_in
    idx = [int(i) for i in np.cumsum(IN_SPLITS)[:-1]]
    q_m, k_m, v_m, o_m, if_m, q_a, k_a, v_a, g_m, g_a = jnp.split(proj, idx, axis=-1)

    qk = jax.nn.silu(causal_depthwise_conv(jnp.concatenate([q_m, k_m], axis=-1), conv_w))
    q_m, k_m = jnp.split(qk, 2, axis=-1)
    heads = lambda t: t.reshape(B, S, MLSTM_HEADS, MLSTM_HEAD_DIM)
    if_m = if_m + gate_b
    i_pre, f_pre = if_m[..., :MLSTM_HEADS], if_m[..., MLSTM_HEADS:]
    hm = mlstm_chunkwise(heads(q_m), heads(k_m), heads(v_m), i_pre, f_pre)
    hm = hm * lax.rsqrt(jnp.mean(hm * hm, axis=-1, keepdims=True) + EPS)
    hm = hm.reshape(B, S, MLSTM_WIDTH) * norm_g.astype(jnp.float32)
    h_m = (jax.nn.sigmoid(o_m.astype(jnp.float32)) * hm).astype(u.dtype)

    ahead = lambda t: t.reshape(B, S, ATTN_HEADS, ATTN_HEAD_DIM)
    q_a, k_a, v_a = ahead(q_a), ahead(k_a), ahead(v_a)
    slopes = 2.0 ** (-ALIBI_MAX_BIAS * jnp.arange(1, ATTN_HEADS + 1, dtype=jnp.float32) / ATTN_HEADS)
    outs, lses = [], []
    for gi, (win, dil) in enumerate(ATTN_PATTERNS):
        hs = slice(gi * ATTN_GROUP_HEADS, (gi + 1) * ATTN_GROUP_HEADS)
        o_g, l_g = dilated_window_attention(q_a[:, :, hs], k_a[:, :, hs], v_a[:, :, hs], win, dil, slopes[hs])
        outs.append(o_g)
        lses.append(l_g)
    alpha = jax.nn.softmax(jnp.stack(lses, axis=0), axis=0)
    h_a = jnp.einsum("gbsh,gbshd->bshd", alpha, jnp.stack(outs, axis=0))
    h_a = h_a.reshape(B, S, ATTN_OUT_WIDTH).astype(u.dtype)

    y = jax.nn.sigmoid(g_m) * (h_m @ w_branch_m) + jax.nn.sigmoid(g_a) * (h_a @ w_branch_a)
    return y @ w_out

def moe(u, router_w, router_b, w_gate, w_up, w_down):
    B, S, D = u.shape
    xt = u.reshape(B * S, D)
    scores = jax.nn.sigmoid(xt.astype(jnp.float32) @ router_w.astype(jnp.float32))
    sel = scores + router_b.astype(jnp.float32)
    grp = sel.reshape(-1, N_EXPERT_GROUPS, EXPERTS_PER_GROUP)
    group_score = jnp.sum(lax.top_k(grp, TOP_K)[0], axis=-1)
    best_group = jnp.argmax(group_score, axis=-1)
    in_group = jnp.repeat(jax.nn.one_hot(best_group, N_EXPERT_GROUPS, dtype=jnp.float32) > 0,
                          EXPERTS_PER_GROUP, axis=-1)
    _, top_idx = lax.top_k(jnp.where(in_group, sel, -jnp.inf), TOP_K)
    top_s = jnp.take_along_axis(scores, top_idx, axis=-1)
    weights = top_s / jnp.sum(top_s, axis=-1, keepdims=True)
    combine = jnp.sum(jax.nn.one_hot(top_idx, N_EXPERTS, dtype=jnp.float32) * weights[..., None], axis=1)
    combine = combine.astype(u.dtype)
    out = jnp.zeros_like(xt)
    for e in range(N_EXPERTS):
        he = jax.nn.silu(xt @ w_gate[e]) * (xt @ w_up[e])
        out = out + combine[:, e:e + 1] * (he @ w_down[e])
    return out.reshape(B, S, D)

def setup_inputs(seed: int = 0) -> dict:
    key = jax.random.key(seed)
    ks = jax.random.split(key, 24)
    nrm = lambda k, shape, s: jax.random.normal(k, shape, jnp.float32) * s
    D, H = D_MODEL, MLSTM_HEADS
    i_b = nrm(ks[5], (DEPTH, H), 0.1)
    f_b = jnp.linspace(3.0, 6.0, H, dtype=jnp.float32)[None, :] + nrm(ks[6], (DEPTH, H), 0.1)
    return {
        "x": nrm(ks[0], (BATCH, SEQ, D), 1.0),
        "c": nrm(ks[1], (BATCH, D), 1.0),
        "ada_w": nrm(ks[2], (DEPTH, D, 6 * D), 0.5 * D ** -0.5),
        "ada_b": nrm(ks[3], (DEPTH, 6 * D), 0.02),
        "w_in": nrm(ks[4], (DEPTH, D, IN_COLS), D ** -0.5),
        "mlstm_conv": nrm(ks[7], (DEPTH, CONV_WIDTH, 2 * MLSTM_WIDTH), CONV_WIDTH ** -0.5),
        "mlstm_gate_b": jnp.concatenate([i_b, f_b], axis=-1),
        "mlstm_norm_g": 1.0 + nrm(ks[8], (DEPTH, MLSTM_WIDTH), 0.02),
        "w_branch_m": nrm(ks[9], (DEPTH, MLSTM_WIDTH, D), MLSTM_WIDTH ** -0.5),
        "w_branch_a": nrm(ks[10], (DEPTH, ATTN_OUT_WIDTH, D), ATTN_OUT_WIDTH ** -0.5),
        "w_out": nrm(ks[11], (DEPTH, D, D), D ** -0.5),
        "router_w": nrm(ks[12], (D, N_EXPERTS), D ** -0.5),
        "router_b": nrm(ks[13], (N_EXPERTS,), 0.01),
        "w_gate_e": nrm(ks[14], (DEPTH, N_EXPERTS, D, D_FF_EXPERT), D ** -0.5),
        "w_up_e": nrm(ks[15], (DEPTH, N_EXPERTS, D, D_FF_EXPERT), D ** -0.5),
        "w_down_e": nrm(ks[16], (DEPTH, N_EXPERTS, D_FF_EXPERT, D), D_FF_EXPERT ** -0.5),
        "norm_mix_g": 1.0 + nrm(ks[17], (DEPTH, D), 0.02),
        "norm_ffn_g": 1.0 + nrm(ks[18], (DEPTH, D), 0.02),
        "final_norm_g": 1.0 + nrm(ks[19], (D,), 0.02),
    }

def reference(x, c, ada_w, ada_b, w_in, mlstm_conv, mlstm_gate_b, mlstm_norm_g, w_branch_m,
              w_branch_a, w_out, router_w, router_b, w_gate_e, w_up_e, w_down_e,
              norm_mix_g, norm_ffn_g, final_norm_g):
    c_act = jax.nn.silu(c)
    for l in range(DEPTH):
        mod = c_act @ ada_w[l] + ada_b[l]
        sh_a, sc_a, gt_a, sh_f, sc_f, gt_f = jnp.split(mod, 6, axis=-1)
        u = modulate(rms_norm(x, norm_mix_g[l]), sh_a, sc_a)
        x = x + gt_a[:, None, :] * mixer(u, w_in[l], mlstm_conv[l], mlstm_gate_b[l], mlstm_norm_g[l],
                                         w_branch_m[l], w_branch_a[l], w_out[l])
        u = modulate(rms_norm(x, norm_ffn_g[l]), sh_f, sc_f)
        x = x + gt_f[:, None, :] * moe(u, router_w, router_b, w_gate_e[l], w_up_e[l], w_down_e[l])
    return rms_norm(x, final_norm_g)


_drawn_inputs = setup_inputs


def setup_inputs(seed=0):
    import zlib

    import numpy as np

    out = dict(_drawn_inputs(seed))
    spreads = {}
    factors = {'mlstm_norm_g': 8.0, 'norm_mix_g': 5.663, 'norm_ffn_g': 2.811, 'final_norm_g': 2.838}
    for name, (base, spread) in spreads.items():
        noise = np.random.default_rng([zlib.crc32(name.encode()), seed]).standard_normal(out[name].shape)
        drawn = base * np.exp(spread * noise) if base else spread * noise
        out[name] = __import__('jax').numpy.asarray(drawn.astype(out[name].dtype))
    for name, factor in factors.items():
        out[name] = (out[name] * factor).astype(out[name].dtype)
    return out
```

```python
import math
from contextlib import ExitStack

import concourse.bass as bass
from concourse import mybir

ALU = mybir.AluOpType
ACT = mybir.ActivationFunctionType
F32 = mybir.dt.float32
F32R = mybir.dt.float32r
I32 = mybir.dt.int32
AX_X = mybir.AxisListType.X

P = 128
D = 1024
KT = D // P
T = 256
TT = T // P
NB = 512
KB = 4
EPS = 1e-6
NEG = -1e30
MH, MD = 4, 256
AH, AD, AG = 12, 128, 3
AM = AH // AG
PATTERNS = ((128, 1), (512, 4), (2048, 16))
NE, FF = 16, 512
GROUPS, PER = 4, 4
SLOTS = 64
VISITS = T // SLOTS
RAW, RING = 4, 3
IF_AT = 4 * D
IF_N = 2 * MH

IN_GROUPS = (
    [("qk", c, True) for c in range(0, 2 * D, NB)]
    + [("vm", c, False) for c in range(2 * D, 3 * D, NB)]
    + [("qa", c, True) for c in range(IF_AT + IF_N, IF_AT + IF_N + 1536, NB)]
    + [("ka", c, True) for c in range(IF_AT + IF_N + 1536, IF_AT + IF_N + 3072, NB)]
    + [("va", c, False) for c in range(IF_AT + IF_N + 3072, IF_AT + IF_N + 4608, NB)]
    + [("o", c, False) for c in range(3 * D, 4 * D, NB)]
    + [("gm", c, True) for c in range(IF_AT + IF_N + 4608, IF_AT + IF_N + 4608 + D, NB)]
    + [("ga", c, True) for c in range(IF_AT + IF_N + 4608 + D, IF_AT + IF_N + 4608 + 2 * D, NB)]
)
GROUP_LIST = IN_GROUPS + [("bm", 0, True), ("bm", NB, True), ("ba", 0, True), ("ba", NB, True),
                          ("wo", 0, False), ("wo", NB, False)]
BLOCKS = []
for _g, (_kind, _c, _cm) in enumerate(GROUP_LIST):
    _halves = 1 if _kind == "ba" else 2
    for _h in range(_halves):
        BLOCKS.append((_g, _h * KB, _h == 0, _h == _halves - 1))
LAST_BLOCK = {g: b for b, (g, _, _, end) in enumerate(BLOCKS) if end}
NBLK = len(BLOCKS)
BLK_IN = 2 * len(IN_GROUPS)
AHEAD = RING - 1

GATES_AT, CUMSUM_AT, GATE_T_AT, GATE_BACK_AT = 1, 3, 5, 7
SCORE_M_AT = [12 + 2 * h for h in range(MH)]
VALUE_M_AT = [13 + 2 * h for h in range(MH)]
M_SCALE_AT = 20
SCORE_A_AT = [30, 33, 36, 39]
TURN_A_AT = [32, 35, 38, 41]
VALUE_A_AT = [33, 36, 39, 41]
M_OUT_AT = 34
M_TURN_AT = BLK_IN - 1
BCAST_AT = [43, 44, 45, 46]
ADA_FIRST = 8
ADA_REST = 16
ADA_AT = {s: ADA_FIRST + i for i, s in enumerate([8, 10, 12, 13, 15, 16, 18, 19, 21, 22, 24, 25, 27, 28, 29, 31])}

STREAM = [("ada", a) for a in range(ADA_FIRST)] + [("w", b) for b in range(AHEAD)]
for _s in range(NBLK):
    if _s + AHEAD < NBLK:
        STREAM.append(("w", _s + AHEAD))
    if _s in ADA_AT:
        STREAM.append(("ada", ADA_AT[_s]))
POS = {item: n for n, item in enumerate(STREAM)}


def build(nc, A, out):
    with ExitStack() as ctx:
        base = (nc.sbuf_base + 63) // 64 * 64
        ctx.enter_context(nc.sbuf_tensor("arena", [P, (nc.sbuf_usable_end - base) // 4 - 32], F32))
        K = 1024

        def at(name, kib, shape, dt=F32):
            return nc.alloc_sbuf_tensor_at(name, shape, dt, offset=base + int(kib * K))

        small_at = [192 * K]

        def small(name, shape, dt=F32):
            n = 4
            for s in shape[1:]:
                n *= s
            t = nc.alloc_sbuf_tensor_at(name, shape, dt, offset=base + small_at[0])
            small_at[0] += (n + 31) // 32 * 32
            assert base + small_at[0] <= nc.sbuf_usable_end - 256, (name, small_at[0])
            return t

        def sem(name):
            return ctx.enter_context(nc.semaphore(name))

        raw = [at(f"raw{i}", 8 * i, [P, KB, NB]) for i in range(RAW)]
        hi = [at(f"hi{i}", 32 + 8 * i, [P, KB, NB], F32R) for i in range(RING)]
        lo = [at(f"lo{i}", 56 + 8 * i, [P, KB, NB], F32R) for i in range(RING)]
        u_hi = at("u_hi", 80, [P, KT, T], F32R)
        u_lo = at("u_lo", 88, [P, KT, T], F32R)
        hm_hi = at("hm_hi", 80, [P, KT, T], F32R)
        hm_lo = at("hm_lo", 88, [P, KT, T], F32R)
        qk_m = at("qk_m", 96, [P, 2 * KT, T])
        v_m = at("v_m", 112, [P, TT, D])
        sig_o = at("sig_o", 96, [P, TT, D])
        sig_gm = at("sig_gm", 104, [P, KT, T])
        sig_ga = at("sig_ga", 112, [P, KT, T])
        acc_a = at("acc_a", 120, [P, 2 * D])
        u_f32 = at("u_f32", 128, [P, KT, T])
        q_a = at("q_a", 120, [P, AH, T])
        k_a = at("k_a", 132, [P, AH, T])
        v_a = at("v_a", 144, [P, TT, AH * AD])
        hm_f32 = at("hm_f32", 120, [P, KT, T])
        y_hi = at("y_hi", 120, [P, KT, T], F32R)
        y_lo = at("y_lo", 128, [P, KT, T], F32R)
        x_in = at("x_in", 156, [P, TT, D])
        prob = at("prob", 156, [P, 1152])
        ha_hi = at("ha_hi", 156, [P, AM, T], F32R)
        ha_lo = at("ha_lo", 160, [P, AM, T], F32R)
        h_m = at("h_m", 164, [P, TT, D])
        x_res = at("x_res", 164, [P, TT, D])
        mod = at("mod", 172, [P, 4, D])
        ha_f32 = at("ha_f32", 188, [P, AM, T])
        w_gate = [at("w_gate0", 0, [P, KT, FF]), at("w_gate1", 32, [P, KT, FF])]
        w_up = [at("w_up0", 16, [P, KT, FF]), at("w_up1", 48, [P, KT, FF])]
        w_down = [at("w_down0", 140, [P, FF // P, D]), at("w_down1", 64, [P, FF // P, D])]
        fin_g = at("fin_g", 80, [P, D])
        xe_t = at("xe_t", 84, [P, KT, SLOTS])
        onehot = at("onehot", 86, [P, TT, 2 * SLOTS])
        scat = [at("scat0", 87, [P, T + 1]), at("scat1", 88.5, [P, T + 1])]
        sg = at("sg", 90, [P, FF])
        he = at("he", 92, [P, FF])
        he_t = at("he_t", 94, [P, FF // P, SLOTS])
        u_ffn = at("u_ffn", 96, [P, TT, D])
        u_ffn_t = at("u_ffn_t", 104, [P, KT, T])
        scratch = at("scratch", 112, [P, TT, D])
        y_e = at("y_e", 120, [P, NB])
        zeros = at("zeros", 122, [P, NB])
        slot_tab = at("slot_tab", 124, [P, TT, VISITS * NE + 1])
        comb_tab = at("comb_tab", 125, [P, TT, VISITS * NE + 1])
        rt = at("rt", 126, [P, 24, TT, NE])

        ident = small("ident", [P, P])
        ones = small("ones", [P, P])
        tri_le = small("tri_le", [P, P])
        neg_tri = small("neg_tri", [P, P])
        turned = small("turned", [P, AG, 384])
        dist = small("dist", [P, T])
        masks = small("masks", [P, AG, T])
        bias_a = small("bias_a", [P, T])
        slot_id = bias_a[:, 0:2 * SLOTS]
        tri_lt = bias_a[:, 128:256]
        w_m = turned[:, 0, :]
        p_m = turned[:, 1, :]
        dist_i = turned[:, 2, 0:T].bitcast(I32)
        dist_m = turned[:, 0, 0:T].bitcast(I32)
        g_ffn = turned[:].rearrange("p a b -> p (a b)")[:, 0:D]
        vec = small("vec", [P, 80])
        rows = turned[:, 1, 0:P]
        cs = small("cs", [P, KT])
        st = small("st", [P, 40])
        chan = small("chan", [P, 3, KT])
        w_if = small("w_if", [P, KT, IF_N])
        wif_hi = small("wif_hi", [P, KT, IF_N], F32R)
        wif_lo = small("wif_lo", [P, KT, IF_N], F32R)
        gate_b = small("gate_b", [P, IF_N])
        gm = small("gm", [P, 12, TT, MH])
        neg_row = h_m[0:MH, 0, 0:T]
        run_row = small("run_row", [MH, T])
        am = small("am", [P, 8])
        rw = small("rw", [P, KT, NE])
        rb = small("rb", [P, NE])
        many = small("many", [P, 2])
        many_i = small("many_i", [P, 2], I32)

        ps = [ctx.enter_context(nc.psum_tensor(f"ps{i}", [P, 512], F32)) for i in range(8)]

        x_loaded, c_loaded, rows_loaded, small_loaded, bias_loaded = (sem(n) for n in (
            "x_loaded", "c_loaded", "rows_loaded", "small_loaded", "bias_loaded"))
        raw_loaded = [sem(f"raw_loaded{i}") for i in range(RAW)]
        ada_done = sem("ada_done")
        hi_ready, lo_ready, block_done = sem("hi_ready"), sem("lo_ready"), sem("block_done")
        evac_act, evac_dve = sem("evac_act"), sem("evac_dve")
        consts_ready, acc_zero = sem("consts_ready"), sem("acc_zero")
        pool_step, act_step, dve_step = sem("pool_step"), sem("act_step"), sem("dve_step")
        pe_side, act_side, dve_side = sem("pe_side"), sem("act_side"), sem("dve_side")
        qk_ready = sem("qk_ready")
        g_ffn_loaded, x_again, fin_loaded = sem("g_ffn_loaded"), sem("x_again"), sem("fin_loaded")
        gate_loaded = [sem("gate_loaded0"), sem("gate_loaded1")]
        up_loaded = [sem("up_loaded0"), sem("up_loaded1")]
        down_loaded = [sem("down_loaded0"), sem("down_loaded1")]
        onehot_ready, gathered, xe_ready, scat_ready = (sem(n) for n in (
            "onehot_ready", "gathered", "xe_ready", "scat_ready"))
        gate_up_done, sg_ready, he_ready, he_turned, he_t_ready, down_done, y_ready, scattered = (sem(n) for n in (
            "gate_up_done", "sg_ready", "he_ready", "he_turned", "he_t_ready", "down_done", "y_ready", "scattered"))
        moe_done, out_ready, stored = (sem(n) for n in ("moe_done", "out_ready", "stored"))

        order = {"pe": [], "act": [], "dve": []}

        def plan():
            pe, act, dve = order["pe"], order["act"], order["dve"]
            pe += ["vec_t", "x_t", "mod_col"]
            act += ["c_silu", "x_ss", "x_sqrt", "wif_hi", "u_hi"]
            dve += ["x_var", "x_norm", "vec", "mod_acc", "u_f32", "wif_lo", "u_lo", "masks"]
            for s in range(NBLK):
                if s == GATES_AT:
                    pe.append("gates"); dve.append("gate_abs"); act += ["gate_exp", "gate_ln"]
                    dve += ["gate_1p", "lf"]
                if s == CUMSUM_AT:
                    pe.append("cumsum"); dve.append("neg_g")
                if s == GATE_T_AT:
                    pe.append("gate_t"); dve.append("run_min")
                if s == GATE_BACK_AT:
                    pe.append("gate_back"); dve.append("m_neg"); act.append("floor")
                if s in SCORE_M_AT:
                    h = SCORE_M_AT.index(s)
                    pe.append(f"m_score{h}"); dve.append(f"m_log{h}"); act.append(f"m_exp{h}"); dve.append(f"m_p{h}")
                if s in VALUE_M_AT:
                    h = VALUE_M_AT.index(s)
                    pe.append(f"m_val{h}"); act.append(f"m_num{h}")
                if s == M_SCALE_AT:
                    dve.append("m_var"); act.append("m_sqrt"); dve.append("m_scale")
                if s in TURN_A_AT:
                    h = TURN_A_AT.index(s)
                    pe.append(f"a_turn{h}"); act.append(f"a_turned{h}")
                if s in VALUE_A_AT:
                    h = VALUE_A_AT.index(s)
                    pe.append(f"a_val{h}"); act.append(f"a_out{h}")
                if s in SCORE_A_AT:
                    h = SCORE_A_AT.index(s)
                    pe.append(f"a_score{h}"); dve.append(f"a_max{h}"); act.append(f"a_exp{h}"); dve.append(f"a_prob{h}")
                if s == M_OUT_AT:
                    dve.append("h_m")
                if s == M_TURN_AT:
                    pe.append("hm_t"); dve.append("hm_f32"); act.append("hm_hi"); dve.append("hm_lo")
                    act.append("ha_hi"); dve.append("ha_lo")
                if s in BCAST_AT:
                    i = BCAST_AT.index(s)
                    pe.append(f"bcast{i}"); act.append(f"mod{i}")
                if s == BCAST_AT[-1]:
                    dve.append("scale_ffn")
                if s == LAST_BLOCK[24]:
                    dve.append("y_f32"); act.append("y_hi"); dve.append("y_lo")
            act += ["x1_ss", "x1_sqrt", "ufT_a", "ufT_b", "scores"]
            dve += ["x1", "x1_var", "u_ffn", "router", "ranks", "zero", "x2", "x2_var"]
            pe += ["u_ffn_t", "logits", "rank_sums", "acc_zeroed"]
            act += ["x2_ss", "x2_sqrt"]

        plan()
        side_sem = {"pe": pe_side, "act": act_side, "dve": dve_side}
        where = {n: (e, i + 1) for e, names in order.items() for i, n in enumerate(names)}
        made = {"pe": 0, "act": 0, "dve": 0}

        def after(eng, *events):
            for e in events:
                engine, count = where[e]
                eng.wait_ge(side_sem[engine], count)

        def event(ins, name):
            engine, count = where[name]
            made[engine] += 1
            assert made[engine] == count, (name, made[engine], count)
            ins.then_inc(side_sem[engine], 1)

        def stepper(eng, s):
            count = [0]

            def step(ins):
                count[0] += 1
                ins.then_inc(s, 1)
                eng.wait_ge(s, count[0])
            return step

        def evac_engine(g):
            return "dve" if GROUP_LIST[g][0] in ("qk", "bm", "ba", "wo") else "act"

        def evacuated(eng, g):
            e = evac_engine(g)
            n = sum(1 for x in range(g + 1) if evac_engine(x) == e)
            eng.wait_ge(evac_dve if e == "dve" else evac_act, n)

        def raw_here(eng, item):
            n = POS[item]
            eng.wait_ge(raw_loaded[n % RAW], 16 * (n // RAW + 1))
            return raw[n % RAW]

        def used_up(eng, item):
            kind, n = item
            eng.wait_ge(lo_ready if kind == "w" else ada_done, n + 1)

        def block_source(item):
            kind, n = item
            if kind == "ada":
                c, h = n // 2, n % 2
                return A["ada_w"][0].rearrange("(p k) n -> p k n", k=KT)[:, KB * h:KB * (h + 1), c * NB:(c + 1) * NB]
            g, k0, _, _ = BLOCKS[n]
            name, c, _ = GROUP_LIST[g]
            w = {"bm": "w_branch_m", "ba": "w_branch_a", "wo": "w_out"}.get(name, "w_in")
            return A[w][0].rearrange("(k p) n -> p k n", p=P)[:, k0:k0 + KB, c:c + NB]

        m_i, m_f, m_abs, m_lf, m_cum, m_ng, m_g, m_floor, m_den, m_ss, m_rec, m_tmp = range(12)
        block = ctx.enter_context(nc.Block())

        @block.sync
        def _(sp):
            sp.dma_start(cs[:], A["c"].rearrange("b (p k) -> (b p) k", k=KT)).then_inc(c_loaded, 16)
            sp.dma_start(x_in[:], A["x"][0].rearrange("(t p) n -> p t n", p=P)).then_inc(x_loaded, 16)
            for n, item in enumerate(STREAM):
                if n == 2:
                    sp.dma_start(rows[0:64, :], A["mlstm_conv"][0].rearrange("j (c p) -> (j c) p", p=P)).then_inc(rows_loaded, 16)
                    sp.dma_start(rows[64:72, :], A["norm_mix_g"][0].rearrange("(c p) -> c p", p=P)).then_inc(rows_loaded, 16)
                    sp.dma_start(rows[72:80, :], A["mlstm_norm_g"][0].rearrange("(c p) -> c p", p=P)).then_inc(rows_loaded, 16)
                    sp.dma_start(w_if[:], A["w_in"][0].rearrange("(k p) n -> p k n", p=P)[:, :, IF_AT:IF_AT + IF_N]).then_inc(small_loaded, 16)
                    sp.dma_start(gate_b[:], A["mlstm_gate_b"][0:1, :].broadcast_to([P, IF_N])).then_inc(small_loaded, 16)
                    sp.dma_start(rw[:], A["router_w"].rearrange("(k p) n -> p k n", p=P)).then_inc(small_loaded, 16)
                    sp.dma_start(rb[:], A["router_b"].rearrange("(a n) -> a n", a=1).broadcast_to([P, NE])).then_inc(small_loaded, 16)
                    sp.wait_ge(acc_zero, 2)
                    sp.dma_start(acc_a[0:1, :], A["ada_b"][0:1, 0:2 * D]).then_inc(bias_loaded, 16)
                    sp.dma_start(mod[0:1, :, :], A["ada_b"][0:1, 2 * D:6 * D].rearrange("a (m n) -> a m n", m=4)).then_inc(bias_loaded, 16)
                if n >= RAW:
                    used_up(sp, STREAM[n - RAW])
                sp.dma_start(raw[n % RAW][:], block_source(item)).then_inc(raw_loaded[n % RAW], 16)
                if item == ("w", BLK_IN + 4):
                    after(sp, "a_val3", "hm_t")
                    sp.dma_start(g_ffn, A["norm_ffn_g"][0:1, :].broadcast_to([P, D])).then_inc(g_ffn_loaded, 16)
                    sp.dma_start(x_res[:], A["x"][0].rearrange("(t p) n -> p t n", p=P)).then_inc(x_again, 16)

            wg = A["w_gate_e"][0].rearrange("e (k p) n -> p e k n", p=P)
            wu = A["w_up_e"][0].rearrange("e (k p) n -> p e k n", p=P)
            wd = A["w_down_e"][0].rearrange("e (k p) n -> p e k n", p=P)

            def load_expert(e, s):
                sp.dma_start(w_gate[s][:], wg[:, e, :, :]).then_inc(gate_loaded[s], 16)
                sp.dma_start(w_up[s][:], wu[:, e, :, :]).then_inc(up_loaded[s], 16)

            def load_down(e, s):
                sp.dma_start(w_down[s][:], wd[:, e, :, :]).then_inc(down_loaded[s], 16)

            load_down(0, 0)
            for item in STREAM[-RAW:]:
                used_up(sp, item)
            load_expert(0, 0)
            sp.wait_ge(block_done, NBLK)
            load_expert(1, 1)
            load_down(1, 1)
            sp.dma_start(fin_g[:], A["final_norm_g"].rearrange("(a n) -> a n", a=1).broadcast_to([P, D])).then_inc(fin_loaded, 16)
            with sp.Fori(0, NE // 2 - 1) as i:
                for s in range(2):
                    sp.wait_ge(gate_up_done, 2 * i + (s + 1))
                    load_expert(2 * i + (s + 2), s)
                    sp.wait_ge(down_done, 2 * i + (s + 1))
                    load_down(2 * i + (s + 2), s)
            after(sp, "ranks")
            again = sp.value_load(many_i[0:1, 0:1], min_val=0, max_val=1)
            with sp.If(again == 1):
                with sp.Fori(1, VISITS) as v:
                    with sp.Fori(0, NE // 2) as i:
                        for s in range(2):
                            sp.wait_ge(gate_up_done, NE * v + 2 * i + (s - 1))
                            load_expert(2 * i + s, s)
                            sp.wait_ge(down_done, NE * v + 2 * i + (s - 1))
                            load_down(2 * i + s, s)
            for t in range(TT):
                sp.wait_ge(out_ready, t + 1)
                sp.dma_start(out[0, t * P:(t + 1) * P, :], scratch[:, t, :]).then_inc(stored, 16)
            sp.wait_ge(stored, 16 * TT)

        @block.gpsimd
        def _(pool):
            step = stepper(pool, pool_step)
            nc.gpsimd.memset(acc_a[:], 0.0).then_inc(acc_zero, 1)
            nc.gpsimd.memset(mod[:], 0.0).then_inc(acc_zero, 1)
            step(nc.gpsimd.memset(ones[:], 1.0))
            step(nc.gpsimd.memset(neg_tri[:], 0.0))
            nc.gpsimd.affine_select(out=ident[:], in_=neg_tri[:], compare_op=ALU.not_equal, fill=1.0, base=0,
                                    pattern=[[-1, P]], channel_multiplier=1).then_inc(consts_ready, 1)
            nc.gpsimd.affine_select(out=tri_le[:], in_=ones[:], compare_op=ALU.is_ge, fill=0.0, base=0,
                                    pattern=[[1, P]], channel_multiplier=-1).then_inc(consts_ready, 1)
            pool.wait_ge(consts_ready, 2)
            nc.gpsimd.affine_select(out=neg_tri[:], in_=neg_tri[:], compare_op=ALU.is_ge, fill=NEG, base=0,
                                    pattern=[[1, P]], channel_multiplier=-1).then_inc(consts_ready, 1)
            nc.gpsimd.iota(dist_i, pattern=[[-1, T]], base=P, channel_multiplier=1).then_inc(consts_ready, 1)
            after(pool, "a_prob3")
            nc.gpsimd.iota(slot_id, pattern=[[0, 2], [1, SLOTS]], base=0, channel_multiplier=0,
                           allow_small_or_imprecise_dtypes=True).then_inc(consts_ready, 1)
            nc.gpsimd.affine_select(out=tri_lt, in_=ones[:], compare_op=ALU.is_ge, fill=0.0, base=-1,
                                    pattern=[[1, P]], channel_multiplier=-1).then_inc(consts_ready, 1)

        @block.scalar
        def _(act):
            A_ = nc.scalar.activation
            step = stepper(act, act_step)

            def split_hi(b):
                src = raw_here(act, ("w", b))
                if b >= RING:
                    act.wait_ge(block_done, b - RING + 1)
                nc.scalar.copy(hi[b % RING][:], src[:]).then_inc(hi_ready, 1)

            act.wait_ge(c_loaded, 16)
            event(A_(cs[:], cs[:], ACT.Silu), "c_silu")
            act.wait_ge(x_loaded, 16)
            step(A_(h_m[:, 0, :], x_in[:, 0, :], ACT.Square, accum_out=st[:, 0:1]))
            event(A_(h_m[:, 0, :], x_in[:, 1, :], ACT.Square, accum_out=st[:, 1:2]), "x_ss")
            after(act, "x_var")
            event(A_(st[:, 4:6], st[:, 2:4], ACT.Sqrt), "x_sqrt")
            act.wait_ge(small_loaded, 64)
            event(nc.scalar.copy(wif_hi[:], w_if[:]), "wif_hi")
            for b in range(AHEAD):
                split_hi(b)
            after(act, "u_f32")
            event(nc.scalar.copy(u_hi[:], u_f32[:]), "u_hi")

            for s in range(NBLK):
                if s + AHEAD < NBLK:
                    split_hi(s + AHEAD)
                g, _, _, end = BLOCKS[s]
                kind, _, _ = GROUP_LIST[g]
                if end and kind == "qk":
                    evacuated(act, g)
                    A_(qk_m[:, 4 * g:4 * g + 4, :], qk_m[:, 4 * g:4 * g + 4, :], ACT.Silu).then_inc(qk_ready, 1)
                elif end and evac_engine(g) == "act":
                    act.wait_ge(block_done, s + 1)
                    first = min(x for x, (n, _, _) in enumerate(GROUP_LIST) if n == kind)
                    j = g - first
                    banks = 2 * (g % 2), 2 * (g % 2) + 1
                    func = ACT.Sigmoid if kind in ("o", "gm", "ga") else ACT.Copy
                    if kind == "o" and j == 0:
                        after(act, "m_val3")
                    if kind == "gm" and j == 0:
                        after(act, "m_val3")
                    if kind == "qa" and j == 0:
                        after(act, "u_lo")
                    dst = {"vm": v_m, "va": v_a, "o": sig_o, "qa": q_a, "ka": k_a, "gm": sig_gm, "ga": sig_ga}[kind]
                    for n, bank in enumerate(banks):
                        if kind in ("vm", "va", "o"):
                            view, src = dst[:, n, j * NB:(j + 1) * NB], ps[bank][:]
                        else:
                            view = dst[:, 4 * j + 2 * n:4 * j + 2 * n + 2, :]
                            src = ps[bank][:].rearrange("p (c t) -> p c t", c=2)
                        ins = A_(view, src, func)
                    ins.then_inc(evac_act, 1)

                if s == GATES_AT:
                    after(act, "gate_abs")
                    event(A_(gm[:, m_tmp], gm[:, m_abs], ACT.Exp, scale=-1.0), "gate_exp")
                    after(act, "gate_1p")
                    event(A_(gm[:, m_abs], gm[:, m_tmp], ACT.Ln), "gate_ln")
                if s == GATE_BACK_AT:
                    after(act, "m_neg")
                    event(A_(gm[:, m_floor], gm[:, m_tmp], ACT.Exp), "floor")
                if s in SCORE_M_AT:
                    h = SCORE_M_AT.index(s)
                    after(act, f"m_log{h}")
                    event(A_(w_m, w_m, ACT.Exp), f"m_exp{h}")
                if s in VALUE_M_AT:
                    h = VALUE_M_AT.index(s)
                    after(act, f"m_val{h}")
                    for t in range(TT):
                        nc.scalar.copy(gm[:, m_den, t, h:h + 1], ps[6 + t][:, MD:MD + 1])
                        nc.scalar.copy(h_m[:, t, h * MD:(h + 1) * MD], ps[6 + t][:, 0:MD])
                        ins = A_(bias_a[:], ps[6 + t][:, 0:MD], ACT.Square, accum_out=gm[:, m_ss, t, h:h + 1])
                        if t == 0:
                            step(ins)
                    event(ins, f"m_num{h}")
                if s == M_SCALE_AT:
                    after(act, "m_var")
                    event(A_(gm[:, m_tmp], gm[:, m_abs], ACT.Sqrt), "m_sqrt")
                if s in TURN_A_AT:
                    h = TURN_A_AT.index(s)
                    after(act, f"a_turn{h}")
                    for n in range(AG):
                        ins = nc.scalar.copy(turned[:, n, :], ps[4 + n][:, 0:384])
                    event(ins, f"a_turned{h}")
                if s in VALUE_A_AT:
                    h = VALUE_A_AT.index(s)
                    after(act, f"a_val{h}")
                    event(nc.scalar.copy(ha_f32[:, h, :], ps[7][:, 0:T]), f"a_out{h}")
                if s in SCORE_A_AT:
                    h = SCORE_A_AT.index(s)
                    after(act, f"a_max{h}")
                    A_(prob[:, 0:384], prob[:, 0:384], ACT.Exp, bias=am[:, 0:1], accum_out=am[:, 2:3])
                    event(A_(prob[:, 384:1152], prob[:, 384:1152], ACT.Exp, bias=am[:, 1:2], accum_out=am[:, 3:4]),
                          f"a_exp{h}")
                if s == M_TURN_AT:
                    after(act, "hm_f32")
                    event(nc.scalar.copy(hm_hi[:], hm_f32[:]), "hm_hi")
                    after(act, "a_out3")
                    event(nc.scalar.copy(ha_hi[:], ha_f32[:]), "ha_hi")
                if s in BCAST_AT:
                    i = BCAST_AT.index(s)
                    after(act, f"bcast{i}")
                    for n in range(2):
                        ins = nc.scalar.copy(mod[:, i, n * NB:(n + 1) * NB], ps[4 + 2 * (i % 2) + n][:])
                    event(ins, f"mod{i}")
                if s == LAST_BLOCK[24]:
                    after(act, "y_f32")
                    event(nc.scalar.copy(y_hi[:], sig_gm[:]), "y_hi")

            after(act, "x1")
            step(A_(scratch[:, 0, :], x_res[:, 0, :], ACT.Square, accum_out=st[:, 8:9]))
            event(A_(scratch[:, 0, :], x_res[:, 1, :], ACT.Square, accum_out=st[:, 9:10]), "x1_ss")
            after(act, "x1_var")
            event(A_(st[:, 12:14], st[:, 10:12], ACT.Sqrt), "x1_sqrt")
            after(act, "u_ffn_t")
            for n in range(4):
                ins = nc.scalar.copy(u_ffn_t[:, 2 * n:2 * n + 2, :], ps[4 + n][:].rearrange("p (c t) -> p c t", c=2))
                if n == 1:
                    event(ins, "ufT_a")
            event(ins, "ufT_b")
            after(act, "logits")
            event(A_(rt[:, 0], ps[0][:, 0:TT * NE].rearrange("p (t e) -> p t e", t=TT), ACT.Sigmoid), "scores")

            def evacuate_gather(n):
                act.wait_ge(gathered, n + 1)
                nc.scalar.copy(xe_t[:], ps[5][:].rearrange("p (k s) -> p k s", k=KT)).then_inc(xe_ready, 1)

            def visit(n):
                act.wait_ge(gate_up_done, n + 1)
                act.wait_ge(scat_ready, n + 2)
                A_(sg[64:128, :], ps[4][0:64, :], ACT.Silu).then_inc(sg_ready, 1)
                act.wait_ge(he_turned, n + 1)
                nc.scalar.copy(he_t[:], ps[6][:, 0:FF // P * SLOTS].rearrange("p (k s) -> p k s", k=FF // P)
                               ).then_inc(he_t_ready, 1)
                evacuate_gather(n + 1)

            evacuate_gather(0)
            with act.Fori(0, NE // 2) as i:
                for s in range(2):
                    visit(2 * i + s)
            after(act, "ranks")
            again = act.value_load(many_i[0:1, 0:1], min_val=0, max_val=1)
            with act.If(again == 1):
                with act.Fori(NE // 2, VISITS * NE // 2) as i:
                    for s in range(2):
                        visit(2 * i + s)

            after(act, "x2")
            step(A_(u_ffn[:, 0, :], x_res[:, 0, :], ACT.Square, accum_out=st[:, 16:17]))
            event(A_(u_ffn[:, 0, :], x_res[:, 1, :], ACT.Square, accum_out=st[:, 17:18]), "x2_ss")
            after(act, "x2_var")
            event(A_(st[:, 20:22], st[:, 18:20], ACT.Sqrt), "x2_sqrt")

        @block.vector
        def _(dve):
            V = nc.vector
            step = stepper(dve, dve_step)

            def split_lo(b):
                dve.wait_ge(hi_ready, b + 1)
                src = raw[POS[("w", b)] % RAW]
                V.tensor_tensor(lo[b % RING][:], src[:], hi[b % RING][:].bitcast(F32), ALU.subtract
                                ).then_inc(lo_ready, 1)

            def ada(a):
                src = raw_here(dve, ("ada", a))
                if a % 2:
                    dve.wait_ge(ada_done, a)
                col = (a // 2) * NB
                dst = acc_a[:, col:col + NB] if a < ADA_FIRST else (
                    mod[:, (col - 2 * D) // D, (col % D):(col % D) + NB])
                for k in range(KB):
                    kk = KB * (a % 2) + k
                    ins = V.scalar_tensor_tensor(out=dst, in0=src[:, k, :], scalar=cs[:, kk:kk + 1], in1=dst,
                                                 op0=ALU.mult, op1=ALU.add)
                    if k < KB - 1:
                        step(ins)
                    else:
                        ins.then_inc(ada_done, 1)
                if a == ADA_FIRST - 1:
                    dve.wait_ge(ada_done, ADA_FIRST)

            def inv_rms(ss, var, name):
                event(V.tensor_scalar(var, ss, 1.0 / D, EPS, ALU.mult, ALU.add), name)

            after(dve, "x_ss")
            inv_rms(st[:, 0:2], st[:, 2:4], "x_var")
            after(dve, "x_sqrt")
            step(V.reciprocal(st[:, 6:8], st[:, 4:6]))
            for t in range(TT):
                ins = V.tensor_scalar(x_in[:, t, :], x_in[:, t, :], st[:, 6 + t:7 + t], None, ALU.mult)
            event(ins, "x_norm")
            after(dve, "vec_t")
            event(V.tensor_copy(vec[:], ps[0][:, 0:80]), "vec")
            after(dve, "c_silu")
            dve.wait_ge(bias_loaded, 32)
            for a in range(ADA_FIRST):
                ada(a)
            event(V.memset(am[:], 0.0), "mod_acc")
            after(dve, "mod_col")
            step(V.tensor_copy(chan[:, 0:2, :], ps[1][:, 0:2 * KT].rearrange("p (a k) -> p a k", a=2)))
            step(V.scalar_tensor_tensor(out=chan[:, 2, :], in0=chan[:, 1, :], scalar=1.0, in1=vec[:, 64:72],
                                        op0=ALU.add, op1=ALU.mult))
            after(dve, "x_t")
            for k in range(KT):
                ins = V.tensor_scalar(u_f32[:, k, :], ps[4 + k // 2][:, (k % 2) * T:(k % 2 + 1) * T],
                                      chan[:, 2, k:k + 1], chan[:, 0, k:k + 1], ALU.mult, ALU.add)
            event(ins, "u_f32")
            after(dve, "wif_hi")
            event(V.tensor_tensor(wif_lo[:], w_if[:], wif_hi[:].bitcast(F32), ALU.subtract), "wif_lo")
            for b in range(AHEAD):
                split_lo(b)
            after(dve, "u_hi")
            event(V.tensor_tensor(u_lo[:], u_f32[:], u_hi[:].bitcast(F32), ALU.subtract), "u_lo")

            dve.wait_ge(consts_ready, 4)
            step(V.tensor_copy(dist[:], dist_i))
            step(V.tensor_scalar(masks[:, 0, :], dist[:], float(PATTERNS[0][0] // PATTERNS[0][1]), NEG, ALU.is_gt, ALU.mult))
            for n in (1, 2):
                step(V.tensor_scalar(dist_m, dist_i, PATTERNS[n][1] - 1, None, ALU.bitwise_and))
                step(V.tensor_scalar(masks[:, n, :], dist_m, 0.0, NEG, ALU.not_equal, ALU.mult))
            step(V.tensor_scalar(bias_a[:], dist[:], 0.0, NEG, ALU.is_lt, ALU.mult))
            for n in range(AG):
                ins = V.tensor_tensor(masks[:, n, :], masks[:, n, :], bias_a[:], ALU.add)
            event(ins, "masks")

            for s in range(NBLK):
                if s + AHEAD < NBLK:
                    split_lo(s + AHEAD)
                g, _, _, end = BLOCKS[s]
                kind, col, _ = GROUP_LIST[g]
                banks = 2 * (g % 2), 2 * (g % 2) + 1
                if end and evac_engine(g) == "dve":
                    dve.wait_ge(block_done, s + 1)
                if end and kind == "qk":
                    src = [ps[banks[c // 2]][:, (c % 2) * T:(c % 2 + 1) * T] for c in range(4)]
                    for c in range(4):
                        ins = V.tensor_scalar(qk_m[:, 4 * g + c, :], src[c], vec[:, 3 * 16 + 4 * g + c:3 * 16 + 4 * g + c + 1],
                                              None, ALU.mult)
                    step(ins)
                    for back in (1, 2, 3):
                        for c in range(4):
                            tap = (3 - back) * 16 + 4 * g + c
                            dst = qk_m[:, 4 * g + c, back:T]
                            ins = V.scalar_tensor_tensor(out=dst, in0=src[c][:, 0:T - back], scalar=vec[:, tap:tap + 1],
                                                         in1=dst, op0=ALU.mult, op1=ALU.add)
                        if back < 3:
                            step(ins)
                    ins.then_inc(evac_dve, 1)
                if end and kind == "bm":
                    j = col // NB
                    for n, bank in enumerate(banks):
                        view = sig_gm[:, 4 * j + 2 * n:4 * j + 2 * n + 2, :]
                        ins = V.tensor_tensor(view, ps[bank][:].rearrange("p (c t) -> p c t", c=2), view, ALU.mult)
                    ins.then_inc(evac_dve, 1)
                if end and kind == "ba":
                    j = col // NB
                    for n, bank in enumerate(banks):
                        view = sig_ga[:, 4 * j + 2 * n:4 * j + 2 * n + 2, :]
                        ins = V.tensor_tensor(view, ps[bank][:].rearrange("p (c t) -> p c t", c=2), view, ALU.mult)
                    ins.then_inc(evac_dve, 1)
                    if j == 1:
                        dve.wait_ge(evac_dve, 8)
                        event(V.tensor_tensor(sig_gm[:], sig_gm[:], sig_ga[:], ALU.add), "y_f32")
                        after(dve, "y_hi")
                        event(V.tensor_tensor(y_lo[:], sig_gm[:], y_hi[:].bitcast(F32), ALU.subtract), "y_lo")
                if end and kind == "wo":
                    j = col // NB
                    if j == 0:
                        dve.wait_ge(x_again, 16)
                    for t in range(TT):
                        ins = V.tensor_tensor(scratch[:, t, col:col + NB], ps[banks[t]][:], mod[:, 0, col:col + NB], ALU.mult)
                    ins.then_inc(evac_dve, 1)
                    dve.wait_ge(evac_dve, 9 + j)
                    for t in range(TT):
                        view = x_res[:, t, col:col + NB]
                        ins = V.tensor_tensor(view, view, scratch[:, t, col:col + NB], ALU.add)
                    if j == 1:
                        event(ins, "x1")
                if s in ADA_AT:
                    ada(ADA_AT[s])

                if s == GATES_AT:
                    after(dve, "gates")
                    for t in range(TT):
                        V.tensor_tensor(gm[:, m_i, t, :], ps[4][:, t * IF_N:t * IF_N + MH], gate_b[:, 0:MH], ALU.add)
                        ins = V.tensor_tensor(gm[:, m_f, t, :], ps[4][:, t * IF_N + MH:(t + 1) * IF_N], gate_b[:, MH:IF_N], ALU.add)
                    step(ins)
                    event(V.scalar_tensor_tensor(out=gm[:, m_abs], in0=gm[:, m_f], scalar=-1.0, in1=gm[:, m_f],
                                                 op0=ALU.mult, op1=ALU.max), "gate_abs")
                    after(dve, "gate_exp")
                    event(V.tensor_scalar(gm[:, m_tmp], gm[:, m_tmp], 1.0, None, ALU.add), "gate_1p")
                    after(dve, "gate_ln")
                    event(V.scalar_tensor_tensor(out=gm[:, m_lf], in0=gm[:, m_f], scalar=0.0, in1=gm[:, m_abs],
                                                 op0=ALU.min, op1=ALU.subtract), "lf")
                if s == CUMSUM_AT:
                    after(dve, "cumsum")
                    step(V.tensor_copy(gm[:, m_cum], ps[4][:, 0:TT * MH].rearrange("p (t h) -> p t h", t=TT)))
                    step(V.tensor_tensor(gm[:, m_g], gm[:, m_i], gm[:, m_cum], ALU.subtract))
                    event(V.tensor_scalar(gm[:, m_ng], gm[:, m_g], -1.0, None, ALU.mult), "neg_g")
                if s == GATE_T_AT:
                    after(dve, "gate_t")
                    step(V.tensor_copy(neg_row, ps[5][0:MH, 0:T]))
                    event(V.tensor_tensor_scan(run_row[:], neg_row, neg_row, 0.0, ALU.min, ALU.min), "run_min")
                if s == GATE_BACK_AT:
                    after(dve, "gate_back")
                    event(V.tensor_tensor(gm[:, m_tmp], ps[4][:, 0:TT * MH].rearrange("p (t h) -> p t h", t=TT),
                                          gm[:, m_cum], ALU.subtract), "m_neg")
                if s in SCORE_M_AT:
                    h = SCORE_M_AT.index(s)
                    after(dve, f"m_score{h}")
                    V.scalar_tensor_tensor(out=w_m[:, 0:P], in0=ps[4][:, 0:P], scalar=gm[:, m_g, 0, h:h + 1],
                                           in1=neg_tri[:], op0=ALU.add, op1=ALU.add)
                    V.tensor_scalar(w_m[:, P:2 * P], ps[4][:, P:2 * P], gm[:, m_g, 0, h:h + 1], None, ALU.add)
                    event(V.scalar_tensor_tensor(out=w_m[:, 2 * P:3 * P], in0=ps[4][:, P:2 * P], scalar=gm[:, m_g, 1, h:h + 1],
                                                 in1=neg_tri[:], op0=ALU.add, op1=ALU.add), f"m_log{h}")
                    after(dve, f"m_exp{h}")
                    event(V.scalar_tensor_tensor(out=p_m, in0=ps[5][:, 0:384], scalar=MD ** -0.5, in1=w_m,
                                                 op0=ALU.mult, op1=ALU.mult), f"m_p{h}")
                if s == M_SCALE_AT:
                    after(dve, "m_num3", "floor")
                    step(V.scalar_tensor_tensor(out=gm[:, m_den], in0=gm[:, m_den], scalar=-1.0, in1=gm[:, m_den],
                                                op0=ALU.mult, op1=ALU.max))
                    step(V.tensor_tensor(gm[:, m_den], gm[:, m_den], gm[:, m_floor], ALU.max))
                    step(V.reciprocal(gm[:, m_rec], gm[:, m_den]))
                    step(V.tensor_tensor(gm[:, m_abs], gm[:, m_ss], gm[:, m_rec], ALU.mult))
                    step(V.tensor_tensor(gm[:, m_abs], gm[:, m_abs], gm[:, m_rec], ALU.mult))
                    event(V.tensor_scalar(gm[:, m_abs], gm[:, m_abs], 1.0 / MD, EPS, ALU.mult, ALU.add), "m_var")
                    after(dve, "m_sqrt")
                    step(V.reciprocal(gm[:, m_tmp], gm[:, m_tmp]))
                    event(V.tensor_tensor(gm[:, m_rec], gm[:, m_rec], gm[:, m_tmp], ALU.mult), "m_scale")
                if s in SCORE_A_AT:
                    h = SCORE_A_AT.index(s)
                    after(dve, f"a_score{h}")
                    if h:
                        after(dve, f"a_turn{h - 1}")
                    for n in range(AG):
                        head = n * AM + h
                        slope = 2.0 ** (-8.0 * (head + 1) / AH)
                        step(V.scalar_tensor_tensor(out=bias_a[:], in0=dist[:], scalar=-slope, in1=masks[:, n, :],
                                                    op0=ALU.mult, op1=ALU.add))
                        V.scalar_tensor_tensor(out=prob[:, n * P:(n + 1) * P], in0=ps[4][:, n * P:(n + 1) * P],
                                               scalar=AD ** -0.5, in1=bias_a[:, P:T], op0=ALU.mult, op1=ALU.add)
                        src = ps[5][:, n * T:(n + 1) * T] if n < 2 else ps[6][:, 0:T]
                        step(V.scalar_tensor_tensor(out=prob[:, 384 + n * T:384 + (n + 1) * T], in0=src,
                                                    scalar=AD ** -0.5, in1=bias_a[:], op0=ALU.mult, op1=ALU.add))
                    V.tensor_reduce(am[:, 0:1], prob[:, 0:384], AX_X, ALU.max, negate=True)
                    event(V.tensor_reduce(am[:, 1:2], prob[:, 384:1152], AX_X, ALU.max, negate=True), f"a_max{h}")
                    after(dve, f"a_exp{h}")
                    step(V.reciprocal(am[:, 4:6], am[:, 2:4]))
                    V.tensor_scalar(prob[:, 0:384], prob[:, 0:384], am[:, 4:5], None, ALU.mult)
                    event(V.tensor_scalar(prob[:, 384:1152], prob[:, 384:1152], am[:, 5:6], None, ALU.mult), f"a_prob{h}")
                if s == M_OUT_AT:
                    evacuated(dve, 16)
                    for t in range(TT):
                        for h in range(MH):
                            view = h_m[:, t, h * MD:(h + 1) * MD]
                            ins = V.scalar_tensor_tensor(out=view, in0=view, scalar=gm[:, m_rec, t, h:h + 1],
                                                         in1=sig_o[:, t, h * MD:(h + 1) * MD], op0=ALU.mult, op1=ALU.mult)
                    event(ins, "h_m")
                if s == M_TURN_AT:
                    after(dve, "hm_t")
                    for k in range(KT):
                        ins = V.tensor_scalar(hm_f32[:, k, :], ps[(4, 5, 6, 3)[k // 2]][:, (k % 2) * T:(k % 2 + 1) * T],
                                              vec[:, 72 + k:73 + k], None, ALU.mult)
                    event(ins, "hm_f32")
                    after(dve, "hm_hi")
                    event(V.tensor_tensor(hm_lo[:], hm_f32[:], hm_hi[:].bitcast(F32), ALU.subtract), "hm_lo")
                    after(dve, "ha_hi")
                    event(V.tensor_tensor(ha_lo[:], ha_f32[:], ha_hi[:].bitcast(F32), ALU.subtract), "ha_lo")
                if s == BCAST_AT[-1]:
                    after(dve, "mod3")
                    dve.wait_ge(g_ffn_loaded, 16)
                    event(V.scalar_tensor_tensor(out=mod[:, 2, :], in0=mod[:, 2, :], scalar=1.0, in1=g_ffn,
                                                 op0=ALU.add, op1=ALU.mult), "scale_ffn")

            after(dve, "x1_ss")
            inv_rms(st[:, 8:10], st[:, 10:12], "x1_var")
            after(dve, "x1_sqrt")
            step(V.reciprocal(st[:, 14:16], st[:, 12:14]))
            for t in range(TT):
                ins = V.scalar_tensor_tensor(out=u_ffn[:, t, :], in0=x_res[:, t, :], scalar=st[:, 14 + t:15 + t],
                                             in1=mod[:, 2, :], op0=ALU.mult, op1=ALU.mult)
            step(ins)
            for t in range(TT):
                ins = V.tensor_tensor(u_ffn[:, t, :], u_ffn[:, t, :], mod[:, 1, :], ALU.add)
            event(ins, "u_ffn")

            SC, SEL, IN, T1, T2, OH1, OH2, KEY, W, PICK, R = range(11)

            ramp = rt[:, 20, 0, :]

            for j in range(NE):
                ins = V.memset(ramp[:, j:j + 1], float(NE - j))
            step(ins)
            after(dve, "scores")
            for t in range(TT):
                ins = V.tensor_tensor(rt[:, SEL, t, :], rt[:, SC, t, :], rb[:], ALU.add)
            step(ins)
            sel4 = rt[:, SEL].rearrange("p t (g j) -> p (t g) j", j=PER)
            pairs = rt[:, 12:15].rearrange("p a t e -> p (a t e)")[:, 0:TT * GROUPS * 6].rearrange("p (g j) -> p g j", j=6)
            n = 0
            for a in range(PER):
                for b in range(a + 1, PER):
                    ins = V.tensor_tensor(pairs[:, :, n:n + 1], sel4[:, :, a:a + 1], sel4[:, :, b:b + 1], ALU.add)
                    n += 1
            step(ins)
            gscore = rt[:, T1].rearrange("p t e -> p (t e)")[:, 0:TT * GROUPS]
            step(V.tensor_reduce(gscore, pairs, AX_X, ALU.max))

            def one_hot_first(src3, best, key, dst3, width):
                step(V.tensor_reduce(best, src3, AX_X, ALU.max))
                for t in range(TT):
                    ins = V.scalar_tensor_tensor(out=key[:, t, :], in0=src3[:, t, :], scalar=best[:, t:t + 1],
                                                 in1=ramp[:, 0:width], op0=ALU.is_equal, op1=ALU.mult)
                step(ins)
                step(V.tensor_reduce(best, key, AX_X, ALU.max))
                for t in range(TT):
                    ins = V.tensor_scalar(dst3[:, t, :], key[:, t, :], best[:, t:t + 1], None, ALU.is_equal)
                step(ins)

            best = st[:, 24:26]
            gs3 = gscore.rearrange("p (t g) -> p t g", t=TT)
            key4 = rt[:, KEY, :, 0:GROUPS]
            ing = rt[:, T2, :, 0:GROUPS]
            one_hot_first(gs3, best, key4, ing, GROUPS)
            step(V.tensor_scalar(ing, ing, 1.0, -NEG, ALU.subtract, ALU.mult))
            for t in range(TT):
                for gi in range(GROUPS):
                    ins = V.tensor_scalar(rt[:, IN, t, gi * PER:(gi + 1) * PER], rt[:, SEL, t, gi * PER:(gi + 1) * PER],
                                          ing[:, t, gi:gi + 1], None, ALU.add)
            step(ins)
            one_hot_first(rt[:, IN], best, rt[:, KEY], rt[:, OH1], NE)
            step(V.scalar_tensor_tensor(out=rt[:, IN], in0=rt[:, OH1], scalar=2 * NEG, in1=rt[:, IN],
                                        op0=ALU.mult, op1=ALU.add))
            one_hot_first(rt[:, IN], best, rt[:, KEY], rt[:, OH2], NE)
            step(V.tensor_tensor(rt[:, PICK], rt[:, OH1], rt[:, OH2], ALU.add))
            step(V.tensor_tensor(rt[:, W], rt[:, PICK], rt[:, SC], ALU.mult))
            step(V.tensor_reduce(st[:, 26:28], rt[:, W], AX_X, ALU.add))
            step(V.reciprocal(st[:, 28:30], st[:, 26:28]))
            V.memset(slot_tab[:, :, VISITS * NE:VISITS * NE + 1], -1.0)
            V.memset(comb_tab[:, :, VISITS * NE:VISITS * NE + 1], 0.0)
            for t in range(TT):
                for v in range(VISITS):
                    ins = V.tensor_scalar(comb_tab[:, t, v * NE:(v + 1) * NE], rt[:, W, t, :], st[:, 28 + t:29 + t], None, ALU.mult)
            event(ins, "router")
            after(dve, "rank_sums")
            for t in range(TT):
                ins = V.scalar_tensor_tensor(out=rt[:, R, t, :], in0=ps[1][:, t * NE:(t + 1) * NE], scalar=1.0,
                                             in1=rt[:, PICK, t, :], op0=ALU.add, op1=ALU.mult)
            step(ins)
            for t in range(TT):
                for v in range(VISITS):
                    ins = V.tensor_scalar(slot_tab[:, t, v * NE:(v + 1) * NE], rt[:, R, t, :], -1.0 - v * SLOTS, None, ALU.add)
            step(ins)
            step(V.tensor_reduce(many[:, 0:1], ps[1][:, TT * NE:(TT + 1) * NE], AX_X, ALU.max))
            event(V.tensor_scalar(many_i[:, 0:1], many[:, 0:1], float(SLOTS), None, ALU.is_gt), "ranks")
            event(V.memset(zeros[:], 0.0), "zero")
            V.memset(scat[1][:], 0.0).then_inc(scat_ready, 1)
            V.memset(y_e[:], 0.0).then_inc(y_ready, 1)

            dve.wait_ge(consts_ready, 6)

            def build_onehot(n):
                V.tensor_copy(st[:, 32:34], comb_tab[:, :, bass.ds(n, 1)].rearrange("p t o -> p (t o)"))
                V.tensor_scalar(onehot[:, 0, :], slot_id, slot_tab[:, 0, bass.ds(n, 1)], None, ALU.is_equal)
                V.tensor_scalar(onehot[:, 1, :], slot_id, slot_tab[:, 1, bass.ds(n, 1)], None, ALU.is_equal).then_inc(onehot_ready, 1)

            def evacuate_scatter(n, s):
                dve.wait_ge(gathered, n + 1)
                V.tensor_copy(scat[s][:], ps[7][:, 0:T + 1]).then_inc(scat_ready, 1)

            def visit(n, s):
                dve.wait_ge(gathered, n + 1)
                build_onehot(n + 1)
                dve.wait_ge(gate_up_done, n + 1)
                dve.wait_ge(sg_ready, n + 1)
                dve.wait_ge(scat_ready, n + 2)
                V.scalar_tensor_tensor(out=he[0:64, :], in0=ps[4][64:128, :], scalar=scat[s][64:128, T:T + 1],
                                       in1=sg[64:128, :], op0=ALU.mult, op1=ALU.mult).then_inc(he_ready, 1)
                evacuate_scatter(n + 1, 1 - s)
                dve.wait_ge(down_done, n + 1)
                V.tensor_copy(y_e[:], ps[6][:]).then_inc(y_ready, 1)

            build_onehot(0)
            evacuate_scatter(0, 0)
            with dve.Fori(0, NE // 2) as i:
                for s in range(2):
                    visit(2 * i + s, s)
            after(dve, "ranks")
            again = dve.value_load(many_i[0:1, 0:1], min_val=0, max_val=1)
            with dve.If(again == 1):
                with dve.Fori(NE // 2, VISITS * NE // 2) as i:
                    for s in range(2):
                        visit(2 * i + s, s)

            dve.wait_ge(moe_done, 1)
            for t in range(TT):
                for h in range(2):
                    ins = V.tensor_tensor(scratch[:, t, h * NB:(h + 1) * NB], ps[2 * t + h][:],
                                          mod[:, 3, h * NB:(h + 1) * NB], ALU.mult)
            step(ins)
            event(V.tensor_tensor(x_res[:], x_res[:], scratch[:], ALU.add), "x2")
            after(dve, "x2_ss")
            inv_rms(st[:, 16:18], st[:, 18:20], "x2_var")
            after(dve, "x2_sqrt")
            step(V.reciprocal(st[:, 22:24], st[:, 20:22]))
            dve.wait_ge(fin_loaded, 16)
            for t in range(TT):
                V.scalar_tensor_tensor(out=scratch[:, t, :], in0=x_res[:, t, :], scalar=st[:, 22 + t:23 + t],
                                       in1=fin_g[:], op0=ALU.mult, op1=ALU.mult).then_inc(out_ready, 1)

        @block.tensor
        def _(pe):
            mm, tr = nc.tensor.matmul, nc.tensor.transpose

            pe.wait_ge(consts_ready, 2)
            pe.wait_ge(rows_loaded, 48)
            event(tr(ps[0][:, 0:80], rows[0:80, :], ident[0:80, 0:80]), "vec_t")
            after(pe, "x_norm")
            for k in range(KT):
                for t in range(TT):
                    ins = tr(ps[4 + k // 2][:, (k % 2) * T + t * P:(k % 2) * T + (t + 1) * P],
                             x_in[:, t, k * P:(k + 1) * P], ident[:])
            event(ins, "x_t")
            after(pe, "mod_acc")
            for n in range(2 * KT):
                ins = mm(ps[1][:, n:n + 1], acc_a[:, n * P:(n + 1) * P], ones[:, 0:1], start=True, stop=True)
            event(ins, "mod_col")

            for s, (g, k0, first, end) in enumerate(BLOCKS):
                kind, _, channel_major = GROUP_LIST[g]
                if s == 0:
                    after(pe, "u_lo")
                if first and g >= 2:
                    evacuated(pe, g - 2)
                if kind == "bm" and first and g == 21:
                    after(pe, "hm_lo")
                if kind == "ba" and g == 23:
                    after(pe, "ha_lo")
                if kind == "wo" and g == 25 and first:
                    after(pe, "y_lo")
                x_hi, x_lo = {"bm": (hm_hi, hm_lo), "ba": (ha_hi, ha_lo), "wo": (y_hi, y_lo)}.get(kind, (u_hi, u_lo))
                pe.wait_ge(lo_ready, s + 1)
                w_hi, w_lo = hi[s % RING], lo[s % RING]
                banks = 2 * (g % 2), 2 * (g % 2) + 1
                if channel_major:
                    for c in range(4):
                        dst = ps[banks[c // 2]][:, (c % 2) * T:(c % 2 + 1) * T]
                        cols = slice(c * P, (c + 1) * P)
                        for k in range(KB):
                            for n, (w, x) in enumerate(((w_hi, x_hi), (w_hi, x_lo), (w_lo, x_hi))):
                                ins = mm(dst, w[:, k, cols], x[:, k0 + k, :],
                                         start=(first and c % 2 == 0 and k == 0 and n == 0),
                                         stop=(end and k == KB - 1 and n == 2), skip_group_check=True)
                else:
                    for t in range(TT):
                        rows_t = slice(t * P, (t + 1) * P)
                        for k in range(KB):
                            for n, (w, x) in enumerate(((w_hi, x_hi), (w_hi, x_lo), (w_lo, x_hi))):
                                ins = mm(ps[banks[t]][:], x[:, k0 + k, rows_t], w[:, k, :],
                                         start=(first and k == 0 and n == 0), stop=(end and k == KB - 1 and n == 2))
                ins.then_inc(block_done, 1)

                if s == GATES_AT:
                    after(pe, "wif_lo")
                    for t in range(TT):
                        for k in range(KT):
                            for n, (w, x) in enumerate(((wif_hi, u_hi), (wif_hi, u_lo), (wif_lo, u_hi))):
                                ins = mm(ps[4][:, t * IF_N:(t + 1) * IF_N], x[:, k, t * P:(t + 1) * P], w[:, k, :],
                                         start=(k == 0 and n == 0), stop=(k == KT - 1 and n == 2))
                    event(ins, "gates")
                if s == CUMSUM_AT:
                    after(pe, "lf")
                    mm(ps[4][:, 0:MH], tri_le[:], gm[:, m_lf, 0, :], start=True, stop=True)
                    mm(ps[4][:, MH:2 * MH], ones[:], gm[:, m_lf, 0, :], start=True, stop=False)
                    event(mm(ps[4][:, MH:2 * MH], tri_le[:], gm[:, m_lf, 1, :], start=False, stop=True), "cumsum")
                if s == GATE_T_AT:
                    after(pe, "neg_g")
                    for t in range(TT):
                        ins = tr(ps[5][0:MH, t * P:(t + 1) * P], gm[:, m_ng, t, :], ident[:])
                    event(ins, "gate_t")
                if s == GATE_BACK_AT:
                    after(pe, "run_min")
                    for t in range(TT):
                        ins = tr(ps[4][:, t * MH:(t + 1) * MH], run_row[:, t * P:(t + 1) * P], ident[0:MH, 0:MH])
                    event(ins, "gate_back")
                if s in SCORE_M_AT:
                    h = SCORE_M_AT.index(s)
                    if h == 0:
                        pe.wait_ge(qk_ready, 4)
                        after(pe, "m_neg")
                    else:
                        after(pe, f"m_p{h - 1}")
                    mm(ps[4][:, 0:T], ident[0:MH, h:h + 1].broadcast_to([MH, P]), run_row[:], start=True, stop=True)
                    for k in range(2):
                        mm(ps[5][:, 0:T], qk_m[:, KT + 2 * h + k, 0:P], qk_m[:, 2 * h + k, :], start=(k == 0), stop=(k == 1))
                    for k in range(2):
                        ins = mm(ps[5][:, T:T + P], qk_m[:, KT + 2 * h + k, P:T], qk_m[:, 2 * h + k, P:T],
                                 start=(k == 0), stop=(k == 1))
                    event(ins, f"m_score{h}")
                if s in VALUE_M_AT:
                    h = VALUE_M_AT.index(s)
                    after(pe, f"m_p{h}")
                    if h == 0:
                        evacuated(pe, 5)
                    else:
                        after(pe, f"m_num{h - 1}")
                    for t, parts in ((0, ((0, 0),)), (1, ((P, 0), (2 * P, 1)))):
                        for n, (at_p, sk) in enumerate(parts):
                            mm(ps[6 + t][:, 0:MD], p_m[:, at_p:at_p + P], v_m[:, sk, h * MD:(h + 1) * MD],
                               start=(n == 0), stop=(n == len(parts) - 1))
                        for n, (at_p, sk) in enumerate(parts):
                            ins = mm(ps[6 + t][:, MD:MD + 1], p_m[:, at_p:at_p + P], ones[:, 0:1],
                                     start=(n == 0), stop=(n == len(parts) - 1))
                    event(ins, f"m_val{h}")
                if s in TURN_A_AT:
                    h = TURN_A_AT.index(s)
                    after(pe, f"a_prob{h}")
                    for n in range(AG):
                        for m, src in enumerate((prob[:, n * P:(n + 1) * P], prob[:, 384 + n * T:384 + n * T + P],
                                                 prob[:, 384 + n * T + P:384 + (n + 1) * T])):
                            ins = tr(ps[4 + n][:, m * P:(m + 1) * P], src, ident[:])
                    event(ins, f"a_turn{h}")
                if s in VALUE_A_AT:
                    h = VALUE_A_AT.index(s)
                    after(pe, f"a_turned{h}")
                    if h:
                        after(pe, f"a_out{h - 1}")
                    else:
                        after(pe, "m_num3")
                    for n in range(AG):
                        cols = slice((n * AM + h) * AD, (n * AM + h + 1) * AD)
                        mm(ps[7][:, 0:T], v_a[:, 0, cols], turned[:, n, 0:T], start=(n == 0), stop=False, skip_group_check=True)
                        ins = mm(ps[7][:, P:T], v_a[:, 1, cols], turned[:, n, T:384], start=False, stop=(n == AG - 1),
                                 skip_group_check=True)
                    event(ins, f"a_val{h}")
                if s in SCORE_A_AT:
                    h = SCORE_A_AT.index(s)
                    if h == 0:
                        evacuated(pe, 14)
                        after(pe, "m_p3", "masks")
                    else:
                        after(pe, f"a_turned{h - 1}")
                    for n in range(AG):
                        head = n * AM + h
                        mm(ps[4][:, n * P:(n + 1) * P], q_a[:, head, 0:P], k_a[:, head, 0:P], start=True, stop=True)
                        dst = ps[5][:, n * T:(n + 1) * T] if n < 2 else ps[6][:, 0:T]
                        ins = mm(dst, q_a[:, head, P:T], k_a[:, head, :], start=True, stop=True)
                    event(ins, f"a_score{h}")
                if s == M_TURN_AT:
                    after(pe, "h_m", "a_turned3")
                    evacuated(pe, 19)
                    for k in range(KT):
                        for t in range(TT):
                            ins = tr(ps[(4, 5, 6, 3)[k // 2]][:, (k % 2) * T + t * P:(k % 2) * T + (t + 1) * P],
                                     h_m[:, t, k * P:(k + 1) * P], ident[:])
                    event(ins, "hm_t")
                if s in BCAST_AT:
                    i = BCAST_AT.index(s)
                    if i == 0:
                        pe.wait_ge(ada_done, ADA_FIRST + ADA_REST)
                        after(pe, "hm_f32")
                    elif i == 1:
                        after(pe, "a_out3")
                    else:
                        after(pe, f"mod{i - 2}")
                    for n in range(2):
                        ins = mm(ps[4 + 2 * (i % 2) + n][:], ones[:], mod[:, i, n * NB:(n + 1) * NB], start=True, stop=True)
                    event(ins, f"bcast{i}")

            after(pe, "u_ffn", "mod3")
            for k in range(KT):
                for t in range(TT):
                    ins = tr(ps[4 + k // 2][:, (k % 2) * T + t * P:(k % 2) * T + (t + 1) * P],
                             u_ffn[:, t, k * P:(k + 1) * P], ident[:])
            event(ins, "u_ffn_t")
            after(pe, "ufT_b")
            evacuated(pe, 26)
            for t in range(TT):
                for k in range(KT):
                    ins = mm(ps[0][:, t * NE:(t + 1) * NE], u_ffn_t[:, k, t * P:(t + 1) * P], rw[:, k, :],
                             start=(k == 0), stop=(k == KT - 1))
            event(ins, "logits")
            after(pe, "router")
            pe.wait_ge(consts_ready, 6)
            pick = rt[:, 9]
            mm(ps[1][:, 0:NE], tri_lt, pick[:, 0, :], start=True, stop=True)
            mm(ps[1][:, NE:2 * NE], ones[:], pick[:, 0, :], start=True, stop=False)
            mm(ps[1][:, NE:2 * NE], tri_lt, pick[:, 1, :], start=False, stop=True)
            mm(ps[1][:, 2 * NE:3 * NE], ones[:], pick[:, 0, :], start=True, stop=False)
            event(mm(ps[1][:, 2 * NE:3 * NE], ones[:], pick[:, 1, :], start=False, stop=True), "rank_sums")
            after(pe, "zero")
            for b in range(4):
                ins = mm(ps[b][:], zeros[:, 0:P], zeros[:], start=True, stop=False, skip_group_check=True)
            event(ins, "acc_zeroed")

            def gather(n):
                pe.wait_ge(onehot_ready, n + 1)
                for k in range(KT):
                    for t in range(TT):
                        mm(ps[5][:, k * SLOTS:(k + 1) * SLOTS], u_ffn[:, t, k * P:(k + 1) * P], onehot[:, t, 0:SLOTS],
                           start=(t == 0), stop=(t == TT - 1))
                for t in range(TT):
                    tr(ps[7][:, t * P:(t + 1) * P], onehot[:, t, :], ident[:])
                for t in range(TT):
                    ins = mm(ps[7][:, T:T + 1], onehot[:, t, :], st[:, 32 + t:33 + t], start=(t == 0), stop=(t == TT - 1))
                ins.then_inc(gathered, 1)

            def scatter(s):
                for t in range(TT):
                    for h in range(2):
                        ins = mm(ps[2 * t + h][:], scat[s][64 * h:64 * h + 64, t * P:(t + 1) * P], y_e[64 * h:64 * h + 64, :],
                                 start=False, stop=False, skip_group_check=True)
                ins.then_inc(scattered, 1)

            def visit(n, i, s):
                pe.wait_ge(xe_ready, n + 1)
                pe.wait_ge(scat_ready, n + 2)
                pe.wait_ge(gate_loaded[s], 16 * i + 16)
                pe.wait_ge(up_loaded[s], 16 * i + 16)
                for k in range(KT):
                    mm(ps[4][0:64, :], xe_t[:, k, :], w_gate[s][:, k, :], start=(k == 0), stop=(k == KT - 1))
                    ins = mm(ps[4][64:128, :], xe_t[:, k, :], w_up[s][:, k, :], start=(k == 0), stop=(k == KT - 1))
                ins.then_inc(gate_up_done, 1)
                pe.wait_ge(y_ready, n + 1)
                scatter(1 - s)
                pe.wait_ge(he_ready, n + 1)
                for k in range(FF // P):
                    ins = mm(ps[6][:, k * SLOTS:(k + 1) * SLOTS], he[0:64, k * P:(k + 1) * P], ident[0:64, 0:64],
                             start=True, stop=True)
                ins.then_inc(he_turned, 1)
                gather(n + 1)
                pe.wait_ge(he_t_ready, n + 1)
                pe.wait_ge(down_loaded[s], 16 * i + 16)
                for k in range(FF // P):
                    for h in range(2):
                        ins = mm(ps[6][64 * h:64 * h + 64, :], he_t[:, k, :], w_down[s][:, k, h * NB:(h + 1) * NB],
                                 start=(k == 0), stop=(k == FF // P - 1))
                ins.then_inc(down_done, 1)

            gather(0)
            with pe.Fori(0, NE // 2) as i:
                for s in range(2):
                    visit(2 * i + s, i, s)
            pe.wait_ge(y_ready, NE + 1)
            after(pe, "ranks")
            again = pe.value_load(many_i[0:1, 0:1], min_val=0, max_val=1)
            with pe.If(again == 1):
                with pe.Fori(NE // 2, VISITS * NE // 2) as i:
                    for s in range(2):
                        visit(2 * i + s, i, s)
                pe.wait_ge(y_ready, VISITS * NE + 1)
            for t in range(TT):
                for h in range(2):
                    ins = mm(ps[2 * t + h][:], scat[1][64 * h:64 * h + 64, t * P:(t + 1) * P], y_e[64 * h:64 * h + 64, :],
                             start=False, stop=True, skip_group_check=True)
            ins.then_inc(moe_done, 1)


_INS = ["x", "c", "ada_w", "ada_b", "w_in", "mlstm_conv", "mlstm_gate_b", "mlstm_norm_g", "w_branch_m", "w_branch_a",
        "w_out", "router_w", "router_b", "w_gate_e", "w_up_e", "w_down_e", "norm_mix_g", "norm_ffn_g", "final_norm_g"]
_OUTS = [((1, 256, 1024), "float32")]


def kernel(**inputs):
    import numpy as _np
    import concourse.bacc as _bacc
    from concourse import mybir as _mybir
    from concourse.bass_utils import run_bass_kernel_spmd as _run

    nc = _bacc.Bacc("TRN2", target_bir_lowering=False, num_devices=1)
    arrays, aps = {}, {}
    for name in _INS:
        a = _np.ascontiguousarray(inputs[name])
        arrays[f"in_{name}_dram"] = a
        aps[name] = nc.dram_tensor(f"in_{name}_dram", a.shape, _mybir.dt.from_np(a.dtype), kind="ExternalInput").ap()
    shape, dtype = _OUTS[0]
    out = nc.dram_tensor("out_0_dram", shape, _mybir.dt.from_np(_np.dtype(dtype)), kind="ExternalOutput").ap()
    build(nc, aps, out)
    r = _run(nc, [arrays], core_ids=[0])
    return r.results[0]["out_0_dram"]
```

```python
import math
from contextlib import ExitStack

import concourse.bass as bass
from concourse import mybir

ALU = mybir.AluOpType
ACT = mybir.ActivationFunctionType
F32 = mybir.dt.float32
F32R = mybir.dt.float32r
I32 = mybir.dt.int32
AX_X = mybir.AxisListType.X

P = 128
D = 1024
KT = D // P
T = 256
TT = T // P
NB = 512
KB = 4
EPS = 1e-6
NEG = -1e30
MH, MD = 4, 256
AH, AD, AG = 12, 128, 3
AM = AH // AG
PATTERNS = ((128, 1), (512, 4), (2048, 16))
NE, FF = 16, 512
GROUPS, PER = 4, 4
SLOTS = 64
VISITS = T // SLOTS
RAW, RING = 4, 3
IF_AT = 4 * D
IF_N = 2 * MH

IN_GROUPS = (
    [("qk", c, True) for c in range(0, 2 * D, NB)]
    + [("vm", c, False) for c in range(2 * D, 3 * D, NB)]
    + [("qa", c, True) for c in range(IF_AT + IF_N, IF_AT + IF_N + 1536, NB)]
    + [("ka", c, True) for c in range(IF_AT + IF_N + 1536, IF_AT + IF_N + 3072, NB)]
    + [("va", c, False) for c in range(IF_AT + IF_N + 3072, IF_AT + IF_N + 4608, NB)]
    + [("o", c, False) for c in range(3 * D, 4 * D, NB)]
    + [("gm", c, True) for c in range(IF_AT + IF_N + 4608, IF_AT + IF_N + 4608 + D, NB)]
    + [("ga", c, True) for c in range(IF_AT + IF_N + 4608 + D, IF_AT + IF_N + 4608 + 2 * D, NB)]
)
GROUP_LIST = IN_GROUPS + [("bm", 0, True), ("bm", NB, True), ("ba", 0, True), ("ba", NB, True),
                          ("wo", 0, False), ("wo", NB, False)]
BLOCKS = []
for _g, (_kind, _c, _cm) in enumerate(GROUP_LIST):
    _halves = 1 if _kind == "ba" else 2
    for _h in range(_halves):
        BLOCKS.append((_g, _h * KB, _h == 0, _h == _halves - 1))
LAST_BLOCK = {g: b for b, (g, _, _, end) in enumerate(BLOCKS) if end}
NBLK = len(BLOCKS)
BLK_IN = 2 * len(IN_GROUPS)
AHEAD = RING - 1

GATES_AT, CUMSUM_AT, GATE_T_AT, GATE_BACK_AT = 1, 3, 5, 7
SCORE_M_AT = [12 + 2 * h for h in range(MH)]
VALUE_M_AT = [13 + 2 * h for h in range(MH)]
M_SCALE_AT = 20
MASKS_AT = 2
SCORE_A_AT = [30, 33, 36, 38]
TURN_A_AT = [32, 35, 37, 40]
VALUE_A_AT = [33, 36, 38, 41]
M_OUT_AT = 34
M_TURN_AT = [BLK_IN - 2, BLK_IN - 1]
BCAST_AT = [43, 44, 45, 46]
ADA_FIRST = 8
ADA_REST = 16
ADA_AT = {s: ADA_FIRST + i for i, s in enumerate([10, 12, 13, 14, 16, 17, 18, 20, 21, 22, 23, 24, 25, 26, 27, 28])}

STREAM = [("ada", a) for a in range(ADA_FIRST)] + [("w", b) for b in range(AHEAD)]
for _s in range(NBLK):
    if _s + AHEAD < NBLK:
        STREAM.append(("w", _s + AHEAD))
    if _s in ADA_AT:
        STREAM.append(("ada", ADA_AT[_s]))
POS = {item: n for n, item in enumerate(STREAM)}

CHUNKS = 8
PAIRS = NE // 2
BODY = 8


def build(nc, A, out):
    with ExitStack() as ctx:
        base = (nc.sbuf_base + 63) // 64 * 64
        ctx.enter_context(nc.sbuf_tensor("arena", [P, (nc.sbuf_usable_end - base) // 4 - 32], F32))
        K = 1024

        def at(name, kib, shape, dt=F32):
            return nc.alloc_sbuf_tensor_at(name, shape, dt, offset=base + int(kib * K))

        small_at = [192 * K]

        def small(name, shape, dt=F32):
            n = 4
            for s in shape[1:]:
                n *= s
            t = nc.alloc_sbuf_tensor_at(name, shape, dt, offset=base + small_at[0])
            small_at[0] += (n + 31) // 32 * 32
            assert base + small_at[0] <= nc.sbuf_usable_end - 256, (name, small_at[0])
            return t

        def sem(name):
            return ctx.enter_context(nc.semaphore(name))

        raw = [at(f"raw{i}", 8 * i, [P, KB, NB]) for i in range(RAW)]
        hi = [at(f"hi{i}", 32 + 8 * i, [P, KB, NB], F32R) for i in range(RING)]
        lo = [at(f"lo{i}", 56 + 8 * i, [P, KB, NB], F32R) for i in range(RING)]
        u_hi = at("u_hi", 80, [P, KT, T], F32R)
        u_lo = at("u_lo", 88, [P, KT, T], F32R)
        hm_hi = at("hm_hi", 80, [P, KT, T], F32R)
        hm_lo = at("hm_lo", 88, [P, KT, T], F32R)
        qk_m = at("qk_m", 96, [P, 2 * KT, T])
        v_m = at("v_m", 112, [P, TT, D])
        sig_o = at("sig_o", 96, [P, TT, D])
        sig_gm = at("sig_gm", 104, [P, KT, T])
        sig_ga = at("sig_ga", 112, [P, KT, T])
        acc_a = at("acc_a", 120, [P, 2 * D])
        u_f32 = at("u_f32", 128, [P, KT, T])
        q_a = at("q_a", 120, [P, AH, T])
        k_a = at("k_a", 132, [P, AH, T])
        v_a = at("v_a", 144, [P, TT, AH * AD])
        hm_f32 = at("hm_f32", 120, [P, KT, T])
        y_hi = at("y_hi", 120, [P, KT, T], F32R)
        y_lo = at("y_lo", 128, [P, KT, T], F32R)
        x_in = at("x_in", 156, [P, TT, D])
        prob = at("prob", 156, [P, 1152])
        ha_hi = at("ha_hi", 156, [P, AM, T], F32R)
        ha_lo = at("ha_lo", 160, [P, AM, T], F32R)
        h_m = at("h_m", 164, [P, TT, D])
        x_res = at("x_res", 164, [P, TT, D])
        mod = at("mod", 172, [P, 4, D])
        ha_f32 = at("ha_f32", 188, [P, AM, T])
        ring = [at(f"ring{i}", k, [P, KT * FF]) for i, k in enumerate((80, 140, 104, 0, 16, 32, 48, 64))]
        scratch = at("scratch", 96, [P, TT, D])
        u_ffn = at("u_ffn", 120, [P, TT, D])
        u_ffn_t = at("u_ffn_t", 128, [P, KT, T])
        xe_t = at("xe_t", 128, [P, KT, 2 * SLOTS])
        y_e = at("y_e", 132, [P, D])
        he = at("he", 136, [P, FF])
        sg = at("sg", 138, [P, FF])
        rt = at("rt", 156, [P, 16, TT, NE])
        zeros = at("zeros", 158, [P, NB])
        onehot = at("onehot", 160, [P, TT, 2 * SLOTS])
        he_t = at("he_t", 161, [P, FF // P, SLOTS])
        scat = [at("scat0", 162, [P, T + 2]), at("scat1", 188, [P, T + 2])]
        slot_tab = at("slot_tab", 189.5, [P, TT, VISITS * NE + 2])
        comb_tab = at("comb_tab", 190.25, [P, TT, VISITS * NE + 2])
        fin_g = at("fin_g", 172, [P, D])

        ident = small("ident", [P, P])
        ones = small("ones", [P, P])
        tri_le = small("tri_le", [P, P])
        neg_tri = small("neg_tri", [P, P])
        turned = small("turned", [P, AG, 384])
        dist = small("dist", [P, T])
        masks = small("masks", [P, AG, T])
        bias_a = small("bias_a", [P, T])
        slot_id = bias_a[:, 0:SLOTS]
        tri_lt = bias_a[:, 128:256]
        w_m = turned[:, 0, :]
        p_m = turned[:, 1, :]
        dist_i = turned[:, 2, 0:T].bitcast(I32)
        dist_m = turned[:, 0, 0:T].bitcast(I32)
        g_ffn = turned[:].rearrange("p a b -> p (a b)")[:, 0:D]
        vec = small("vec", [P, 80])
        rows = turned[:, 1, 0:P]
        cs = small("cs", [P, KT])
        st = small("st", [P, 40])
        chan = small("chan", [P, 3, KT])
        w_if = small("w_if", [P, KT, IF_N])
        wif_hi = small("wif_hi", [P, KT, IF_N], F32R)
        wif_lo = small("wif_lo", [P, KT, IF_N], F32R)
        gate_b = small("gate_b", [P, IF_N])
        gm = small("gm", [P, 12, TT, MH])
        neg_row = h_m[0:MH, 0, 0:T]
        run_row = small("run_row", [MH, T])
        am = small("am", [P, 8])
        rw = small("rw", [P, KT, NE])
        rb = small("rb", [P, NE])
        w_pair = small("w_pair", [P, TT, 2])
        many = small("many", [P, 2])
        many_i = small("many_i", [P, 2], I32)

        ps = [ctx.enter_context(nc.psum_tensor(f"ps{i}", [P, 512], F32)) for i in range(8)]

        x_loaded, c_loaded, rows_loaded, small_loaded, bias_loaded = (sem(n) for n in (
            "x_loaded", "c_loaded", "rows_loaded", "small_loaded", "bias_loaded"))
        raw_loaded = [sem(f"raw_loaded{i}") for i in range(RAW)]
        ada_done = sem("ada_done")
        hi_ready, lo_ready, block_done = sem("hi_ready"), sem("lo_ready"), sem("block_done")
        evac_act, evac_dve = sem("evac_act"), sem("evac_dve")
        consts_ready, acc_zero = sem("consts_ready"), sem("acc_zero")
        pool_step, act_step, dve_step = sem("pool_step"), sem("act_step"), sem("dve_step")
        pe_side, act_side, dve_side = sem("pe_side"), sem("act_side"), sem("dve_side")
        qk_ready = sem("qk_ready")
        g_ffn_loaded, x_again, fin_loaded = sem("g_ffn_loaded"), sem("x_again"), sem("fin_loaded")
        ring_loaded = [sem(f"ring_loaded{i}") for i in range(CHUNKS)]
        onehot_ready, slots_turned, gathered, xe_ready, scat_ready = (sem(n) for n in (
            "onehot_ready", "slots_turned", "gathered", "xe_ready", "scat_ready"))
        gate_up_done, sg_ready, he_ready, he_turned, he_t_ready, down_done, y_ready = (sem(n) for n in (
            "gate_up_done", "sg_ready", "he_ready", "he_turned", "he_t_ready", "down_done", "y_ready"))
        moe_done, out_ready, stored = (sem(n) for n in ("moe_done", "out_ready", "stored"))

        order = {"pe": [], "act": [], "dve": []}

        def plan():
            pe, act, dve = order["pe"], order["act"], order["dve"]
            pe += ["vec_t", "x_t", "mod_col"]
            act += ["c_silu", "x_ss", "x_sqrt", "u_hi0", "u_hi1", "wif_hi"]
            dve += ["x_var", "x_norm", "vec", "u_f32_0", "u_f32_1", "u_lo0", "u_lo1", "wif_lo"]
            for s in range(NBLK):
                if s == GATES_AT:
                    pe.append("gates"); dve.append("gate_abs"); act += ["gate_exp", "gate_ln"]
                    dve += ["gate_1p", "lf"]
                if s == MASKS_AT:
                    dve.append("masks")
                if s == CUMSUM_AT:
                    pe.append("cumsum"); dve.append("neg_g")
                if s == GATE_T_AT:
                    pe.append("gate_t"); dve.append("run_min")
                if s == GATE_BACK_AT:
                    pe.append("gate_back"); dve.append("m_neg"); act.append("floor")
                if s in SCORE_M_AT:
                    h = SCORE_M_AT.index(s)
                    pe.append(f"m_score{h}"); dve.append(f"m_log{h}"); act.append(f"m_exp{h}"); dve.append(f"m_p{h}")
                if s in VALUE_M_AT:
                    h = VALUE_M_AT.index(s)
                    pe.append(f"m_val{h}"); act.append(f"m_num{h}")
                if s == M_SCALE_AT:
                    dve.append("m_var"); act.append("m_sqrt"); dve.append("m_scale")
                if s in TURN_A_AT:
                    h = TURN_A_AT.index(s)
                    pe.append(f"a_turn{h}"); act.append(f"a_turned{h}")
                if s in VALUE_A_AT:
                    h = VALUE_A_AT.index(s)
                    pe.append(f"a_val{h}"); act.append(f"a_out{h}")
                if s in SCORE_A_AT:
                    h = SCORE_A_AT.index(s)
                    pe.append(f"a_score{h}"); dve.append(f"a_max{h}"); act.append(f"a_exp{h}"); dve.append(f"a_prob{h}")
                if s == M_OUT_AT:
                    dve.append("h_m")
                if s in M_TURN_AT:
                    h = M_TURN_AT.index(s)
                    pe.append(f"hm_t{h}"); act.append(f"hm_hi{h}"); dve.append(f"hm_lo{h}")
                if s == M_TURN_AT[1]:
                    act.append("ha_hi"); dve.append("ha_lo")
                if s in BCAST_AT:
                    i = BCAST_AT.index(s)
                    pe.append(f"bcast{i}"); act.append(f"mod{i}")
                if s in (LAST_BLOCK[23], LAST_BLOCK[24]):
                    j = s - LAST_BLOCK[23]
                    dve.append(f"y_f32_{j}"); act.append(f"y_hi{j}"); dve.append(f"y_lo{j}")
                if s == BCAST_AT[-1]:
                    dve.append("scale_ffn")
                if s == LAST_BLOCK[25]:
                    dve.append("x1_0"); act.append("x1_ss0")
            act += ["x1_ss1", "x1_sqrt", "ufT0", "ufT1", "scores"]
            dve += ["x1_1", "x1_var", "u_ffn0", "u_ffn1", "zero", "router", "ranks", "x2", "x2_var"]
            pe += ["u_ffn_t0", "u_ffn_t1", "logits", "acc_zeroed", "rank_sums"]
            act += ["x2_ss", "x2_sqrt"]

        plan()
        side_sem = {"pe": pe_side, "act": act_side, "dve": dve_side}
        where = {n: (e, i + 1) for e, names in order.items() for i, n in enumerate(names)}
        made = {"pe": 0, "act": 0, "dve": 0}

        def after(eng, *events):
            for e in events:
                engine, count = where[e]
                eng.wait_ge(side_sem[engine], count)

        def event(ins, name):
            engine, count = where[name]
            made[engine] += 1
            assert made[engine] == count, (name, made[engine], count)
            ins.then_inc(side_sem[engine], 1)

        def stepper(eng, s):
            count = [0]

            def step(ins):
                count[0] += 1
                ins.then_inc(s, 1)
                eng.wait_ge(s, count[0])
            return step

        def evac_engine(g):
            return "dve" if GROUP_LIST[g][0] in ("qk", "bm", "ba", "wo") else "act"

        def evacuated(eng, g):
            e = evac_engine(g)
            n = sum(1 for x in range(g + 1) if evac_engine(x) == e)
            eng.wait_ge(evac_dve if e == "dve" else evac_act, n)

        def raw_here(eng, item):
            n = POS[item]
            eng.wait_ge(raw_loaded[n % RAW], 16 * (n // RAW + 1))
            return raw[n % RAW]

        def used_up(eng, item):
            kind, n = item
            eng.wait_ge(lo_ready if kind == "w" else ada_done, n + 1)

        def block_source(item):
            kind, n = item
            if kind == "ada":
                c, h = n // 2, n % 2
                return A["ada_w"][0].rearrange("(p k) n -> p k n", k=KT)[:, KB * h:KB * (h + 1), c * NB:(c + 1) * NB]
            g, k0, _, _ = BLOCKS[n]
            name, c, _ = GROUP_LIST[g]
            w = {"bm": "w_branch_m", "ba": "w_branch_a", "wo": "w_out"}.get(name, "w_in")
            return A[w][0].rearrange("(k p) n -> p k n", p=P)[:, k0:k0 + KB, c:c + NB]

        def hm_bank(h, k):
            return ps[(2, 3, 4, 5)[2 * h + k // 2]][:, (k % 2) * T:(k % 2 + 1) * T]

        m_i, m_f, m_abs, m_lf, m_cum, m_ng, m_g, m_floor, m_den, m_ss, m_rec, m_tmp = range(12)
        block = ctx.enter_context(nc.Block())

        @block.sync
        def _(sp):
            sp.dma_start(cs[:], A["c"].rearrange("b (p k) -> (b p) k", k=KT)).then_inc(c_loaded, 16)
            sp.dma_start(x_in[:], A["x"][0].rearrange("(t p) n -> p t n", p=P)).then_inc(x_loaded, 16)
            for n, item in enumerate(STREAM):
                if n >= RAW:
                    used_up(sp, STREAM[n - RAW])
                sp.dma_start(raw[n % RAW][:], block_source(item)).then_inc(raw_loaded[n % RAW], 16)
                if item == ("w", BLK_IN + 4):
                    after(sp, "a_val3", "hm_t1")
                    sp.dma_start(g_ffn, A["norm_ffn_g"][0:1, :].broadcast_to([P, D])).then_inc(g_ffn_loaded, 16)
                    sp.dma_start(x_res[:], A["x"][0].rearrange("(t p) n -> p t n", p=P)).then_inc(x_again, 16)

            sources = (A["w_gate_e"][0], A["w_up_e"][0], A["w_down_e"][0])

            def load_chunk(c):
                w = sources[c % 3][(c // 3) % NE].rearrange("(k p) n -> p k n", p=P)
                dst = ring[c % CHUNKS][:].rearrange("p (k n) -> p k n", k=w.shape[1])
                sp.dma_start(dst, w).then_inc(ring_loaded[c % CHUNKS], 16)

            def refill(v, js):
                for j in js:
                    sp.wait_ge(down_done if j % 3 == 2 else gate_up_done, NE * v + (j // 3 + 1))
                    load_chunk(CHUNKS + j)

            sp.wait_ge(block_done, BLK_IN + 4)
            load_chunk(0)
            load_chunk(1)
            after(sp, "y_lo1")
            load_chunk(2)
            for n in range(2):
                used_up(sp, STREAM[-1])
                load_chunk(3 + n)
            sp.wait_ge(block_done, NBLK)
            for c in range(5, CHUNKS):
                load_chunk(c)
            after(sp, "x1_1")
            sp.dma_start(fin_g[:], A["final_norm_g"].rearrange("(a n) -> a n", a=1).broadcast_to([P, D])).then_inc(fin_loaded, 16)
            per_visit = 3 * NE
            refill(0, range(per_visit - CHUNKS))
            after(sp, "ranks")
            again = sp.value_load(many_i[0:1, 0:1], min_val=0, max_val=1)
            with sp.If(again == 1):
                refill(0, range(per_visit - CHUNKS, per_visit))
                with sp.Fori(1, VISITS - 1) as v:
                    refill(v, range(per_visit))
                refill(VISITS - 1, range(per_visit - CHUNKS))
            for t in range(TT):
                sp.wait_ge(out_ready, t + 1)
                sp.dma_start(out[0, t * P:(t + 1) * P, :], scratch[:, t, :]).then_inc(stored, 16)
            sp.wait_ge(stored, 16 * TT)

        @block.gpsimd
        def _(pool):
            step = stepper(pool, pool_step)
            nc.gpsimd.memset(acc_a[:], 0.0).then_inc(acc_zero, 1)
            nc.gpsimd.memset(mod[:], 0.0).then_inc(acc_zero, 1)
            step(nc.gpsimd.memset(ones[:], 1.0))
            step(nc.gpsimd.memset(neg_tri[:], 0.0))
            nc.gpsimd.affine_select(out=ident[:], in_=neg_tri[:], compare_op=ALU.not_equal, fill=1.0, base=0,
                                    pattern=[[-1, P]], channel_multiplier=1).then_inc(consts_ready, 1)
            nc.gpsimd.affine_select(out=tri_le[:], in_=ones[:], compare_op=ALU.is_ge, fill=0.0, base=0,
                                    pattern=[[1, P]], channel_multiplier=-1).then_inc(consts_ready, 1)
            pool.wait_ge(consts_ready, 2)
            nc.gpsimd.affine_select(out=neg_tri[:], in_=neg_tri[:], compare_op=ALU.is_ge, fill=NEG, base=0,
                                    pattern=[[1, P]], channel_multiplier=-1).then_inc(consts_ready, 1)
            nc.gpsimd.iota(dist_i, pattern=[[-1, T]], base=P, channel_multiplier=1).then_inc(consts_ready, 1)
            after(pool, "a_prob3")
            nc.gpsimd.iota(slot_id, pattern=[[1, SLOTS]], base=0, channel_multiplier=0,
                           allow_small_or_imprecise_dtypes=True).then_inc(consts_ready, 1)
            nc.gpsimd.affine_select(out=tri_lt, in_=ones[:], compare_op=ALU.is_ge, fill=0.0, base=-1,
                                    pattern=[[1, P]], channel_multiplier=-1).then_inc(consts_ready, 1)

        @block.scalar
        def _(act):
            A_ = nc.scalar.activation
            step = stepper(act, act_step)

            def split_hi(b):
                src = raw_here(act, ("w", b))
                if b >= RING:
                    act.wait_ge(block_done, b - RING + 1)
                nc.scalar.copy(hi[b % RING][:], src[:]).then_inc(hi_ready, 1)

            act.dma_start(rows[0:64, :], A["mlstm_conv"][0].rearrange("j (c p) -> (j c) p", p=P)).then_inc(rows_loaded, 16)
            act.dma_start(rows[64:72, :], A["norm_mix_g"][0].rearrange("(c p) -> c p", p=P)).then_inc(rows_loaded, 16)
            act.dma_start(rows[72:80, :], A["mlstm_norm_g"][0].rearrange("(c p) -> c p", p=P)).then_inc(rows_loaded, 16)
            act.wait_ge(acc_zero, 2)
            act.dma_start(acc_a[0:1, :], A["ada_b"][0:1, 0:2 * D]).then_inc(bias_loaded, 16)
            act.dma_start(mod[0:1, :, :], A["ada_b"][0:1, 2 * D:6 * D].rearrange("a (m n) -> a m n", m=4)).then_inc(bias_loaded, 16)
            act.wait_ge(c_loaded, 16)
            event(A_(cs[:], cs[:], ACT.Silu), "c_silu")
            act.wait_ge(x_loaded, 16)
            step(A_(h_m[:, 0, :], x_in[:, 0, :], ACT.Square, accum_out=st[:, 0:1]))
            event(A_(h_m[:, 0, :], x_in[:, 1, :], ACT.Square, accum_out=st[:, 1:2]), "x_ss")
            after(act, "x_var")
            event(A_(st[:, 4:6], st[:, 2:4], ACT.Sqrt), "x_sqrt")
            act.dma_start(w_if[:], A["w_in"][0].rearrange("(k p) n -> p k n", p=P)[:, :, IF_AT:IF_AT + IF_N]).then_inc(small_loaded, 16)
            act.dma_start(gate_b[:], A["mlstm_gate_b"][0:1, :].broadcast_to([P, IF_N])).then_inc(small_loaded, 16)
            act.dma_start(rw[:], A["router_w"].rearrange("(k p) n -> p k n", p=P)).then_inc(small_loaded, 16)
            act.dma_start(rb[:], A["router_b"].rearrange("(a n) -> a n", a=1).broadcast_to([P, NE])).then_inc(small_loaded, 16)
            for j in range(2):
                after(act, f"u_f32_{j}")
                half = slice(KB * j, KB * (j + 1))
                event(nc.scalar.copy(u_hi[:, half, :], u_f32[:, half, :]), f"u_hi{j}")
                split_hi(j)
            act.wait_ge(small_loaded, 64)
            event(nc.scalar.copy(wif_hi[:], w_if[:]), "wif_hi")

            for s in range(NBLK):
                if s + AHEAD < NBLK:
                    split_hi(s + AHEAD)
                g, _, _, end = BLOCKS[s]
                kind, _, _ = GROUP_LIST[g]
                if end and kind == "qk":
                    evacuated(act, g)
                    A_(qk_m[:, 4 * g:4 * g + 4, :], qk_m[:, 4 * g:4 * g + 4, :], ACT.Silu).then_inc(qk_ready, 1)
                elif end and evac_engine(g) == "act":
                    act.wait_ge(block_done, s + 1)
                    first = min(x for x, (n, _, _) in enumerate(GROUP_LIST) if n == kind)
                    j = g - first
                    banks = 2 * (g % 2), 2 * (g % 2) + 1
                    func = ACT.Sigmoid if kind in ("o", "gm", "ga") else ACT.Copy
                    if kind == "o" and j == 0:
                        after(act, "m_val3")
                    if kind == "gm" and j == 0:
                        after(act, "m_val3")
                    if kind == "qa" and j == 0:
                        after(act, "u_lo1")
                    dst = {"vm": v_m, "va": v_a, "o": sig_o, "qa": q_a, "ka": k_a, "gm": sig_gm, "ga": sig_ga}[kind]
                    for n, bank in enumerate(banks):
                        if kind in ("vm", "va", "o"):
                            view, src = dst[:, n, j * NB:(j + 1) * NB], ps[bank][:]
                        else:
                            view = dst[:, 4 * j + 2 * n:4 * j + 2 * n + 2, :]
                            src = ps[bank][:].rearrange("p (c t) -> p c t", c=2)
                        ins = A_(view, src, func)
                    ins.then_inc(evac_act, 1)

                if s == GATES_AT:
                    after(act, "gate_abs")
                    event(A_(gm[:, m_tmp], gm[:, m_abs], ACT.Exp, scale=-1.0), "gate_exp")
                    after(act, "gate_1p")
                    event(A_(gm[:, m_abs], gm[:, m_tmp], ACT.Ln), "gate_ln")
                if s == GATE_BACK_AT:
                    after(act, "m_neg")
                    event(A_(gm[:, m_floor], gm[:, m_tmp], ACT.Exp), "floor")
                if s in SCORE_M_AT:
                    h = SCORE_M_AT.index(s)
                    after(act, f"m_log{h}")
                    event(A_(w_m, w_m, ACT.Exp), f"m_exp{h}")
                if s in VALUE_M_AT:
                    h = VALUE_M_AT.index(s)
                    after(act, f"m_val{h}")
                    for t in range(TT):
                        nc.scalar.copy(gm[:, m_den, t, h:h + 1], ps[6 + t][:, MD:MD + 1])
                        nc.scalar.copy(h_m[:, t, h * MD:(h + 1) * MD], ps[6 + t][:, 0:MD])
                        ins = A_(bias_a[:], ps[6 + t][:, 0:MD], ACT.Square, accum_out=gm[:, m_ss, t, h:h + 1])
                        if t == 0:
                            step(ins)
                    event(ins, f"m_num{h}")
                if s == M_SCALE_AT:
                    after(act, "m_var")
                    event(A_(gm[:, m_tmp], gm[:, m_abs], ACT.Sqrt), "m_sqrt")
                if s in TURN_A_AT:
                    h = TURN_A_AT.index(s)
                    after(act, f"a_turn{h}")
                    for n in range(AG):
                        ins = nc.scalar.copy(turned[:, n, :], ps[4 + n][:, 0:384])
                    event(ins, f"a_turned{h}")
                if s in VALUE_A_AT:
                    h = VALUE_A_AT.index(s)
                    after(act, f"a_val{h}")
                    event(nc.scalar.copy(ha_f32[:, h, :], ps[7][:, 0:T]), f"a_out{h}")
                if s in SCORE_A_AT:
                    h = SCORE_A_AT.index(s)
                    after(act, f"a_max{h}")
                    A_(prob[:, 0:384], prob[:, 0:384], ACT.Exp, bias=am[:, 0:1], accum_out=am[:, 2:3])
                    event(A_(prob[:, 384:1152], prob[:, 384:1152], ACT.Exp, bias=am[:, 1:2], accum_out=am[:, 3:4]),
                          f"a_exp{h}")
                if s in M_TURN_AT:
                    h = M_TURN_AT.index(s)
                    after(act, f"hm_t{h}")
                    for k in range(KB):
                        ins = A_(hm_hi[:, KB * h + k, :], hm_bank(h, k), ACT.Copy, scale=vec[:, 72 + KB * h + k:73 + KB * h + k])
                    event(ins, f"hm_hi{h}")
                if s == M_TURN_AT[1]:
                    after(act, "a_out3")
                    event(nc.scalar.copy(ha_hi[:], ha_f32[:]), "ha_hi")
                if s in BCAST_AT:
                    i = BCAST_AT.index(s)
                    after(act, f"bcast{i}")
                    for n in range(2):
                        ins = nc.scalar.copy(mod[:, i, n * NB:(n + 1) * NB], ps[4 + 2 * (i % 2) + n][:])
                    event(ins, f"mod{i}")
                if s in (LAST_BLOCK[23], LAST_BLOCK[24]):
                    j = s - LAST_BLOCK[23]
                    half = slice(KB * j, KB * (j + 1))
                    after(act, f"y_f32_{j}")
                    event(nc.scalar.copy(y_hi[:, half, :], sig_gm[:, half, :]), f"y_hi{j}")
                if s in (LAST_BLOCK[25], LAST_BLOCK[26]):
                    j = s > LAST_BLOCK[25]
                    cols = slice(NB * j, NB * (j + 1))
                    after(act, f"x1_{int(j)}")
                    if j:
                        after(act, "x1_ss0")
                    step(A_(prob[:, 0:NB], x_res[:, 0, cols], ACT.Square, accum_out=st[:, 8 + 2 * j:9 + 2 * j]))
                    event(A_(prob[:, 0:NB], x_res[:, 1, cols], ACT.Square, accum_out=st[:, 9 + 2 * j:10 + 2 * j]),
                          f"x1_ss{int(j)}")

            after(act, "x1_var")
            event(A_(st[:, 24:26], st[:, 24:26], ACT.Sqrt), "x1_sqrt")
            for t in range(TT):
                after(act, f"u_ffn_t{t}")
                for n in range(2):
                    ins = nc.scalar.copy(u_ffn_t[:, 4 * n:4 * n + 4, t * P:(t + 1) * P],
                                         ps[4 + 2 * t + n][:].rearrange("p (c t) -> p c t", c=4))
                event(ins, f"ufT{t}")
            after(act, "logits")
            event(A_(rt[:, 0], ps[0][:, 0:TT * NE].rearrange("p (t e) -> p t e", t=TT), ACT.Sigmoid), "scores")

            def evacuate_gather(p, j):
                act.wait_ge(gathered, 2 * p + (j + 1))
                nc.scalar.copy(xe_t[:, KB * j:KB * (j + 1), :], ps[5 + 2 * j][:].rearrange("p (k s) -> p k s", k=KB)
                               ).then_inc(xe_ready, 1)

            def evacuate_turned(n):
                act.wait_ge(he_turned, n + 1)
                nc.scalar.copy(he_t[:], ps[6][:, 0:FF // P * SLOTS].rearrange("p (k s) -> p k s", k=FF // P)
                               ).then_inc(he_t_ready, 1)

            def work_pair(i, q):
                p, n = BODY // 2 * i + q, BODY * i + 2 * q
                act.wait_ge(gate_up_done, n + 1)
                act.wait_ge(scat_ready, p + 2)
                A_(sg[0:64, :], ps[4][64:128, :], ACT.Silu).then_inc(sg_ready, 1)
                evacuate_turned(n)
                act.wait_ge(gate_up_done, n + 2)
                act.wait_ge(he_ready, n + 1)
                A_(sg[64:128, :], ps[4][0:64, :], ACT.Silu).then_inc(sg_ready, 1)
                evacuate_gather(p + 1, 0)
                evacuate_turned(n + 1)
                evacuate_gather(p + 1, 1)

            evacuate_gather(0, 0)
            evacuate_gather(0, 1)
            with act.Fori(0, NE // BODY) as i:
                for q in range(BODY // 2):
                    work_pair(i, q)
            after(act, "ranks")
            again = act.value_load(many_i[0:1, 0:1], min_val=0, max_val=1)
            with act.If(again == 1):
                with act.Fori(NE // BODY, VISITS * NE // BODY) as i:
                    for q in range(BODY // 2):
                        work_pair(i, q)

            after(act, "x2")
            step(A_(u_ffn[:, 0, :], x_res[:, 0, :], ACT.Square, accum_out=st[:, 16:17]))
            event(A_(u_ffn[:, 0, :], x_res[:, 1, :], ACT.Square, accum_out=st[:, 17:18]), "x2_ss")
            after(act, "x2_var")
            event(A_(st[:, 20:22], st[:, 18:20], ACT.Sqrt), "x2_sqrt")

        @block.vector
        def _(dve):
            V = nc.vector
            step = stepper(dve, dve_step)

            def split_lo(b):
                dve.wait_ge(hi_ready, b + 1)
                src = raw[POS[("w", b)] % RAW]
                V.tensor_tensor(lo[b % RING][:], src[:], hi[b % RING][:].bitcast(F32), ALU.subtract
                                ).then_inc(lo_ready, 1)

            def ada(a):
                src = raw_here(dve, ("ada", a))
                if a % 2:
                    dve.wait_ge(ada_done, a)
                col = (a // 2) * NB
                dst = acc_a[:, col:col + NB] if a < ADA_FIRST else (
                    mod[:, (col - 2 * D) // D, (col % D):(col % D) + NB])
                for k in range(KB):
                    kk = KB * (a % 2) + k
                    ins = V.scalar_tensor_tensor(out=dst, in0=src[:, k, :], scalar=cs[:, kk:kk + 1], in1=dst,
                                                 op0=ALU.mult, op1=ALU.add)
                    if k < KB - 1:
                        step(ins)
                    else:
                        ins.then_inc(ada_done, 1)
                if a == ADA_FIRST - 1:
                    dve.wait_ge(ada_done, ADA_FIRST)

            def inv_rms(ss, var, name):
                event(V.tensor_scalar(var, ss, 1.0 / D, EPS, ALU.mult, ALU.add), name)

            after(dve, "x_ss")
            inv_rms(st[:, 0:2], st[:, 2:4], "x_var")
            after(dve, "x_sqrt")
            step(V.reciprocal(st[:, 6:8], st[:, 4:6]))
            for t in range(TT):
                ins = V.tensor_scalar(x_in[:, t, :], x_in[:, t, :], st[:, 6 + t:7 + t], None, ALU.mult)
            event(ins, "x_norm")
            after(dve, "vec_t")
            event(V.tensor_copy(vec[:], ps[0][:, 0:80]), "vec")
            after(dve, "c_silu")
            dve.wait_ge(bias_loaded, 32)
            for a in range(ADA_FIRST):
                ada(a)
            after(dve, "mod_col")
            step(V.tensor_copy(chan[:, 0:2, :], ps[1][:, 0:2 * KT].rearrange("p (a k) -> p a k", a=2)))
            step(V.scalar_tensor_tensor(out=chan[:, 2, :], in0=chan[:, 1, :], scalar=1.0, in1=vec[:, 64:72],
                                        op0=ALU.add, op1=ALU.mult))
            after(dve, "x_t")
            for j in range(2):
                for k in range(KB * j, KB * (j + 1)):
                    ins = V.tensor_scalar(u_f32[:, k, :], ps[4 + k // 2][:, (k % 2) * T:(k % 2 + 1) * T],
                                          chan[:, 2, k:k + 1], chan[:, 0, k:k + 1], ALU.mult, ALU.add)
                event(ins, f"u_f32_{j}")
            for j in range(2):
                after(dve, f"u_hi{j}")
                half = slice(KB * j, KB * (j + 1))
                event(V.tensor_tensor(u_lo[:, half, :], u_f32[:, half, :], u_hi[:, half, :].bitcast(F32), ALU.subtract),
                      f"u_lo{j}")
                split_lo(j)
            after(dve, "wif_hi")
            event(V.tensor_tensor(wif_lo[:], w_if[:], wif_hi[:].bitcast(F32), ALU.subtract), "wif_lo")

            for s in range(NBLK):
                if s + AHEAD < NBLK:
                    split_lo(s + AHEAD)
                g, _, _, end = BLOCKS[s]
                kind, col, _ = GROUP_LIST[g]
                banks = 2 * (g % 2), 2 * (g % 2) + 1
                if end and evac_engine(g) == "dve":
                    dve.wait_ge(block_done, s + 1)
                if end and kind == "qk":
                    src = [ps[banks[c // 2]][:, (c % 2) * T:(c % 2 + 1) * T] for c in range(4)]
                    for c in range(4):
                        ins = V.tensor_scalar(qk_m[:, 4 * g + c, :], src[c], vec[:, 3 * 16 + 4 * g + c:3 * 16 + 4 * g + c + 1],
                                              None, ALU.mult)
                    step(ins)
                    for back in (1, 2, 3):
                        for c in range(4):
                            tap = (3 - back) * 16 + 4 * g + c
                            dst = qk_m[:, 4 * g + c, back:T]
                            ins = V.scalar_tensor_tensor(out=dst, in0=src[c][:, 0:T - back], scalar=vec[:, tap:tap + 1],
                                                         in1=dst, op0=ALU.mult, op1=ALU.add)
                        if back < 3:
                            step(ins)
                    ins.then_inc(evac_dve, 1)
                if end and kind == "bm":
                    j = col // NB
                    for n, bank in enumerate(banks):
                        view = sig_gm[:, 4 * j + 2 * n:4 * j + 2 * n + 2, :]
                        ins = V.tensor_tensor(view, ps[bank][:].rearrange("p (c t) -> p c t", c=2), view, ALU.mult)
                    ins.then_inc(evac_dve, 1)
                if end and kind == "ba":
                    j = col // NB
                    for n, bank in enumerate(banks):
                        view = sig_ga[:, 4 * j + 2 * n:4 * j + 2 * n + 2, :]
                        ins = V.tensor_tensor(view, ps[bank][:].rearrange("p (c t) -> p c t", c=2), view, ALU.mult)
                    ins.then_inc(evac_dve, 1)
                    dve.wait_ge(evac_dve, 7 + j)
                    half = slice(KB * j, KB * (j + 1))
                    event(V.tensor_tensor(sig_gm[:, half, :], sig_gm[:, half, :], sig_ga[:, half, :], ALU.add), f"y_f32_{j}")
                    after(dve, f"y_hi{j}")
                    event(V.tensor_tensor(y_lo[:, half, :], sig_gm[:, half, :], y_hi[:, half, :].bitcast(F32), ALU.subtract),
                          f"y_lo{j}")
                if end and kind == "wo":
                    j = col // NB
                    if j == 0:
                        dve.wait_ge(x_again, 16)
                    for t in range(TT):
                        ins = V.tensor_tensor(scratch[:, t, col:col + NB], ps[banks[t]][:], mod[:, 0, col:col + NB], ALU.mult)
                    ins.then_inc(evac_dve, 1)
                    dve.wait_ge(evac_dve, 9 + j)
                    for t in range(TT):
                        view = x_res[:, t, col:col + NB]
                        ins = V.tensor_tensor(view, view, scratch[:, t, col:col + NB], ALU.add)
                    event(ins, f"x1_{j}")
                if s in ADA_AT:
                    ada(ADA_AT[s])

                if s == MASKS_AT:
                    dve.wait_ge(consts_ready, 4)
                    step(V.tensor_copy(dist[:], dist_i))
                    step(V.tensor_scalar(masks[:, 0, :], dist[:], float(PATTERNS[0][0] // PATTERNS[0][1]), NEG,
                                         ALU.is_gt, ALU.mult))
                    for n in (1, 2):
                        step(V.tensor_scalar(dist_m, dist_i, PATTERNS[n][1] - 1, None, ALU.bitwise_and))
                        step(V.tensor_scalar(masks[:, n, :], dist_m, 0.0, NEG, ALU.not_equal, ALU.mult))
                    step(V.tensor_scalar(bias_a[:], dist[:], 0.0, NEG, ALU.is_lt, ALU.mult))
                    for n in range(AG):
                        ins = V.tensor_tensor(masks[:, n, :], masks[:, n, :], bias_a[:], ALU.add)
                    event(ins, "masks")
                if s == GATES_AT:
                    after(dve, "gates")
                    for t in range(TT):
                        V.tensor_tensor(gm[:, m_i, t, :], ps[4][:, t * IF_N:t * IF_N + MH], gate_b[:, 0:MH], ALU.add)
                        ins = V.tensor_tensor(gm[:, m_f, t, :], ps[4][:, t * IF_N + MH:(t + 1) * IF_N], gate_b[:, MH:IF_N], ALU.add)
                    step(ins)
                    event(V.scalar_tensor_tensor(out=gm[:, m_abs], in0=gm[:, m_f], scalar=-1.0, in1=gm[:, m_f],
                                                 op0=ALU.mult, op1=ALU.max), "gate_abs")
                    after(dve, "gate_exp")
                    event(V.tensor_scalar(gm[:, m_tmp], gm[:, m_tmp], 1.0, None, ALU.add), "gate_1p")
                    after(dve, "gate_ln")
                    event(V.scalar_tensor_tensor(out=gm[:, m_lf], in0=gm[:, m_f], scalar=0.0, in1=gm[:, m_abs],
                                                 op0=ALU.min, op1=ALU.subtract), "lf")
                if s == CUMSUM_AT:
                    after(dve, "cumsum")
                    step(V.tensor_copy(gm[:, m_cum], ps[4][:, 0:TT * MH].rearrange("p (t h) -> p t h", t=TT)))
                    step(V.tensor_tensor(gm[:, m_g], gm[:, m_i], gm[:, m_cum], ALU.subtract))
                    event(V.tensor_scalar(gm[:, m_ng], gm[:, m_g], -1.0, None, ALU.mult), "neg_g")
                if s == GATE_T_AT:
                    after(dve, "gate_t")
                    step(V.tensor_copy(neg_row, ps[5][0:MH, 0:T]))
                    event(V.tensor_tensor_scan(run_row[:], neg_row, neg_row, 0.0, ALU.min, ALU.min), "run_min")
                if s == GATE_BACK_AT:
                    after(dve, "gate_back")
                    event(V.tensor_tensor(gm[:, m_tmp], ps[4][:, 0:TT * MH].rearrange("p (t h) -> p t h", t=TT),
                                          gm[:, m_cum], ALU.subtract), "m_neg")
                if s in SCORE_M_AT:
                    h = SCORE_M_AT.index(s)
                    after(dve, f"m_score{h}")
                    V.scalar_tensor_tensor(out=w_m[:, 0:P], in0=ps[4][:, 0:P], scalar=gm[:, m_g, 0, h:h + 1],
                                           in1=neg_tri[:], op0=ALU.add, op1=ALU.add)
                    V.tensor_scalar(w_m[:, P:2 * P], ps[4][:, P:2 * P], gm[:, m_g, 0, h:h + 1], None, ALU.add)
                    event(V.scalar_tensor_tensor(out=w_m[:, 2 * P:3 * P], in0=ps[4][:, P:2 * P], scalar=gm[:, m_g, 1, h:h + 1],
                                                 in1=neg_tri[:], op0=ALU.add, op1=ALU.add), f"m_log{h}")
                    after(dve, f"m_exp{h}")
                    event(V.scalar_tensor_tensor(out=p_m, in0=ps[5][:, 0:384], scalar=MD ** -0.5, in1=w_m,
                                                 op0=ALU.mult, op1=ALU.mult), f"m_p{h}")
                if s == M_SCALE_AT:
                    after(dve, "m_num3", "floor")
                    step(V.scalar_tensor_tensor(out=gm[:, m_den], in0=gm[:, m_den], scalar=-1.0, in1=gm[:, m_den],
                                                op0=ALU.mult, op1=ALU.max))
                    step(V.tensor_tensor(gm[:, m_den], gm[:, m_den], gm[:, m_floor], ALU.max))
                    step(V.reciprocal(gm[:, m_rec], gm[:, m_den]))
                    step(V.tensor_tensor(gm[:, m_abs], gm[:, m_ss], gm[:, m_rec], ALU.mult))
                    step(V.tensor_tensor(gm[:, m_abs], gm[:, m_abs], gm[:, m_rec], ALU.mult))
                    event(V.tensor_scalar(gm[:, m_abs], gm[:, m_abs], 1.0 / MD, EPS, ALU.mult, ALU.add), "m_var")
                    after(dve, "m_sqrt")
                    step(V.reciprocal(gm[:, m_tmp], gm[:, m_tmp]))
                    event(V.tensor_tensor(gm[:, m_rec], gm[:, m_rec], gm[:, m_tmp], ALU.mult), "m_scale")
                if s in SCORE_A_AT:
                    h = SCORE_A_AT.index(s)
                    after(dve, f"a_score{h}")
                    if h:
                        after(dve, f"a_turn{h - 1}")
                    for n in range(AG):
                        head = n * AM + h
                        slope = 2.0 ** (-8.0 * (head + 1) / AH)
                        step(V.scalar_tensor_tensor(out=bias_a[:], in0=dist[:], scalar=-slope, in1=masks[:, n, :],
                                                    op0=ALU.mult, op1=ALU.add))
                        V.scalar_tensor_tensor(out=prob[:, n * P:(n + 1) * P], in0=ps[4][:, n * P:(n + 1) * P],
                                               scalar=AD ** -0.5, in1=bias_a[:, P:T], op0=ALU.mult, op1=ALU.add)
                        src = ps[5][:, n * T:(n + 1) * T] if n < 2 else ps[6][:, 0:T]
                        step(V.scalar_tensor_tensor(out=prob[:, 384 + n * T:384 + (n + 1) * T], in0=src,
                                                    scalar=AD ** -0.5, in1=bias_a[:], op0=ALU.mult, op1=ALU.add))
                    V.tensor_reduce(am[:, 0:1], prob[:, 0:384], AX_X, ALU.max, negate=True)
                    event(V.tensor_reduce(am[:, 1:2], prob[:, 384:1152], AX_X, ALU.max, negate=True), f"a_max{h}")
                    after(dve, f"a_exp{h}")
                    step(V.reciprocal(am[:, 4:6], am[:, 2:4]))
                    V.tensor_scalar(prob[:, 0:384], prob[:, 0:384], am[:, 4:5], None, ALU.mult)
                    event(V.tensor_scalar(prob[:, 384:1152], prob[:, 384:1152], am[:, 5:6], None, ALU.mult), f"a_prob{h}")
                if s == M_OUT_AT:
                    evacuated(dve, 16)
                    for t in range(TT):
                        for h in range(MH):
                            view = h_m[:, t, h * MD:(h + 1) * MD]
                            ins = V.scalar_tensor_tensor(out=view, in0=view, scalar=gm[:, m_rec, t, h:h + 1],
                                                         in1=sig_o[:, t, h * MD:(h + 1) * MD], op0=ALU.mult, op1=ALU.mult)
                    event(ins, "h_m")
                if s in M_TURN_AT:
                    h = M_TURN_AT.index(s)
                    after(dve, f"hm_hi{h}")
                    for k in range(KB):
                        kk = KB * h + k
                        ins = V.scalar_tensor_tensor(out=hm_lo[:, kk, :], in0=hm_bank(h, k), scalar=vec[:, 72 + kk:73 + kk],
                                                     in1=hm_hi[:, kk, :].bitcast(F32), op0=ALU.mult, op1=ALU.subtract)
                    event(ins, f"hm_lo{h}")
                if s == M_TURN_AT[1]:
                    after(dve, "ha_hi")
                    event(V.tensor_tensor(ha_lo[:], ha_f32[:], ha_hi[:].bitcast(F32), ALU.subtract), "ha_lo")
                if s == BCAST_AT[-1]:
                    after(dve, "mod3")
                    dve.wait_ge(g_ffn_loaded, 16)
                    event(V.scalar_tensor_tensor(out=mod[:, 2, :], in0=mod[:, 2, :], scalar=1.0, in1=g_ffn,
                                                 op0=ALU.add, op1=ALU.mult), "scale_ffn")

            after(dve, "x1_ss0", "x1_ss1")
            step(V.tensor_tensor(st[:, 24:26], st[:, 8:10], st[:, 10:12], ALU.add))
            inv_rms(st[:, 24:26], st[:, 24:26], "x1_var")
            after(dve, "x1_sqrt")
            step(V.reciprocal(st[:, 14:16], st[:, 24:26]))
            for t in range(TT):
                step(V.scalar_tensor_tensor(out=u_ffn[:, t, :], in0=x_res[:, t, :], scalar=st[:, 14 + t:15 + t],
                                            in1=mod[:, 2, :], op0=ALU.mult, op1=ALU.mult))
                event(V.tensor_tensor(u_ffn[:, t, :], u_ffn[:, t, :], mod[:, 1, :], ALU.add), f"u_ffn{t}")
            event(V.memset(zeros[:], 0.0), "zero")
            V.memset(slot_tab[:, :, VISITS * NE:VISITS * NE + 2], -1.0)
            V.memset(comb_tab[:, :, VISITS * NE:VISITS * NE + 2], 0.0)

            SC, SEL, IN, T1, T2, OH1, OH2, KEY, W, PICK, R = range(11)

            ramp = rt[:, 15, 0, :]

            for j in range(NE):
                ins = V.memset(ramp[:, j:j + 1], float(NE - j))
            step(ins)
            after(dve, "scores")
            for t in range(TT):
                ins = V.tensor_tensor(rt[:, SEL, t, :], rt[:, SC, t, :], rb[:], ALU.add)
            step(ins)
            sel4 = rt[:, SEL].rearrange("p t (g j) -> p (t g) j", j=PER)
            pairs = rt[:, 12:15].rearrange("p a t e -> p (a t e)")[:, 0:TT * GROUPS * 6].rearrange("p (g j) -> p g j", j=6)
            n = 0
            for a in range(PER):
                for b in range(a + 1, PER):
                    ins = V.tensor_tensor(pairs[:, :, n:n + 1], sel4[:, :, a:a + 1], sel4[:, :, b:b + 1], ALU.add)
                    n += 1
            step(ins)
            gscore = rt[:, T1].rearrange("p t e -> p (t e)")[:, 0:TT * GROUPS]
            step(V.tensor_reduce(gscore, pairs, AX_X, ALU.max))

            def one_hot_first(src3, best, key, dst3, width):
                step(V.tensor_reduce(best, src3, AX_X, ALU.max))
                for t in range(TT):
                    ins = V.scalar_tensor_tensor(out=key[:, t, :], in0=src3[:, t, :], scalar=best[:, t:t + 1],
                                                 in1=ramp[:, 0:width], op0=ALU.is_equal, op1=ALU.mult)
                step(ins)
                step(V.tensor_reduce(best, key, AX_X, ALU.max))
                for t in range(TT):
                    ins = V.tensor_scalar(dst3[:, t, :], key[:, t, :], best[:, t:t + 1], None, ALU.is_equal)
                step(ins)

            best = st[:, 24:26]
            gs3 = gscore.rearrange("p (t g) -> p t g", t=TT)
            key4 = rt[:, KEY, :, 0:GROUPS]
            ing = rt[:, T2, :, 0:GROUPS]
            one_hot_first(gs3, best, key4, ing, GROUPS)
            step(V.tensor_scalar(ing, ing, 1.0, -NEG, ALU.subtract, ALU.mult))
            for t in range(TT):
                for gi in range(GROUPS):
                    ins = V.tensor_scalar(rt[:, IN, t, gi * PER:(gi + 1) * PER], rt[:, SEL, t, gi * PER:(gi + 1) * PER],
                                          ing[:, t, gi:gi + 1], None, ALU.add)
            step(ins)
            one_hot_first(rt[:, IN], best, rt[:, KEY], rt[:, OH1], NE)
            step(V.scalar_tensor_tensor(out=rt[:, IN], in0=rt[:, OH1], scalar=2 * NEG, in1=rt[:, IN],
                                        op0=ALU.mult, op1=ALU.add))
            one_hot_first(rt[:, IN], best, rt[:, KEY], rt[:, OH2], NE)
            step(V.tensor_tensor(rt[:, PICK], rt[:, OH1], rt[:, OH2], ALU.add))
            step(V.tensor_tensor(rt[:, W], rt[:, PICK], rt[:, SC], ALU.mult))
            step(V.tensor_reduce(st[:, 26:28], rt[:, W], AX_X, ALU.add))
            step(V.reciprocal(st[:, 28:30], st[:, 26:28]))
            for t in range(TT):
                for v in range(VISITS):
                    ins = V.tensor_scalar(comb_tab[:, t, v * NE:(v + 1) * NE], rt[:, W, t, :], st[:, 28 + t:29 + t], None, ALU.mult)
            event(ins, "router")
            after(dve, "rank_sums")
            for t in range(TT):
                ins = V.scalar_tensor_tensor(out=rt[:, R, t, :], in0=ps[4][:, t * NE:(t + 1) * NE], scalar=1.0,
                                             in1=rt[:, PICK, t, :], op0=ALU.add, op1=ALU.mult)
            step(ins)
            for t in range(TT):
                for v in range(VISITS):
                    ins = V.tensor_scalar(slot_tab[:, t, v * NE:(v + 1) * NE], rt[:, R, t, :], -1.0 - v * SLOTS, None, ALU.add)
            step(ins)
            step(V.tensor_reduce(many[:, 0:1], ps[4][:, TT * NE:(TT + 1) * NE], AX_X, ALU.max))
            event(V.tensor_scalar(many_i[:, 0:1], many[:, 0:1], float(SLOTS), None, ALU.is_gt), "ranks")
            V.memset(scat[1][:], 0.0).then_inc(scat_ready, 1)
            after(dve, "logits")
            V.memset(y_e[:], 0.0).then_inc(y_ready, 1)

            def build_onehot(p):
                V.tensor_copy(w_pair[:], comb_tab[:, :, bass.ds(2 * p, 2)])
                for t in range(TT):
                    for s in range(2):
                        ins = V.tensor_scalar(onehot[:, t, s * SLOTS:(s + 1) * SLOTS], slot_id,
                                              slot_tab[:, t, bass.ds(2 * p + s, 1)], None, ALU.is_equal)
                ins.then_inc(onehot_ready, 1)

            def evacuate_slots(p, side):
                dve.wait_ge(slots_turned, p + 1)
                V.tensor_copy(scat[side][:], ps[6][:, 0:T + 2]).then_inc(scat_ready, 1)

            def weigh(n, s, side):
                dve.wait_ge(sg_ready, n + 1)
                rows_s = slice(64 * s, 64 * s + 64)
                V.scalar_tensor_tensor(out=he[rows_s, :], in0=ps[4][rows_s, :], scalar=scat[side][rows_s, T + s:T + s + 1],
                                       in1=sg[rows_s, :], op0=ALU.mult, op1=ALU.mult).then_inc(he_ready, 1)

            def evacuate_down(n, s):
                dve.wait_ge(down_done, n + 1)
                for h in range(2):
                    ins = V.tensor_copy(y_e[64 * s:64 * s + 64, h * NB:(h + 1) * NB], ps[6][64 * h:64 * h + 64, :])
                ins.then_inc(y_ready, 1)

            def work_pair(i, q):
                p, n = BODY // 2 * i + q, BODY * i + 2 * q
                dve.wait_ge(gathered, 2 * p + 2)
                build_onehot(p + 1)
                dve.wait_ge(scat_ready, p + 2)
                weigh(n, 0, q % 2)
                evacuate_down(n, 0)
                weigh(n + 1, 1, q % 2)
                evacuate_slots(p + 1, (q + 1) % 2)
                evacuate_down(n + 1, 1)

            dve.wait_ge(consts_ready, 6)
            build_onehot(0)
            evacuate_slots(0, 0)
            with dve.Fori(0, NE // BODY) as i:
                for q in range(BODY // 2):
                    work_pair(i, q)
            after(dve, "ranks")
            again = dve.value_load(many_i[0:1, 0:1], min_val=0, max_val=1)
            with dve.If(again == 1):
                with dve.Fori(NE // BODY, VISITS * NE // BODY) as i:
                    for q in range(BODY // 2):
                        work_pair(i, q)

            dve.wait_ge(moe_done, 1)
            for t in range(TT):
                for h in range(2):
                    ins = V.tensor_tensor(scratch[:, t, h * NB:(h + 1) * NB], ps[2 * t + h][:],
                                          mod[:, 3, h * NB:(h + 1) * NB], ALU.mult)
            step(ins)
            event(V.tensor_tensor(x_res[:], x_res[:], scratch[:], ALU.add), "x2")
            after(dve, "x2_ss")
            inv_rms(st[:, 16:18], st[:, 18:20], "x2_var")
            after(dve, "x2_sqrt")
            step(V.reciprocal(st[:, 22:24], st[:, 20:22]))
            dve.wait_ge(fin_loaded, 16)
            for t in range(TT):
                V.scalar_tensor_tensor(out=scratch[:, t, :], in0=x_res[:, t, :], scalar=st[:, 22 + t:23 + t],
                                       in1=fin_g[:], op0=ALU.mult, op1=ALU.mult).then_inc(out_ready, 1)

        @block.tensor
        def _(pe):
            mm, tr = nc.tensor.matmul, nc.tensor.transpose

            pe.wait_ge(consts_ready, 2)
            pe.wait_ge(rows_loaded, 48)
            event(tr(ps[0][:, 0:80], rows[0:80, :], ident[0:80, 0:80]), "vec_t")
            after(pe, "x_norm")
            for k in range(KT):
                for t in range(TT):
                    ins = tr(ps[4 + k // 2][:, (k % 2) * T + t * P:(k % 2) * T + (t + 1) * P],
                             x_in[:, t, k * P:(k + 1) * P], ident[:])
            event(ins, "x_t")
            for n in range(2 * KT):
                if n in (0, KT, KT + KT // 2):
                    pe.wait_ge(ada_done, {0: 4, KT: 6, KT + KT // 2: 8}[n])
                ins = mm(ps[1][:, n:n + 1], acc_a[:, n * P:(n + 1) * P], ones[:, 0:1], start=True, stop=True)
            event(ins, "mod_col")

            for s, (g, k0, first, end) in enumerate(BLOCKS):
                kind, _, channel_major = GROUP_LIST[g]
                if s < 2:
                    after(pe, f"u_lo{s}")
                if s == 0:
                    after(pe, "u_f32_1")
                if first and g >= 2:
                    evacuated(pe, g - 2)
                if g == 21:
                    after(pe, f"hm_lo{k0 // KB}")
                if g == 23:
                    after(pe, "ha_lo")
                if g == 25:
                    after(pe, f"y_lo{k0 // KB}")
                x_hi, x_lo = {"bm": (hm_hi, hm_lo), "ba": (ha_hi, ha_lo), "wo": (y_hi, y_lo)}.get(kind, (u_hi, u_lo))
                pe.wait_ge(lo_ready, s + 1)
                w_hi, w_lo = hi[s % RING], lo[s % RING]
                banks = 2 * (g % 2), 2 * (g % 2) + 1
                if channel_major:
                    for c in range(4):
                        dst = ps[banks[c // 2]][:, (c % 2) * T:(c % 2 + 1) * T]
                        cols = slice(c * P, (c + 1) * P)
                        for k in range(KB):
                            for n, (w, x) in enumerate(((w_hi, x_hi), (w_hi, x_lo), (w_lo, x_hi))):
                                ins = mm(dst, w[:, k, cols], x[:, k0 + k, :],
                                         start=(first and c % 2 == 0 and k == 0 and n == 0),
                                         stop=(end and k == KB - 1 and n == 2), skip_group_check=True)
                else:
                    for t in range(TT):
                        rows_t = slice(t * P, (t + 1) * P)
                        for k in range(KB):
                            for n, (w, x) in enumerate(((w_hi, x_hi), (w_hi, x_lo), (w_lo, x_hi))):
                                ins = mm(ps[banks[t]][:], x[:, k0 + k, rows_t], w[:, k, :],
                                         start=(first and k == 0 and n == 0), stop=(end and k == KB - 1 and n == 2))
                ins.then_inc(block_done, 1)

                if s == GATES_AT:
                    after(pe, "wif_lo")
                    for t in range(TT):
                        for k in range(KT):
                            for n, (w, x) in enumerate(((wif_hi, u_hi), (wif_hi, u_lo), (wif_lo, u_hi))):
                                ins = mm(ps[4][:, t * IF_N:(t + 1) * IF_N], x[:, k, t * P:(t + 1) * P], w[:, k, :],
                                         start=(k == 0 and n == 0), stop=(k == KT - 1 and n == 2))
                    event(ins, "gates")
                if s == CUMSUM_AT:
                    after(pe, "lf")
                    mm(ps[4][:, 0:MH], tri_le[:], gm[:, m_lf, 0, :], start=True, stop=True)
                    mm(ps[4][:, MH:2 * MH], ones[:], gm[:, m_lf, 0, :], start=True, stop=False)
                    event(mm(ps[4][:, MH:2 * MH], tri_le[:], gm[:, m_lf, 1, :], start=False, stop=True), "cumsum")
                if s == GATE_T_AT:
                    after(pe, "neg_g")
                    for t in range(TT):
                        ins = tr(ps[5][0:MH, t * P:(t + 1) * P], gm[:, m_ng, t, :], ident[:])
                    event(ins, "gate_t")
                if s == GATE_BACK_AT:
                    after(pe, "run_min")
                    for t in range(TT):
                        ins = tr(ps[4][:, t * MH:(t + 1) * MH], run_row[:, t * P:(t + 1) * P], ident[0:MH, 0:MH])
                    event(ins, "gate_back")
                if s in SCORE_M_AT:
                    h = SCORE_M_AT.index(s)
                    if h == 0:
                        pe.wait_ge(qk_ready, 4)
                        after(pe, "m_neg")
                    else:
                        after(pe, f"m_p{h - 1}")
                    mm(ps[4][:, 0:T], ident[0:MH, h:h + 1].broadcast_to([MH, P]), run_row[:], start=True, stop=True)
                    for k in range(2):
                        mm(ps[5][:, 0:T], qk_m[:, KT + 2 * h + k, 0:P], qk_m[:, 2 * h + k, :], start=(k == 0), stop=(k == 1))
                    for k in range(2):
                        ins = mm(ps[5][:, T:T + P], qk_m[:, KT + 2 * h + k, P:T], qk_m[:, 2 * h + k, P:T],
                                 start=(k == 0), stop=(k == 1))
                    event(ins, f"m_score{h}")
                if s in VALUE_M_AT:
                    h = VALUE_M_AT.index(s)
                    after(pe, f"m_p{h}")
                    if h == 0:
                        evacuated(pe, 5)
                    else:
                        after(pe, f"m_num{h - 1}")
                    for t, parts in ((0, ((0, 0),)), (1, ((P, 0), (2 * P, 1)))):
                        for n, (at_p, sk) in enumerate(parts):
                            mm(ps[6 + t][:, 0:MD], p_m[:, at_p:at_p + P], v_m[:, sk, h * MD:(h + 1) * MD],
                               start=(n == 0), stop=(n == len(parts) - 1))
                        for n, (at_p, sk) in enumerate(parts):
                            ins = mm(ps[6 + t][:, MD:MD + 1], p_m[:, at_p:at_p + P], ones[:, 0:1],
                                     start=(n == 0), stop=(n == len(parts) - 1))
                    event(ins, f"m_val{h}")
                if s in TURN_A_AT:
                    h = TURN_A_AT.index(s)
                    after(pe, f"a_prob{h}")
                    for n in range(AG):
                        for m, src in enumerate((prob[:, n * P:(n + 1) * P], prob[:, 384 + n * T:384 + n * T + P],
                                                 prob[:, 384 + n * T + P:384 + (n + 1) * T])):
                            ins = tr(ps[4 + n][:, m * P:(m + 1) * P], src, ident[:])
                    event(ins, f"a_turn{h}")
                if s in VALUE_A_AT:
                    h = VALUE_A_AT.index(s)
                    after(pe, f"a_turned{h}")
                    if h:
                        after(pe, f"a_out{h - 1}")
                    else:
                        after(pe, "m_num3")
                    for n in range(AG):
                        cols = slice((n * AM + h) * AD, (n * AM + h + 1) * AD)
                        mm(ps[7][:, 0:T], v_a[:, 0, cols], turned[:, n, 0:T], start=(n == 0), stop=False, skip_group_check=True)
                        ins = mm(ps[7][:, P:T], v_a[:, 1, cols], turned[:, n, T:384], start=False, stop=(n == AG - 1),
                                 skip_group_check=True)
                    event(ins, f"a_val{h}")
                if s in SCORE_A_AT:
                    h = SCORE_A_AT.index(s)
                    if h == 0:
                        evacuated(pe, 14)
                        after(pe, "m_p3", "masks")
                    else:
                        after(pe, f"a_turned{h - 1}")
                    for n in range(AG):
                        head = n * AM + h
                        mm(ps[4][:, n * P:(n + 1) * P], q_a[:, head, 0:P], k_a[:, head, 0:P], start=True, stop=True)
                        dst = ps[5][:, n * T:(n + 1) * T] if n < 2 else ps[6][:, 0:T]
                        ins = mm(dst, q_a[:, head, P:T], k_a[:, head, :], start=True, stop=True)
                    event(ins, f"a_score{h}")
                if s in M_TURN_AT:
                    h = M_TURN_AT.index(s)
                    if h == 0:
                        after(pe, "h_m")
                        evacuated(pe, 19)
                    else:
                        after(pe, "a_turned3")
                    for k in range(KB):
                        for t in range(TT):
                            ins = tr(hm_bank(h, k)[:, t * P:(t + 1) * P],
                                     h_m[:, t, (KB * h + k) * P:(KB * h + k + 1) * P], ident[:])
                    event(ins, f"hm_t{h}")
                if s in BCAST_AT:
                    i = BCAST_AT.index(s)
                    if i == 0:
                        pe.wait_ge(ada_done, ADA_FIRST + ADA_REST)
                        after(pe, "hm_lo1")
                    elif i == 1:
                        after(pe, "a_out3")
                    else:
                        after(pe, f"mod{i - 2}")
                    for n in range(2):
                        ins = mm(ps[4 + 2 * (i % 2) + n][:], ones[:], mod[:, i, n * NB:(n + 1) * NB], start=True, stop=True)
                    event(ins, f"bcast{i}")

            after(pe, "mod3")
            for t in range(TT):
                after(pe, f"u_ffn{t}")
                for k in range(KT):
                    ins = tr(ps[4 + 2 * t + k // 4][:, (k % 4) * P:(k % 4 + 1) * P], u_ffn[:, t, k * P:(k + 1) * P], ident[:])
                event(ins, f"u_ffn_t{t}")
            evacuated(pe, 26)
            for t in range(TT):
                after(pe, f"ufT{t}")
                for k in range(KT):
                    ins = mm(ps[0][:, t * NE:(t + 1) * NE], u_ffn_t[:, k, t * P:(t + 1) * P], rw[:, k, :],
                             start=(k == 0), stop=(k == KT - 1))
            event(ins, "logits")
            after(pe, "zero", "scores")
            for b in range(4):
                ins = mm(ps[b][:], zeros[:, 0:P], zeros[:], start=True, stop=False, skip_group_check=True)
            event(ins, "acc_zeroed")
            after(pe, "router")
            pe.wait_ge(consts_ready, 6)
            pick = rt[:, 9]
            mm(ps[4][:, 0:NE], tri_lt, pick[:, 0, :], start=True, stop=True)
            mm(ps[4][:, NE:2 * NE], ones[:], pick[:, 0, :], start=True, stop=False)
            mm(ps[4][:, NE:2 * NE], tri_lt, pick[:, 1, :], start=False, stop=True)
            mm(ps[4][:, 2 * NE:3 * NE], ones[:], pick[:, 0, :], start=True, stop=False)
            event(mm(ps[4][:, 2 * NE:3 * NE], ones[:], pick[:, 1, :], start=False, stop=True), "rank_sums")

            def turn_slots(p):
                pe.wait_ge(onehot_ready, p + 1)
                for t in range(TT):
                    tr(ps[6][:, t * P:(t + 1) * P], onehot[:, t, :], ident[:])
                for t in range(TT):
                    ins = mm(ps[6][:, T:T + 2], onehot[:, t, :], w_pair[:, t, :], start=(t == 0), stop=(t == TT - 1))
                ins.then_inc(slots_turned, 1)

            def gather(j):
                for k in range(KB):
                    for t in range(TT):
                        ins = mm(ps[5 + 2 * j][:, k * P:(k + 1) * P], u_ffn[:, t, (KB * j + k) * P:(KB * j + k + 1) * P],
                                 onehot[:, t, :], start=(t == 0), stop=(t == TT - 1))
                ins.then_inc(gathered, 1)

            def scatter(side, t):
                for h in range(2):
                    ins = mm(ps[2 * t + h][:], scat[side][:, t * P:(t + 1) * P], y_e[:, h * NB:(h + 1) * NB],
                             start=False, stop=False, skip_group_check=True)
                return ins

            def chunk(i, m, w):
                c = 3 * m + w
                pe.wait_ge(ring_loaded[c % CHUNKS], 16 * (3 * BODY // CHUNKS) * i + 16 * (c // CHUNKS + 1))
                return ring[c % CHUNKS][:].rearrange("p (k n) -> p k n", k=FF // P if w == 2 else KT)

            def gate_up(i, m, s):
                w_gate, w_up = chunk(i, m, 0), chunk(i, m, 1)
                up, gate = ps[4][64 * s:64 * s + 64, :], ps[4][64 * (1 - s):64 * (1 - s) + 64, :]
                for k in range(KT):
                    x = xe_t[:, k, s * SLOTS:(s + 1) * SLOTS]
                    mm(gate, x, w_gate[:, k, :], start=(k == 0), stop=(k == KT - 1))
                    ins = mm(up, x, w_up[:, k, :], start=(k == 0), stop=(k == KT - 1))
                ins.then_inc(gate_up_done, 1)

            def turn_he(n, s):
                pe.wait_ge(he_ready, n + 1)
                half = slice(64 * s, 64 * s + 64)
                for k in range(FF // P):
                    ins = mm(ps[6][:, k * SLOTS:(k + 1) * SLOTS], he[half, k * P:(k + 1) * P], ident[half, half],
                             start=True, stop=True)
                ins.then_inc(he_turned, 1)

            def down(i, m, n):
                pe.wait_ge(he_t_ready, n + 1)
                w_down = chunk(i, m, 2)
                for k in range(FF // P):
                    for h in range(2):
                        ins = mm(ps[6][64 * h:64 * h + 64, :], he_t[:, k, :], w_down[:, k, h * NB:(h + 1) * NB],
                                 start=(k == 0), stop=(k == FF // P - 1))
                ins.then_inc(down_done, 1)

            def work_pair(i, q):
                p, n = BODY // 2 * i + q, BODY * i + 2 * q
                pe.wait_ge(xe_ready, 2 * p + 2)
                pe.wait_ge(scat_ready, p + 2)
                gate_up(i, 2 * q, 0)
                pe.wait_ge(y_ready, n + 1)
                scatter((q + 1) % 2, 0)
                turn_he(n, 0)
                scatter((q + 1) % 2, 1)
                down(i, 2 * q, n)
                pe.wait_ge(he_ready, n + 1)
                gate_up(i, 2 * q + 1, 1)
                pe.wait_ge(y_ready, n + 2)
                turn_slots(p + 1)
                gather(0)
                pe.wait_ge(scat_ready, p + 3)
                turn_he(n + 1, 1)
                gather(1)
                down(i, 2 * q + 1, n + 1)

            turn_slots(0)
            gather(0)
            gather(1)
            with pe.Fori(0, NE // BODY) as i:
                for q in range(BODY // 2):
                    work_pair(i, q)
            pe.wait_ge(y_ready, NE + 1)
            after(pe, "ranks")
            again = pe.value_load(many_i[0:1, 0:1], min_val=0, max_val=1)
            with pe.If(again == 1):
                with pe.Fori(NE // BODY, VISITS * NE // BODY) as i:
                    for q in range(BODY // 2):
                        work_pair(i, q)
                pe.wait_ge(y_ready, VISITS * NE + 1)
            for t in range(TT):
                ins = scatter(1, t)
            ins.then_inc(moe_done, 1)


_INS = ["x", "c", "ada_w", "ada_b", "w_in", "mlstm_conv", "mlstm_gate_b", "mlstm_norm_g", "w_branch_m", "w_branch_a",
        "w_out", "router_w", "router_b", "w_gate_e", "w_up_e", "w_down_e", "norm_mix_g", "norm_ffn_g", "final_norm_g"]
_OUTS = [((1, 256, 1024), "float32")]


def kernel(**inputs):
    import numpy as _np
    import concourse.bacc as _bacc
    from concourse import mybir as _mybir
    from concourse.bass_utils import run_bass_kernel_spmd as _run

    nc = _bacc.Bacc("TRN2", target_bir_lowering=False, num_devices=1)
    arrays, aps = {}, {}
    for name in _INS:
        a = _np.ascontiguousarray(inputs[name])
        arrays[f"in_{name}_dram"] = a
        aps[name] = nc.dram_tensor(f"in_{name}_dram", a.shape, _mybir.dt.from_np(a.dtype), kind="ExternalInput").ap()
    shape, dtype = _OUTS[0]
    out = nc.dram_tensor("out_0_dram", shape, _mybir.dt.from_np(_np.dtype(dtype)), kind="ExternalOutput").ap()
    build(nc, aps, out)
    r = _run(nc, [arrays], core_ids=[0])
    return r.results[0]["out_0_dram"]
```

```python
import math
from contextlib import ExitStack

import concourse.bass as bass
from concourse import mybir

ALU = mybir.AluOpType
ACT = mybir.ActivationFunctionType
F32 = mybir.dt.float32
F32R = mybir.dt.float32r
I32 = mybir.dt.int32
AX_X = mybir.AxisListType.X

P = 128
D = 1024
KT = D // P
T = 256
TT = T // P
NB = 512
KB = 4
EPS = 1e-6
NEG = -1e30
MH, MD = 4, 256
AH, AD, AG = 12, 128, 3
AM = AH // AG
PATTERNS = ((128, 1), (512, 4), (2048, 16))
NE, FF = 16, 512
GROUPS, PER = 4, 4
SLOTS = 64
VISITS = T // SLOTS
RAW, RING = 4, 3
IF_AT = 4 * D
IF_N = 2 * MH

IN_GROUPS = (
    [("qk", c, True) for c in range(0, 2 * D, NB)]
    + [("vm", c, False) for c in range(2 * D, 3 * D, NB)]
    + [("qa", c, True) for c in range(IF_AT + IF_N, IF_AT + IF_N + 1536, NB)]
    + [("ka", c, True) for c in range(IF_AT + IF_N + 1536, IF_AT + IF_N + 3072, NB)]
    + [("va", c, False) for c in range(IF_AT + IF_N + 3072, IF_AT + IF_N + 4608, NB)]
    + [("o", c, False) for c in range(3 * D, 4 * D, NB)]
    + [("gm", c, True) for c in range(IF_AT + IF_N + 4608, IF_AT + IF_N + 4608 + D, NB)]
    + [("ga", c, True) for c in range(IF_AT + IF_N + 4608 + D, IF_AT + IF_N + 4608 + 2 * D, NB)]
)
GROUP_LIST = IN_GROUPS + [("bm", 0, True), ("bm", NB, True), ("ba", 0, True), ("ba", NB, True),
                          ("wo", 0, False), ("wo", NB, False)]
EARLY = 3
BLOCKS = [(_g, _h * KB, _h == 0, _h == 1) for _h in range(2) for _g in range(EARLY)]
for _g, (_kind, _c, _cm) in list(enumerate(GROUP_LIST))[EARLY:]:
    _halves = 1 if _kind == "ba" else 2
    for _h in range(_halves):
        BLOCKS.append((_g, _h * KB, _h == 0, _h == _halves - 1))
LAST_BLOCK = {g: b for b, (g, _, _, end) in enumerate(BLOCKS) if end}
NBLK = len(BLOCKS)
BLK_IN = 2 * len(IN_GROUPS)
AHEAD = RING - 1

CONV_AT = {3: (0, 0), 4: (0, 1), 5: (1, 0), 6: (1, 1), 7: (2, 0), 8: (3, 0), 9: (3, 1), 10: (2, 1)}
GATES_AT, CUMSUM_AT, GATE_T_AT, GATE_BACK_AT = 9, 11, 12, 13
SCORE_M_AT = [14 + 2 * h for h in range(MH)]
VALUE_M_AT = [15 + 2 * h for h in range(MH)]
M_SCALE_AT = 22
MASKS_AT = 24
SCORE_A_AT = [28, 31, 34, 37]
TURN_A_AT = [30, 33, 36, 39]
VALUE_A_AT = [31, 34, 37, 40]
M_OUT_AT = 35
M_TURN_AT = [BLK_IN - 2, BLK_IN - 1]
FFN_COL_AT, SHIFT_LOGIT_AT = (42, 43), 44
BCAST_AT = {45: 0, 46: 3}
ADA_FIRST = 8
ADA_REST = 16
ADA_PE = (0,)
ADA_DVE = (1, 4, 5, 2, 3, 6, 7)
ADA_AT = {s: ADA_FIRST + i for i, s in enumerate([12, 13, 14, 15, 17, 18, 19, 21, 22, 23, 25, 26, 27, 30, 33, 36])}

STREAM = ([("ada", a) for a in (0, 1, 4, 5)] + [("w", 0), ("w", 1), ("ada", 2), ("ada", 3), ("w", 2)]
          + [("ada", 6), ("ada", 7), ("w", 3)])
for _s in range(2, NBLK):
    if _s + AHEAD < NBLK:
        STREAM.append(("w", _s + AHEAD))
    if _s in ADA_AT:
        STREAM.append(("ada", ADA_AT[_s]))
POS = {item: n for n, item in enumerate(STREAM)}

CHUNKS = 8
PAIR_CHUNKS = (("gate", 0), ("up", 0), ("gate", 1), ("up", 1), ("down", 0), ("down", 1))
BODY = 8


def build(nc, A, out):
    with ExitStack() as ctx:
        base = (nc.sbuf_base + 63) // 64 * 64
        ctx.enter_context(nc.sbuf_tensor("arena", [P, (nc.sbuf_usable_end - base) // 4 - 32], F32))
        K = 1024

        def at(name, kib, shape, dt=F32):
            return nc.alloc_sbuf_tensor_at(name, shape, dt, offset=base + int(kib * K))

        small_at = [192 * K]

        def small(name, shape, dt=F32):
            n = 4
            for s in shape[1:]:
                n *= s
            t = nc.alloc_sbuf_tensor_at(name, shape, dt, offset=base + small_at[0])
            small_at[0] += (n + 31) // 32 * 32
            assert base + small_at[0] <= nc.sbuf_usable_end - 256, (name, small_at[0])
            return t

        def sem(name):
            return ctx.enter_context(nc.semaphore(name))

        raw = [at(f"raw{i}", 8 * i, [P, KB, NB]) for i in range(RAW)]
        hi = [at(f"hi{i}", 32 + 8 * i, [P, KB, NB], F32R) for i in range(RING)]
        lo = [at(f"lo{i}", 56 + 8 * i, [P, KB, NB], F32R) for i in range(RING)]
        u_hi = at("u_hi", 80, [P, KT, T], F32R)
        u_lo = at("u_lo", 88, [P, KT, T], F32R)
        hm_hi = at("hm_hi", 80, [P, KT, T], F32R)
        hm_lo = at("hm_lo", 88, [P, KT, T], F32R)
        qk_m = at("qk_m", 96, [P, 2 * KT, T])
        v_m = at("v_m", 112, [P, TT, D])
        sig_o = at("sig_o", 96, [P, TT, D])
        sig_gm = at("sig_gm", 104, [P, KT, T])
        sig_ga = at("sig_ga", 112, [P, KT, T])
        acc_a = at("acc_a", 120, [P, 2 * D])
        u_f32 = at("u_f32", 128, [P, KT, T])
        x_t = at("x_t", 136, [P, KT, T])
        q_a = at("q_a", 120, [P, AH, T])
        k_a = at("k_a", 132, [P, AH, T])
        v_a = at("v_a", 144, [P, TT, AH * AD])
        y_hi = at("y_hi", 120, [P, KT, T], F32R)
        y_lo = at("y_lo", 128, [P, KT, T], F32R)
        x_in = at("x_in", 156, [P, TT, D])
        prob = at("prob", 156, [P, 1152])
        ha_hi = at("ha_hi", 156, [P, AM, T], F32R)
        ha_lo = at("ha_lo", 160, [P, AM, T], F32R)
        h_m = at("h_m", 164, [P, TT, D])
        x_res = at("x_res", 164, [P, TT, D])
        mod = at("mod", 172, [P, 4, D])
        ha_f32 = at("ha_f32", 188, [P, AM, T])
        ring = [at(f"ring{i}", k, [P, KT * FF]) for i, k in enumerate((80, 140, 104, 0, 16, 32, 48, 64))]
        scratch = at("scratch", 96, [P, TT, D])
        x_hat = at("x_hat", 120, [P, TT, D])
        x_res_t = [at("x_res_t0", 160, [P, KB, T]), at("x_res_t1", 128, [P, KB, T])]
        squares = at("squares", 138, [P, NB])
        xe_t = at("xe_t", 128, [P, KT, 2 * SLOTS])
        y_e = at("y_e", 132, [P, D])
        he = at("he", 136, [P, FF])
        sg = at("sg", 138, [P, FF])
        rt = at("rt", 156, [P, 16, TT, NE])
        zeros = at("zeros", 158, [P, NB])
        onehot = at("onehot", 160, [P, TT, 2 * SLOTS])
        he_t = at("he_t", 161, [P, 2, FF // P, SLOTS])
        scat = [at("scat0", 176, [P, T + 2]), at("scat1", 188, [P, T + 2])]
        slot_off = at("slot_off", 178, [P, VISITS, NE])
        rw_scaled = at("rw_scaled", 179, [P, KT, NE])
        slot_tab = at("slot_tab", 189.5, [P, TT, VISITS * NE + 2])
        comb_tab = at("comb_tab", 190.25, [P, TT, VISITS * NE + 2])
        fin_g = at("fin_g", 172, [P, D])

        ident = small("ident", [P, P])
        ones = small("ones", [P, P])
        tri_le = small("tri_le", [P, P])
        neg_tri = small("neg_tri", [P, P])
        turned = small("turned", [P, AG, 384])
        dist = small("dist", [P, T])
        masks = small("masks", [P, AG, T])
        bias_a = small("bias_a", [P, T])
        slot_id = bias_a[:, 0:SLOTS]
        tri_lt = bias_a[:, 128:256]
        w_m = turned[:, 0, :]
        p_m = turned[:, 1, :]
        dist_i = turned[:, 2, 0:T].bitcast(I32)
        dist_m = turned[:, 0, 0:T].bitcast(I32)
        vec = small("vec", [P, 104])
        rows = turned[:, 1, 0:P]
        cs = small("cs", [P, KT])
        st = small("st", [P, 40])
        chan = small("chan", [P, 3, KT])
        w_if = small("w_if", [P, KT, IF_N])
        wif = small("wif", [P, KT, 2 * IF_N], F32R)
        gate_b = small("gate_b", [P, IF_N])
        gm = small("gm", [P, 12, TT, MH])
        neg_row = h_m[0:MH, 0, 0:T]
        run_row = small("run_row", [MH, T])
        am = small("am", [P, 8])
        rw = small("rw", [P, KT, NE])
        rb = small("rb", [P, NE])
        ffn_col = small("ffn_col", [P, 2, KT])
        logit_shift = small("logit_shift", [P, NE])
        w_pair = small("w_pair", [P, TT, 2])
        many = small("many", [P, 2])
        many_i = small("many_i", [P, 2], I32)

        ps = [ctx.enter_context(nc.psum_tensor(f"ps{i}", [P, 512], F32)) for i in range(8)]

        x_loaded, c_loaded, rows_loaded, small_loaded, bias_loaded = (sem(n) for n in (
            "x_loaded", "c_loaded", "rows_loaded", "small_loaded", "bias_loaded"))
        raw_loaded = [sem(f"raw_loaded{i}") for i in range(RAW)]
        ada_done, ada_turned = sem("ada_done"), sem("ada_turned")
        hi_ready, lo_ready, block_done = sem("hi_ready"), sem("lo_ready"), sem("block_done")
        evac_act, evac_dve = sem("evac_act"), sem("evac_dve")
        consts_ready, acc_zero = sem("consts_ready"), sem("acc_zero")
        pool_step, act_step, dve_step = sem("pool_step"), sem("act_step"), sem("dve_step")
        pe_side, act_side, dve_side = sem("pe_side"), sem("act_side"), sem("dve_side")
        qk_ready = sem("qk_ready")
        x_again, fin_loaded = sem("x_again"), sem("fin_loaded")
        ring_loaded = [sem(f"ring_loaded{i}") for i in range(CHUNKS)]
        onehot_ready, slots_turned, gathered, xe_ready, scat_ready = (sem(n) for n in (
            "onehot_ready", "slots_turned", "gathered", "xe_ready", "scat_ready"))
        gate_up_half = sem("gate_up_half")
        gate_up_done, sg_ready, he_ready, he_turned, he_t_ready, down_done, y_ready = (sem(n) for n in (
            "gate_up_done", "sg_ready", "he_ready", "he_turned", "he_t_ready", "down_done", "y_ready"))
        moe_done, out_ready, stored = (sem(n) for n in ("moe_done", "out_ready", "stored"))

        order = {"pe": [], "act": [], "dve": []}

        def plan():
            pe, act, dve = order["pe"], order["act"], order["dve"]
            pe += ["x_t", "vec_t", "mod_col0"]
            act += ["c_silu", "x_ss", "x_sqrt", "x_up", "u_hi0"]
            dve += ["x_var", "x_norm", "vec", "chan0", "u_f32_0", "u_lo0"]
            for s in range(NBLK):
                if s == 0:
                    dve += ["chan1", "u_f32_1"]
                if s == 1:
                    act += ["u_hi1", "wif_hi"]; dve += ["u_lo1", "wif_lo"]
                if s == EARLY - 1:
                    pe.append("mod_col1")
                if s in CONV_AT:
                    act.append(f"conv{s}")
                if s == GATES_AT:
                    pe.append("gates"); dve.append("gate_abs"); act += ["gate_exp", "gate_ln"]
                    dve += ["gate_1p", "lf"]
                if s == MASKS_AT:
                    dve.append("masks")
                if s == CUMSUM_AT:
                    pe.append("cumsum"); dve.append("neg_g")
                if s == GATE_T_AT:
                    pe.append("gate_t"); dve.append("run_min")
                if s == GATE_BACK_AT:
                    pe.append("gate_back"); dve.append("m_neg"); act.append("floor")
                if s in SCORE_M_AT:
                    h = SCORE_M_AT.index(s)
                    pe.append(f"m_score{h}"); dve.append(f"m_log{h}"); act.append(f"m_exp{h}"); dve.append(f"m_p{h}")
                if s in VALUE_M_AT:
                    h = VALUE_M_AT.index(s)
                    pe.append(f"m_val{h}"); act.append(f"m_num{h}")
                if s == M_SCALE_AT:
                    dve.append("m_var"); act.append("m_sqrt"); dve.append("m_scale")
                if s in TURN_A_AT:
                    h = TURN_A_AT.index(s)
                    pe.append(f"a_turn{h}"); act.append(f"a_turned{h}")
                if s in VALUE_A_AT:
                    h = VALUE_A_AT.index(s)
                    pe.append(f"a_val{h}"); act.append(f"a_out{h}")
                if s in SCORE_A_AT:
                    h = SCORE_A_AT.index(s)
                    pe.append(f"a_score{h}"); dve.append(f"a_max{h}"); act.append(f"a_exp{h}"); dve.append(f"a_prob{h}")
                if s == M_OUT_AT:
                    dve.append("h_m")
                if s in M_TURN_AT:
                    h = M_TURN_AT.index(s)
                    pe.append(f"hm_t{h}"); act.append(f"hm_hi{h}"); dve.append(f"hm_lo{h}")
                if s == M_TURN_AT[1]:
                    act.append("ha_hi"); dve.append("ha_lo")
                if s == FFN_COL_AT[1]:
                    pe.append("ffn_col"); dve.append("rw_scaled")
                if s == SHIFT_LOGIT_AT:
                    pe.append("shift_logit"); dve.append("logit_shift")
                if s in BCAST_AT:
                    i = BCAST_AT[s]
                    pe.append(f"bcast{i}"); act.append(f"mod{i}")
                if s in (LAST_BLOCK[23], LAST_BLOCK[24]):
                    j = s - LAST_BLOCK[23]
                    dve.append(f"y_f32_{j}"); act.append(f"y_hi{j}"); dve.append(f"y_lo{j}")
                if s == LAST_BLOCK[25]:
                    dve += ["x1_0", "zero"]; act.append("x1_ss0")
                if s == LAST_BLOCK[25] + 1:
                    pe.append("x1_turn0"); act.append("x1_turned0")
            pe += ["wo_t0", "x1_turn1_t0", "x1_turn1_t1", "logits", "rank_sums"]
            act += ["x1_ss1_t0", "x1_turned1_t0", "x1_ss1_t1", "x1_turned1_t1", "x1_sqrt", "scores", "x_hat"]
            dve += ["x1_1_t0", "x1_1_t1", "x1_var", "x1_rms", "logits_all", "picked", "ranks", "many",
                    "x2_t0", "x2_t1", "x2_var0", "x2_var1"]
            act += ["x2_ss0", "x2_sqrt0", "x2_ss1", "x2_sqrt1"]

        plan()
        side_sem = {"pe": pe_side, "act": act_side, "dve": dve_side}
        where = {n: (e, i + 1) for e, names in order.items() for i, n in enumerate(names)}
        made = {"pe": 0, "act": 0, "dve": 0}

        def after(eng, *events):
            for e in events:
                engine, count = where[e]
                eng.wait_ge(side_sem[engine], count)

        def event(ins, name):
            engine, count = where[name]
            made[engine] += 1
            assert made[engine] == count, (name, made[engine], count)
            ins.then_inc(side_sem[engine], 1)

        def stepper(eng, s):
            count = [0]

            def step(ins):
                count[0] += 1
                ins.then_inc(s, 1)
                eng.wait_ge(s, count[0])
            return step

        conv_order = [g for g, half in CONV_AT.values() if half == 1]

        def evac_engine(g):
            return "dve" if GROUP_LIST[g][0] in ("qk", "bm", "ba", "wo") else "act"

        def banks_of(g):
            n = g if g < EARLY else (g - EARLY) % 2
            return 2 * n, 2 * n + 1

        def evacuated(eng, g):
            e = evac_engine(g)
            groups = [x for x in range(len(GROUP_LIST)) if evac_engine(x) == e]
            if e == "dve":
                groups = conv_order + groups[len(conv_order):]
            eng.wait_ge(evac_dve if e == "dve" else evac_act, groups.index(g) + 1)

        def raw_here(eng, item):
            n = POS[item]
            eng.wait_ge(raw_loaded[n % RAW], 16 * (n // RAW + 1))
            return raw[n % RAW]

        def used_up(eng, item):
            kind, n = item
            if kind == "w":
                eng.wait_ge(lo_ready, n + 1)
            elif n in ADA_PE:
                eng.wait_ge(ada_turned, ADA_PE.index(n) + 1)
            else:
                eng.wait_ge(ada_done, ada_count(n))

        def ada_count(a):
            return ADA_DVE.index(a) + 1 if a < ADA_FIRST else a + 1 - len(ADA_PE)

        def block_source(item):
            kind, n = item
            if kind == "ada":
                c, h = n // 2, n % 2
                return A["ada_w"][0].rearrange("(p k) n -> p k n", k=KT)[:, KB * h:KB * (h + 1), c * NB:(c + 1) * NB]
            g, k0, _, _ = BLOCKS[n]
            name, c, _ = GROUP_LIST[g]
            w = {"bm": "w_branch_m", "ba": "w_branch_a", "wo": "w_out"}.get(name, "w_in")
            return A[w][0].rearrange("(k p) n -> p k n", p=P)[:, k0:k0 + KB, c:c + NB]

        def hm_bank(h, k):
            return ps[(0, 1, 4, 5)[2 * h + k // 2]][:, (k % 2) * T:(k % 2 + 1) * T]

        m_i, m_f, m_abs, m_lf, m_cum, m_ng, m_g, m_floor, m_den, m_ss, m_rec, m_tmp = range(12)
        block = ctx.enter_context(nc.Block())

        @block.sync
        def _(sp):
            sp.dma_start(cs[:], A["c"].rearrange("b (p k) -> (b p) k", k=KT)).then_inc(c_loaded, 16)
            sp.dma_start(x_in[:], A["x"][0].rearrange("(t p) n -> p t n", p=P)).then_inc(x_loaded, 16)
            for n, item in enumerate(STREAM):
                if n >= RAW:
                    used_up(sp, STREAM[n - RAW])
                sp.dma_start(raw[n % RAW][:], block_source(item)).then_inc(raw_loaded[n % RAW], 16)
                if item == ("w", EARLY + 1):
                    sp.wait_ge(acc_zero, 1)
                    sp.dma_start(mod[0:1, :, :], A["ada_b"][0:1, 2 * D:6 * D].rearrange("a (m n) -> a m n", m=4)
                                 ).then_inc(bias_loaded, 16)
                if item == ("w", BLK_IN + 4):
                    after(sp, "hm_t1")
                    sp.dma_start(x_res[:], A["x"][0].rearrange("(t p) n -> p t n", p=P)).then_inc(x_again, 16)

            matrices = {"gate": A["w_gate_e"][0], "up": A["w_up_e"][0], "down": A["w_down_e"][0]}
            per_pair = len(PAIR_CHUNKS)

            def load_half(c, h):
                matrix, m = PAIR_CHUNKS[c % per_pair]
                w = matrices[matrix][(2 * (c // per_pair) + m) % NE].rearrange("(k p) n -> p k n", p=P)
                k = w.shape[1] // 2
                dst = ring[c % CHUNKS][:].rearrange("p (k n) -> p k n", k=2 * k)
                sp.dma_start(dst[:, h * k:(h + 1) * k, :], w[:, h * k:(h + 1) * k, :]).then_inc(ring_loaded[c % CHUNKS], 16)

            def load_chunk(c):
                load_half(c, 0)
                load_half(c, 1)

            def refill(v, js):
                for j in js:
                    matrix, m = PAIR_CHUNKS[j % per_pair]
                    n = NE * v + (2 * (j // per_pair) + m + 1)
                    if matrix == "down":
                        sp.wait_ge(down_done, n)
                        load_chunk(CHUNKS + j)
                    elif matrix == "gate":
                        for h, used in enumerate((gate_up_half, gate_up_done)):
                            sp.wait_ge(used, n)
                            load_half(CHUNKS + j, h)
                            load_half(CHUNKS + j + 1, h)

            sp.wait_ge(block_done, BLK_IN + 4)
            load_chunk(0)
            load_chunk(1)
            after(sp, "y_lo1")
            load_chunk(2)
            for n in range(2):
                used_up(sp, STREAM[-1])
                load_chunk(3 + n)
            sp.wait_ge(block_done, NBLK)
            for c in range(5, CHUNKS):
                load_chunk(c)
            after(sp, "x1_1_t1")
            sp.dma_start(fin_g[:], A["final_norm_g"].rearrange("(a n) -> a n", a=1).broadcast_to([P, D])).then_inc(fin_loaded, 16)
            per_visit = 3 * NE
            refill(0, range(per_visit - CHUNKS))
            after(sp, "many")
            again = sp.value_load(many_i[0:1, 0:1], min_val=0, max_val=1)
            with sp.If(again == 1):
                refill(0, range(per_visit - CHUNKS, per_visit))
                with sp.Fori(1, VISITS - 1) as v:
                    refill(v, range(per_visit))
                refill(VISITS - 1, range(per_visit - CHUNKS))
            for t in range(TT):
                sp.wait_ge(out_ready, t + 1)
                sp.dma_start(out[0, t * P:(t + 1) * P, :], scratch[:, t, :]).then_inc(stored, 16)
            sp.wait_ge(stored, 16 * TT)

        @block.gpsimd
        def _(pool):
            step = stepper(pool, pool_step)
            step(nc.gpsimd.memset(ones[:], 1.0))
            step(nc.gpsimd.memset(neg_tri[:], 0.0))
            nc.gpsimd.affine_select(out=ident[:], in_=neg_tri[:], compare_op=ALU.not_equal, fill=1.0, base=0,
                                    pattern=[[-1, P]], channel_multiplier=1).then_inc(consts_ready, 1)
            nc.gpsimd.affine_select(out=tri_le[:], in_=ones[:], compare_op=ALU.is_ge, fill=0.0, base=0,
                                    pattern=[[1, P]], channel_multiplier=-1).then_inc(consts_ready, 1)
            pool.wait_ge(consts_ready, 2)
            nc.gpsimd.affine_select(out=neg_tri[:], in_=neg_tri[:], compare_op=ALU.is_ge, fill=NEG, base=0,
                                    pattern=[[1, P]], channel_multiplier=-1).then_inc(consts_ready, 1)
            nc.gpsimd.iota(dist_i, pattern=[[-1, T]], base=P, channel_multiplier=1).then_inc(consts_ready, 1)
            nc.gpsimd.memset(mod[:], 0.0).then_inc(acc_zero, 1)
            after(pool, "a_prob3")
            nc.gpsimd.iota(slot_id, pattern=[[1, SLOTS]], base=0, channel_multiplier=0,
                           allow_small_or_imprecise_dtypes=True).then_inc(consts_ready, 1)
            nc.gpsimd.affine_select(out=tri_lt, in_=ones[:], compare_op=ALU.is_ge, fill=0.0, base=-1,
                                    pattern=[[1, P]], channel_multiplier=-1).then_inc(consts_ready, 1)

        @block.scalar
        def _(act):
            A_ = nc.scalar.activation
            step = stepper(act, act_step)

            def split_hi(b):
                src = raw_here(act, ("w", b))
                if b >= RING:
                    act.wait_ge(block_done, b - RING + 1)
                nc.scalar.copy(hi[b % RING][:], src[:]).then_inc(hi_ready, 1)

            act.dma_start(rows[0:64, :], A["mlstm_conv"][0].rearrange("j (c p) -> (j c) p", p=P)).then_inc(rows_loaded, 16)
            act.dma_start(rows[64:72, :], A["norm_mix_g"][0].rearrange("(c p) -> c p", p=P)).then_inc(rows_loaded, 16)
            act.dma_start(rows[72:80, :], A["mlstm_norm_g"][0].rearrange("(c p) -> c p", p=P)).then_inc(rows_loaded, 16)
            act.dma_start(rows[80:96, :], A["ada_b"][0, 0:2 * D].rearrange("(c p) -> c p", p=P)).then_inc(rows_loaded, 16)
            act.dma_start(rows[96:104, :], A["norm_ffn_g"][0].rearrange("(c p) -> c p", p=P)).then_inc(rows_loaded, 16)
            act.wait_ge(c_loaded, 16)
            event(A_(cs[:], cs[:], ACT.Silu), "c_silu")
            act.wait_ge(x_loaded, 16)
            step(A_(h_m[:, 0, :], x_in[:, 0, :], ACT.Square, accum_out=st[:, 0:1]))
            event(A_(h_m[:, 0, :], x_in[:, 1, :], ACT.Square, accum_out=st[:, 1:2]), "x_ss")
            after(act, "x_var")
            event(A_(st[:, 4:6], st[:, 2:4], ACT.Sqrt), "x_sqrt")
            act.dma_start(w_if[:], A["w_in"][0].rearrange("(k p) n -> p k n", p=P)[:, :, IF_AT:IF_AT + IF_N]).then_inc(small_loaded, 16)
            act.dma_start(gate_b[:], A["mlstm_gate_b"][0:1, :].broadcast_to([P, IF_N])).then_inc(small_loaded, 16)
            act.dma_start(rw[:], A["router_w"].rearrange("(k p) n -> p k n", p=P)).then_inc(small_loaded, 16)
            act.dma_start(rb[:], A["router_b"].rearrange("(a n) -> a n", a=1).broadcast_to([P, NE])).then_inc(small_loaded, 16)
            after(act, "x_t")
            for n in range(4):
                ins = nc.scalar.copy(x_t[:, 2 * n:2 * n + 2, :], ps[4 + n][:].rearrange("p (c t) -> p c t", c=2))
            event(ins, "x_up")

            def u_split_hi(j):
                after(act, "x_up", f"chan{j}")
                for k in range(KB * j, KB * (j + 1)):
                    ins = A_(u_hi[:, k, :], x_t[:, k, :], ACT.Identity, scale=chan[:, 2, k:k + 1], bias=chan[:, 0, k:k + 1])
                event(ins, f"u_hi{j}")

            split_hi(0)
            u_split_hi(0)
            split_hi(1)

            for s in range(NBLK):
                if s + AHEAD < NBLK:
                    split_hi(s + AHEAD)
                if s == 1:
                    u_split_hi(1)
                    act.wait_ge(small_loaded, 64)
                    event(nc.scalar.copy(wif[:, :, 0:IF_N], w_if[:]), "wif_hi")
                if s in CONV_AT:
                    gq, half = CONV_AT[s]
                    act.wait_ge(block_done, LAST_BLOCK[gq] + 1)
                    for c in range(2 * half, 2 * half + 2):
                        ins = A_(qk_m[:, 4 * gq + c, :], ps[banks_of(gq)[half]][:, (c % 2) * T:(c % 2 + 1) * T], ACT.Copy,
                                 scale=vec[:, 3 * 16 + 4 * gq + c:3 * 16 + 4 * gq + c + 1])
                    event(ins, f"conv{s}")
                if s - 1 in CONV_AT and CONV_AT[s - 1][1] == 1:
                    gq = CONV_AT[s - 1][0]
                    evacuated(act, gq)
                    A_(qk_m[:, 4 * gq:4 * gq + 4, :], qk_m[:, 4 * gq:4 * gq + 4, :], ACT.Silu).then_inc(qk_ready, 1)
                g, _, _, end = BLOCKS[s]
                kind, _, _ = GROUP_LIST[g]
                if end and evac_engine(g) == "act":
                    act.wait_ge(block_done, s + 1)
                    first = min(x for x, (n, _, _) in enumerate(GROUP_LIST) if n == kind)
                    j = g - first
                    banks = banks_of(g)
                    func = ACT.Sigmoid if kind in ("o", "gm", "ga") else ACT.Copy
                    if kind == "o" and j == 0:
                        after(act, "m_val3")
                    if kind == "gm" and j == 0:
                        after(act, "m_val3")
                    if kind == "qa" and j == 0:
                        after(act, "u_lo1")
                    dst = {"vm": v_m, "va": v_a, "o": sig_o, "qa": q_a, "ka": k_a, "gm": sig_gm, "ga": sig_ga}[kind]
                    for n, bank in enumerate(banks):
                        if kind in ("vm", "va", "o"):
                            view, src = dst[:, n, j * NB:(j + 1) * NB], ps[bank][:]
                        else:
                            view = dst[:, 4 * j + 2 * n:4 * j + 2 * n + 2, :]
                            src = ps[bank][:].rearrange("p (c t) -> p c t", c=2)
                        ins = A_(view, src, func)
                    ins.then_inc(evac_act, 1)

                if s == GATES_AT:
                    after(act, "gate_abs")
                    event(A_(gm[:, m_tmp], gm[:, m_abs], ACT.Exp, scale=-1.0), "gate_exp")
                    after(act, "gate_1p")
                    event(A_(gm[:, m_abs], gm[:, m_tmp], ACT.Ln), "gate_ln")
                if s == GATE_BACK_AT:
                    after(act, "m_neg")
                    event(A_(gm[:, m_floor], gm[:, m_tmp], ACT.Exp), "floor")
                if s in SCORE_M_AT:
                    h = SCORE_M_AT.index(s)
                    after(act, f"m_log{h}")
                    event(A_(w_m, w_m, ACT.Exp), f"m_exp{h}")
                if s in VALUE_M_AT:
                    h = VALUE_M_AT.index(s)
                    after(act, f"m_val{h}")
                    for t in range(TT):
                        nc.scalar.copy(gm[:, m_den, t, h:h + 1], ps[6 + t][:, MD:MD + 1])
                        nc.scalar.copy(h_m[:, t, h * MD:(h + 1) * MD], ps[6 + t][:, 0:MD])
                        ins = A_(bias_a[:], ps[6 + t][:, 0:MD], ACT.Square, accum_out=gm[:, m_ss, t, h:h + 1])
                        if t == 0:
                            step(ins)
                    event(ins, f"m_num{h}")
                if s == M_SCALE_AT:
                    after(act, "m_var")
                    event(A_(gm[:, m_tmp], gm[:, m_abs], ACT.Sqrt), "m_sqrt")
                if s in TURN_A_AT:
                    h = TURN_A_AT.index(s)
                    after(act, f"a_turn{h}")
                    for n in range(AG):
                        ins = nc.scalar.copy(turned[:, n, :], ps[4 + n][:, 0:384])
                    event(ins, f"a_turned{h}")
                if s in VALUE_A_AT:
                    h = VALUE_A_AT.index(s)
                    after(act, f"a_val{h}")
                    event(nc.scalar.copy(ha_f32[:, h, :], ps[7][:, 0:T]), f"a_out{h}")
                if s in SCORE_A_AT:
                    h = SCORE_A_AT.index(s)
                    after(act, f"a_max{h}")
                    A_(prob[:, 0:384], prob[:, 0:384], ACT.Exp, bias=am[:, 0:1], accum_out=am[:, 2:3])
                    event(A_(prob[:, 384:1152], prob[:, 384:1152], ACT.Exp, bias=am[:, 1:2], accum_out=am[:, 3:4]),
                          f"a_exp{h}")
                if s in M_TURN_AT:
                    h = M_TURN_AT.index(s)
                    after(act, f"hm_t{h}")
                    for k in range(KB):
                        ins = A_(hm_hi[:, KB * h + k, :], hm_bank(h, k), ACT.Copy, scale=vec[:, 72 + KB * h + k:73 + KB * h + k])
                    event(ins, f"hm_hi{h}")
                if s == M_TURN_AT[1]:
                    after(act, "a_out3")
                    event(nc.scalar.copy(ha_hi[:], ha_f32[:]), "ha_hi")
                if s in BCAST_AT:
                    i = BCAST_AT[s]
                    after(act, f"bcast{i}")
                    for n in range(2):
                        ins = nc.scalar.copy(mod[:, i, n * NB:(n + 1) * NB], ps[4 + 2 * (i % 2) + n][:])
                    event(ins, f"mod{i}")
                if s in (LAST_BLOCK[23], LAST_BLOCK[24]):
                    j = s - LAST_BLOCK[23]
                    half = slice(KB * j, KB * (j + 1))
                    after(act, f"y_f32_{j}")
                    event(nc.scalar.copy(y_hi[:, half, :], sig_gm[:, half, :]), f"y_hi{j}")
                if s == LAST_BLOCK[25]:
                    after(act, "x1_0")
                    step(A_(squares[:], x_res[:, 0, 0:NB], ACT.Square, accum_out=st[:, 8:9]))
                    event(A_(squares[:], x_res[:, 1, 0:NB], ACT.Square, accum_out=st[:, 9:10]), "x1_ss0")
                    A_(st[:, 30:31], st[:, 2:3], ACT.Sqrt)
                if s == LAST_BLOCK[25] + 1:
                    after(act, "x1_turn0")
                    for t in range(TT):
                        ins = nc.scalar.copy(x_res_t[0][:, :, t * P:(t + 1) * P],
                                             ps[4 + t][:].rearrange("p (c t) -> p c t", c=KB))
                    event(ins, "x1_turned0")

            for t in range(TT):
                after(act, f"x1_1_t{t}", *(("x1_ss0",) if t == 0 else ("x1_ss1_t0",)))
                event(A_(squares[:], x_res[:, t, NB:D], ACT.Square, accum_out=st[:, 10 + t:11 + t]), f"x1_ss1_t{t}")
                after(act, f"x1_turn1_t{t}")
                event(nc.scalar.copy(x_res_t[1][:, :, t * P:(t + 1) * P], ps[6 + t][:].rearrange("p (c t) -> p c t", c=KB)),
                      f"x1_turned1_t{t}")
            after(act, "x1_var")
            event(A_(st[:, 24:26], st[:, 24:26], ACT.Sqrt), "x1_sqrt")
            after(act, "logits_all")
            event(A_(rt[:, 0], rt[:, 1], ACT.Sigmoid), "scores")
            for t in range(TT):
                ins = A_(x_hat[:, t, :], x_res[:, t, :], ACT.Copy, scale=st[:, 14 + t:15 + t])
            event(ins, "x_hat")
            after(act, "zero", "x1_turned1_t1")
            for h in range(2):
                ins = nc.scalar.copy(y_e[:, h * NB:(h + 1) * NB], zeros[:])
            ins.then_inc(y_ready, 1)

            def work_pair(i, q):
                p, n = BODY // 2 * i + q, BODY * i + 2 * q
                for j in range(2):
                    act.wait_ge(gathered, 2 * p + (j + 1))
                    for k in range(KB):
                        kk = KB * j + k
                        ins = A_(xe_t[:, kk, :], ps[5 + 2 * j][:, k * P:(k + 1) * P], ACT.Identity,
                                 scale=ffn_col[:, 1, kk:kk + 1], bias=ffn_col[:, 0, kk:kk + 1])
                    ins.then_inc(xe_ready, 1)
                for s in range(2):
                    act.wait_ge(gate_up_done, n + (s + 1))
                    rows_s, rows_g = slice(64 * s, 64 * s + 64), slice(64 * (1 - s), 64 * (1 - s) + 64)
                    A_(sg[rows_s, :], ps[4 + s][rows_g, :], ACT.Silu).then_inc(sg_ready, 1)
                for s in range(2):
                    act.wait_ge(he_turned, n + (s + 1))
                    nc.scalar.copy(he_t[:, s], ps[6 - s][:, 0:FF // P * SLOTS].rearrange("p (k s) -> p k s", k=FF // P)
                                   ).then_inc(he_t_ready, 1)

            with act.Fori(0, NE // BODY) as i:
                for q in range(BODY // 2):
                    work_pair(i, q)
            after(act, "many")
            again = act.value_load(many_i[0:1, 0:1], min_val=0, max_val=1)
            with act.If(again == 1):
                with act.Fori(NE // BODY, VISITS * NE // BODY) as i:
                    for q in range(BODY // 2):
                        work_pair(i, q)

            A_(st[:, 31:32], st[:, 2:3], ACT.Sqrt)
            for t in range(TT):
                after(act, f"x2_t{t}")
                event(A_(x_hat[:, t, :], x_res[:, t, :], ACT.Square, accum_out=st[:, 16 + t:17 + t]), f"x2_ss{t}")
                after(act, f"x2_var{t}")
                event(A_(st[:, 20 + t:21 + t], st[:, 18 + t:19 + t], ACT.Sqrt), f"x2_sqrt{t}")

        @block.vector
        def _(dve):
            V = nc.vector
            step = stepper(dve, dve_step)
            ramp = rt[:, 15, 0, :]

            def split_lo(b):
                dve.wait_ge(hi_ready, b + 1)
                src = raw[POS[("w", b)] % RAW]
                V.tensor_tensor(lo[b % RING][:], src[:], hi[b % RING][:].bitcast(F32), ALU.subtract
                                ).then_inc(lo_ready, 1)

            def ada(a):
                src = raw_here(dve, ("ada", a))
                fresh = a < ADA_FIRST and (a % 2 == 0 or a - 1 in ADA_PE)
                if a % 2 and not fresh:
                    dve.wait_ge(ada_done, ada_count(a - 1))
                if a == ADA_FIRST:
                    dve.wait_ge(bias_loaded, 16)
                col = (a // 2) * NB
                dst = acc_a[:, col:col + NB] if a < ADA_FIRST else (
                    mod[:, (col - 2 * D) // D, (col % D):(col % D) + NB])
                for k in range(KB):
                    kk = KB * (a % 2) + k
                    if fresh and k == 0:
                        ins = V.tensor_scalar(dst, src[:, k, :], cs[:, kk:kk + 1], None, ALU.mult)
                    else:
                        ins = V.scalar_tensor_tensor(out=dst, in0=src[:, k, :], scalar=cs[:, kk:kk + 1], in1=dst,
                                                     op0=ALU.mult, op1=ALU.add)
                    if k < KB - 1:
                        step(ins)
                    else:
                        ins.then_inc(ada_done, 1)

            def inv_rms(ss, var, name):
                event(V.tensor_scalar(var, ss, 1.0 / D, EPS, ALU.mult, ALU.add), name)

            after(dve, "x_ss")
            inv_rms(st[:, 0:2], st[:, 2:4], "x_var")
            after(dve, "x_sqrt")
            step(V.reciprocal(st[:, 6:8], st[:, 4:6]))
            for t in range(TT):
                ins = V.tensor_scalar(x_in[:, t, :], x_in[:, t, :], st[:, 6 + t:7 + t], None, ALU.mult)
            event(ins, "x_norm")
            after(dve, "c_silu")

            def modulate(j, bank):
                if j == 0:
                    after(dve, "vec_t")
                    event(V.tensor_copy(vec[:], ps[0][:, 0:104]), "vec")
                    after(dve, "vec")
                after(dve, f"mod_col{j}")
                half = slice(KB * j, KB * (j + 1))
                step(V.tensor_tensor(chan[:, 0:2, half], ps[bank][:, 0:2 * KT].rearrange("p (a k) -> p a k", a=2)[:, :, half],
                                     vec[:, 80:96].rearrange("p (a k) -> p a k", a=2)[:, :, half], ALU.add))
                event(V.scalar_tensor_tensor(out=chan[:, 2, half], in0=chan[:, 1, half], scalar=1.0,
                                             in1=vec[:, 64 + KB * j:68 + KB * j], op0=ALU.add, op1=ALU.mult), f"chan{j}")
                after(dve, "x_up", f"chan{j}")
                for k in range(KB * j, KB * (j + 1)):
                    ins = V.tensor_scalar(u_f32[:, k, :], x_t[:, k, :], chan[:, 2, k:k + 1], chan[:, 0, k:k + 1],
                                          ALU.mult, ALU.add)
                event(ins, f"u_f32_{j}")

            def u_split_lo(j):
                after(dve, f"u_f32_{j}", f"u_hi{j}")
                half = slice(KB * j, KB * (j + 1))
                event(V.tensor_tensor(u_lo[:, half, :], u_f32[:, half, :], u_hi[:, half, :].bitcast(F32), ALU.subtract),
                      f"u_lo{j}")

            ada(1)
            ada(4)
            ada(5)
            modulate(0, 1)
            split_lo(0)
            u_split_lo(0)
            split_lo(1)
            ada(2)
            ada(3)

            for s in range(NBLK):
                if s + AHEAD < NBLK and s != 1:
                    split_lo(s + AHEAD)
                if s == 0:
                    ada(6)
                    ada(7)
                    split_lo(EARLY)
                    modulate(1, 7)
                if s == 1:
                    u_split_lo(1)
                    after(dve, "wif_hi")
                    event(V.tensor_tensor(wif[:, :, IF_N:2 * IF_N], w_if[:], wif[:, :, 0:IF_N].bitcast(F32), ALU.subtract),
                          "wif_lo")
                if s in CONV_AT:
                    gq, half = CONV_AT[s]
                    after(dve, f"conv{s}")
                    for back in (1, 2, 3):
                        for c in range(2 * half, 2 * half + 2):
                            tap = (3 - back) * 16 + 4 * gq + c
                            src = ps[banks_of(gq)[half]][:, (c % 2) * T:(c % 2 + 1) * T]
                            dst = qk_m[:, 4 * gq + c, back:T]
                            ins = V.scalar_tensor_tensor(out=dst, in0=src[:, 0:T - back], scalar=vec[:, tap:tap + 1],
                                                         in1=dst, op0=ALU.mult, op1=ALU.add)
                        if back < 3 or half == 0:
                            step(ins)
                    if half == 1:
                        ins.then_inc(evac_dve, 1)
                g, _, _, end = BLOCKS[s]
                kind, col, _ = GROUP_LIST[g]
                banks = banks_of(g)
                if end and kind in ("bm", "ba", "wo") and s < NBLK - 1:
                    dve.wait_ge(block_done, s + 1)
                if end and kind == "bm":
                    j = col // NB
                    for n, bank in enumerate(banks):
                        view = sig_gm[:, 4 * j + 2 * n:4 * j + 2 * n + 2, :]
                        ins = V.tensor_tensor(view, ps[bank][:].rearrange("p (c t) -> p c t", c=2), view, ALU.mult)
                    ins.then_inc(evac_dve, 1)
                if end and kind == "ba":
                    j = col // NB
                    for n, bank in enumerate(banks):
                        view = sig_ga[:, 4 * j + 2 * n:4 * j + 2 * n + 2, :]
                        ins = V.tensor_tensor(view, ps[bank][:].rearrange("p (c t) -> p c t", c=2), view, ALU.mult)
                    ins.then_inc(evac_dve, 1)
                    evacuated(dve, g)
                    half = slice(KB * j, KB * (j + 1))
                    event(V.tensor_tensor(sig_gm[:, half, :], sig_gm[:, half, :], sig_ga[:, half, :], ALU.add), f"y_f32_{j}")
                    after(dve, f"y_hi{j}")
                    event(V.tensor_tensor(y_lo[:, half, :], sig_gm[:, half, :], y_hi[:, half, :].bitcast(F32), ALU.subtract),
                          f"y_lo{j}")
                if end and kind == "wo":
                    j = col // NB
                    if j == 0:
                        dve.wait_ge(x_again, 16)
                        for t in range(TT):
                            ins = V.tensor_tensor(scratch[:, t, col:col + NB], ps[banks[t]][:], mod[:, 0, col:col + NB], ALU.mult)
                        ins.then_inc(evac_dve, 1)
                        evacuated(dve, g)
                        for t in range(TT):
                            view = x_res[:, t, col:col + NB]
                            ins = V.tensor_tensor(view, view, scratch[:, t, col:col + NB], ALU.add)
                        event(ins, "x1_0")
                        V.memset(slot_tab[:, :, VISITS * NE:VISITS * NE + 2], -1.0)
                        V.memset(comb_tab[:, :, VISITS * NE:VISITS * NE + 2], 0.0)
                        for j in range(NE):
                            V.memset(ramp[:, j:j + 1], float(NE - j))
                        for v in range(VISITS):
                            V.memset(slot_off[:, v, :], -1.0 - v * SLOTS)
                        V.memset(scat[1][:], 0.0).then_inc(scat_ready, 1)
                        event(V.memset(zeros[:], 0.0), "zero")
                    else:
                        for t in range(TT):
                            if t == 0:
                                after(dve, "wo_t0")
                            else:
                                dve.wait_ge(block_done, s + 1)
                            ins = V.tensor_tensor(scratch[:, t, col:col + NB], ps[banks[t]][:], mod[:, 0, col:col + NB], ALU.mult)
                            if t == 0:
                                step(ins)
                            else:
                                ins.then_inc(evac_dve, 1)
                                evacuated(dve, g)
                            view = x_res[:, t, col:col + NB]
                            event(V.tensor_tensor(view, view, scratch[:, t, col:col + NB], ALU.add), f"x1_1_t{t}")
                if s in ADA_AT:
                    ada(ADA_AT[s])

                if s == MASKS_AT:
                    dve.wait_ge(consts_ready, 4)
                    step(V.tensor_copy(dist[:], dist_i))
                    step(V.tensor_scalar(masks[:, 0, :], dist[:], float(PATTERNS[0][0] // PATTERNS[0][1]), NEG,
                                         ALU.is_gt, ALU.mult))
                    for n in (1, 2):
                        step(V.tensor_scalar(dist_m, dist_i, PATTERNS[n][1] - 1, None, ALU.bitwise_and))
                        step(V.tensor_scalar(masks[:, n, :], dist_m, 0.0, NEG, ALU.not_equal, ALU.mult))
                    step(V.tensor_scalar(bias_a[:], dist[:], 0.0, NEG, ALU.is_lt, ALU.mult))
                    for n in range(AG):
                        ins = V.tensor_tensor(masks[:, n, :], masks[:, n, :], bias_a[:], ALU.add)
                    event(ins, "masks")
                if s == GATES_AT:
                    after(dve, "gates")
                    pre = ps[6][:, 0:TT * 2 * IF_N].rearrange("p (t w a h) -> p t w a h", t=TT, w=2, a=2)
                    for n, row in enumerate((m_i, m_f)):
                        for t in range(TT):
                            ins = V.tensor_tensor(gm[:, row, t, :], pre[:, t, 1, n, :], gate_b[:, n * MH:(n + 1) * MH], ALU.add)
                    step(ins)
                    for n, row in enumerate((m_i, m_f)):
                        ins = V.tensor_tensor(gm[:, row], gm[:, row], pre[:, :, 0, n, :], ALU.add)
                    step(ins)
                    event(V.scalar_tensor_tensor(out=gm[:, m_abs], in0=gm[:, m_f], scalar=-1.0, in1=gm[:, m_f],
                                                 op0=ALU.mult, op1=ALU.max), "gate_abs")
                    after(dve, "gate_exp")
                    event(V.tensor_scalar(gm[:, m_tmp], gm[:, m_tmp], 1.0, None, ALU.add), "gate_1p")
                    after(dve, "gate_ln")
                    event(V.scalar_tensor_tensor(out=gm[:, m_lf], in0=gm[:, m_f], scalar=0.0, in1=gm[:, m_abs],
                                                 op0=ALU.min, op1=ALU.subtract), "lf")
                if s == CUMSUM_AT:
                    after(dve, "cumsum")
                    step(V.tensor_copy(gm[:, m_cum], ps[6][:, 0:TT * MH].rearrange("p (t h) -> p t h", t=TT)))
                    step(V.tensor_tensor(gm[:, m_g], gm[:, m_i], gm[:, m_cum], ALU.subtract))
                    event(V.tensor_scalar(gm[:, m_ng], gm[:, m_g], -1.0, None, ALU.mult), "neg_g")
                if s == GATE_T_AT:
                    after(dve, "gate_t")
                    step(V.tensor_copy(neg_row, ps[7][0:MH, 0:T]))
                    event(V.tensor_tensor_scan(run_row[:], neg_row, neg_row, 0.0, ALU.min, ALU.min), "run_min")
                if s == GATE_BACK_AT:
                    after(dve, "gate_back")
                    event(V.tensor_tensor(gm[:, m_tmp], ps[6][:, 0:TT * MH].rearrange("p (t h) -> p t h", t=TT),
                                          gm[:, m_cum], ALU.subtract), "m_neg")
                if s in SCORE_M_AT:
                    h = SCORE_M_AT.index(s)
                    after(dve, f"m_score{h}")
                    V.scalar_tensor_tensor(out=w_m[:, 0:P], in0=ps[4][:, 0:P], scalar=gm[:, m_g, 0, h:h + 1],
                                           in1=neg_tri[:], op0=ALU.add, op1=ALU.add)
                    V.tensor_scalar(w_m[:, P:2 * P], ps[4][:, P:2 * P], gm[:, m_g, 0, h:h + 1], None, ALU.add)
                    event(V.scalar_tensor_tensor(out=w_m[:, 2 * P:3 * P], in0=ps[4][:, P:2 * P], scalar=gm[:, m_g, 1, h:h + 1],
                                                 in1=neg_tri[:], op0=ALU.add, op1=ALU.add), f"m_log{h}")
                    after(dve, f"m_exp{h}")
                    event(V.scalar_tensor_tensor(out=p_m, in0=ps[5][:, 0:384], scalar=MD ** -0.5, in1=w_m,
                                                 op0=ALU.mult, op1=ALU.mult), f"m_p{h}")
                if s == M_SCALE_AT:
                    after(dve, "m_num3", "floor")
                    step(V.scalar_tensor_tensor(out=gm[:, m_den], in0=gm[:, m_den], scalar=-1.0, in1=gm[:, m_den],
                                                op0=ALU.mult, op1=ALU.max))
                    step(V.tensor_tensor(gm[:, m_den], gm[:, m_den], gm[:, m_floor], ALU.max))
                    step(V.reciprocal(gm[:, m_rec], gm[:, m_den]))
                    step(V.tensor_tensor(gm[:, m_abs], gm[:, m_ss], gm[:, m_rec], ALU.mult))
                    step(V.tensor_tensor(gm[:, m_abs], gm[:, m_abs], gm[:, m_rec], ALU.mult))
                    event(V.tensor_scalar(gm[:, m_abs], gm[:, m_abs], 1.0 / MD, EPS, ALU.mult, ALU.add), "m_var")
                    after(dve, "m_sqrt")
                    step(V.reciprocal(gm[:, m_tmp], gm[:, m_tmp]))
                    event(V.tensor_tensor(gm[:, m_rec], gm[:, m_rec], gm[:, m_tmp], ALU.mult), "m_scale")
                if s in SCORE_A_AT:
                    h = SCORE_A_AT.index(s)
                    after(dve, f"a_score{h}")
                    if h:
                        after(dve, f"a_turn{h - 1}")
                    for n in range(AG):
                        head = n * AM + h
                        slope = 2.0 ** (-8.0 * (head + 1) / AH)
                        step(V.scalar_tensor_tensor(out=bias_a[:], in0=dist[:], scalar=-slope, in1=masks[:, n, :],
                                                    op0=ALU.mult, op1=ALU.add))
                        V.scalar_tensor_tensor(out=prob[:, n * P:(n + 1) * P], in0=ps[4][:, n * P:(n + 1) * P],
                                               scalar=AD ** -0.5, in1=bias_a[:, P:T], op0=ALU.mult, op1=ALU.add)
                        src = ps[5][:, n * T:(n + 1) * T] if n < 2 else ps[6][:, 0:T]
                        step(V.scalar_tensor_tensor(out=prob[:, 384 + n * T:384 + (n + 1) * T], in0=src,
                                                    scalar=AD ** -0.5, in1=bias_a[:], op0=ALU.mult, op1=ALU.add))
                    V.tensor_reduce(am[:, 0:1], prob[:, 0:384], AX_X, ALU.max, negate=True)
                    event(V.tensor_reduce(am[:, 1:2], prob[:, 384:1152], AX_X, ALU.max, negate=True), f"a_max{h}")
                    after(dve, f"a_exp{h}")
                    step(V.reciprocal(am[:, 4:6], am[:, 2:4]))
                    V.tensor_scalar(prob[:, 0:384], prob[:, 0:384], am[:, 4:5], None, ALU.mult)
                    event(V.tensor_scalar(prob[:, 384:1152], prob[:, 384:1152], am[:, 5:6], None, ALU.mult), f"a_prob{h}")
                if s == M_OUT_AT:
                    evacuated(dve, 16)
                    for t in range(TT):
                        for h in range(MH):
                            view = h_m[:, t, h * MD:(h + 1) * MD]
                            ins = V.scalar_tensor_tensor(out=view, in0=view, scalar=gm[:, m_rec, t, h:h + 1],
                                                         in1=sig_o[:, t, h * MD:(h + 1) * MD], op0=ALU.mult, op1=ALU.mult)
                    event(ins, "h_m")
                if s in M_TURN_AT:
                    h = M_TURN_AT.index(s)
                    after(dve, f"hm_hi{h}")
                    for k in range(KB):
                        kk = KB * h + k
                        ins = V.scalar_tensor_tensor(out=hm_lo[:, kk, :], in0=hm_bank(h, k), scalar=vec[:, 72 + kk:73 + kk],
                                                     in1=hm_hi[:, kk, :].bitcast(F32), op0=ALU.mult, op1=ALU.subtract)
                    event(ins, f"hm_lo{h}")
                if s == M_TURN_AT[1]:
                    after(dve, "ha_hi")
                    event(V.tensor_tensor(ha_lo[:], ha_f32[:], ha_hi[:].bitcast(F32), ALU.subtract), "ha_lo")
                if s == FFN_COL_AT[1]:
                    after(dve, "ffn_col")
                    V.tensor_copy(ffn_col[:, 0, :], ps[6][:, 0:KT])
                    step(V.scalar_tensor_tensor(out=ffn_col[:, 1, :], in0=ps[6][:, KT:2 * KT], scalar=1.0, in1=vec[:, 96:104],
                                                op0=ALU.add, op1=ALU.mult))
                    for k in range(KT):
                        ins = V.tensor_scalar(rw_scaled[:, k, :], rw[:, k, :], ffn_col[:, 1, k:k + 1], None, ALU.mult)
                    event(ins, "rw_scaled")
                if s == SHIFT_LOGIT_AT:
                    after(dve, "shift_logit")
                    event(V.tensor_copy(logit_shift[:], ps[7][:, 0:NE]), "logit_shift")

            after(dve, "x1_ss0", "x1_ss1_t0", "x1_ss1_t1")
            step(V.tensor_tensor(st[:, 24:26], st[:, 8:10], st[:, 10:12], ALU.add))
            inv_rms(st[:, 24:26], st[:, 24:26], "x1_var")
            after(dve, "x1_sqrt")
            event(V.reciprocal(st[:, 14:16], st[:, 24:26]), "x1_rms")

            SC, SEL, IN, T1, T2, OH1, OH2, KEY, W, PICK, R = range(11)

            after(dve, "logits", "x1_rms", "logit_shift")
            for t in range(TT):
                ins = V.scalar_tensor_tensor(out=rt[:, SEL, t, :], in0=ps[0][:, t * NE:(t + 1) * NE], scalar=st[:, 14 + t:15 + t],
                                             in1=logit_shift[:], op0=ALU.mult, op1=ALU.add)
            event(ins, "logits_all")
            after(dve, "scores")
            for t in range(TT):
                ins = V.tensor_tensor(rt[:, SEL, t, :], rt[:, SC, t, :], rb[:], ALU.add)
            step(ins)
            sel4 = rt[:, SEL].rearrange("p t (g j) -> p (t g) j", j=PER)
            pairs = rt[:, 12:15].rearrange("p a t e -> p (a t e)")[:, 0:TT * GROUPS * 6].rearrange("p (g j) -> p g j", j=6)
            n = 0
            for apart in range(1, PER):
                width = PER - apart
                ins = V.tensor_tensor(pairs[:, :, n:n + width], sel4[:, :, 0:width], sel4[:, :, apart:PER], ALU.add)
                n += width
            step(ins)
            gscore = rt[:, T1].rearrange("p t e -> p (t e)")[:, 0:TT * GROUPS]
            step(V.tensor_reduce(gscore, pairs, AX_X, ALU.max))

            def one_hot_first(src3, best, key, dst3, width):
                step(V.tensor_reduce(best, src3, AX_X, ALU.max))
                for t in range(TT):
                    ins = V.scalar_tensor_tensor(out=key[:, t, :], in0=src3[:, t, :], scalar=best[:, t:t + 1],
                                                 in1=ramp[:, 0:width], op0=ALU.is_equal, op1=ALU.mult)
                step(ins)
                step(V.tensor_reduce(best, key, AX_X, ALU.max))
                for t in range(TT):
                    ins = V.tensor_scalar(dst3[:, t, :], key[:, t, :], best[:, t:t + 1], None, ALU.is_equal)
                step(ins)

            best = st[:, 24:26]
            gs3 = gscore.rearrange("p (t g) -> p t g", t=TT)
            key4 = rt[:, KEY, :, 0:GROUPS]
            ing = rt[:, T2, :, 0:GROUPS]
            one_hot_first(gs3, best, key4, ing, GROUPS)
            step(V.tensor_scalar(ing, ing, 1.0, -NEG, ALU.subtract, ALU.mult))
            for t in range(TT):
                ins = V.tensor_tensor(rt[:, IN, t, :].rearrange("p (g j) -> p g j", g=GROUPS),
                                      rt[:, SEL, t, :].rearrange("p (g j) -> p g j", g=GROUPS),
                                      ing[:, t, :].unsqueeze(2).broadcast_to([P, GROUPS, PER]), ALU.add)
            step(ins)
            one_hot_first(rt[:, IN], best, rt[:, KEY], rt[:, OH1], NE)
            step(V.scalar_tensor_tensor(out=rt[:, IN], in0=rt[:, OH1], scalar=2 * NEG, in1=rt[:, IN],
                                        op0=ALU.mult, op1=ALU.add))
            one_hot_first(rt[:, IN], best, rt[:, KEY], rt[:, OH2], NE)
            event(V.tensor_tensor(rt[:, PICK], rt[:, OH1], rt[:, OH2], ALU.add), "picked")
            after(dve, "picked")
            step(V.tensor_tensor(rt[:, W], rt[:, PICK], rt[:, SC], ALU.mult))
            step(V.tensor_reduce(st[:, 26:28], rt[:, W], AX_X, ALU.add))
            step(V.reciprocal(st[:, 28:30], st[:, 26:28]))
            for t in range(TT):
                ins = V.tensor_scalar(comb_tab[:, t, 0:VISITS * NE].rearrange("p (v e) -> p v e", e=NE),
                                      rt[:, W, t, :].unsqueeze(1).broadcast_to([P, VISITS, NE]),
                                      st[:, 28 + t:29 + t], None, ALU.mult)
            step(ins)
            after(dve, "rank_sums")
            step(V.scalar_tensor_tensor(out=rt[:, R], in0=ps[4][:, 0:TT * NE].rearrange("p (t e) -> p t e", t=TT), scalar=1.0,
                                        in1=rt[:, PICK], op0=ALU.add, op1=ALU.mult))
            V.tensor_reduce(many[:, 0:1], ps[4][:, TT * NE:(TT + 1) * NE], AX_X, ALU.max)
            for t in range(TT):
                ins = V.tensor_tensor(slot_tab[:, t, 0:VISITS * NE].rearrange("p (v e) -> p v e", e=NE),
                                      rt[:, R, t, :].unsqueeze(1).broadcast_to([P, VISITS, NE]), slot_off[:], ALU.add)
            event(ins, "ranks")
            after(dve, "ranks")

            def build_onehot(p):
                V.tensor_copy(w_pair[:], comb_tab[:, :, bass.ds(2 * p, 2)])
                for t in range(TT):
                    for s in range(2):
                        ins = V.tensor_scalar(onehot[:, t, s * SLOTS:(s + 1) * SLOTS], slot_id,
                                              slot_tab[:, t, bass.ds(2 * p + s, 1)], None, ALU.is_equal)
                ins.then_inc(onehot_ready, 1)

            def evacuate_slots(p, side):
                dve.wait_ge(slots_turned, p + 1)
                V.tensor_copy(scat[side][:], ps[6][:, 0:T + 2]).then_inc(scat_ready, 1)

            def weigh(n, s, side):
                dve.wait_ge(sg_ready, n + (s + 1))
                rows_s = slice(64 * s, 64 * s + 64)
                V.scalar_tensor_tensor(out=he[rows_s, :], in0=ps[4 + s][rows_s, :], scalar=scat[side][rows_s, T + s:T + s + 1],
                                       in1=sg[rows_s, :], op0=ALU.mult, op1=ALU.mult).then_inc(he_ready, 1)

            def work_pair(i, q):
                p, n = BODY // 2 * i + q, BODY * i + 2 * q
                evacuate_slots(p, q % 2)
                dve.wait_ge(scat_ready, p + 2)
                weigh(n, 0, q % 2)
                build_onehot(p + 1)
                weigh(n, 1, q % 2)
                for s in range(2):
                    dve.wait_ge(down_done, n + (s + 1))
                    for h in range(2):
                        ins = V.tensor_copy(y_e[64 * s:64 * s + 64, h * NB:(h + 1) * NB],
                                            ps[7 if s == 0 else 4][64 * h:64 * h + 64, :])
                    ins.then_inc(y_ready, 1)

            dve.wait_ge(consts_ready, 6)
            build_onehot(0)
            event(V.tensor_scalar(many_i[:, 0:1], many[:, 0:1], float(SLOTS), None, ALU.is_gt), "many")
            with dve.Fori(0, NE // BODY) as i:
                for q in range(BODY // 2):
                    work_pair(i, q)
            after(dve, "many")
            again = dve.value_load(many_i[0:1, 0:1], min_val=0, max_val=1)
            with dve.If(again == 1):
                with dve.Fori(NE // BODY, VISITS * NE // BODY) as i:
                    for q in range(BODY // 2):
                        work_pair(i, q)

            for t in range(TT):
                dve.wait_ge(moe_done, t + 1)
                for h in range(2):
                    ins = V.tensor_tensor(scratch[:, t, h * NB:(h + 1) * NB], ps[2 * t + h][:],
                                          mod[:, 3, h * NB:(h + 1) * NB], ALU.mult)
                step(ins)
                event(V.tensor_tensor(x_res[:, t, :], x_res[:, t, :], scratch[:, t, :], ALU.add), f"x2_t{t}")
            dve.wait_ge(fin_loaded, 16)
            for t in range(TT):
                after(dve, f"x2_ss{t}")
                inv_rms(st[:, 16 + t:17 + t], st[:, 18 + t:19 + t], f"x2_var{t}")
                after(dve, f"x2_sqrt{t}")
                step(V.reciprocal(st[:, 22 + t:23 + t], st[:, 20 + t:21 + t]))
                V.scalar_tensor_tensor(out=scratch[:, t, :], in0=x_res[:, t, :], scalar=st[:, 22 + t:23 + t],
                                       in1=fin_g[:], op0=ALU.mult, op1=ALU.mult).then_inc(out_ready, 1)

        @block.tensor
        def _(pe):
            mm, tr = nc.tensor.matmul, nc.tensor.transpose

            pe.wait_ge(consts_ready, 2)
            def ada_pe(a):
                src = raw_here(pe, ("ada", a))
                for c in range(KB):
                    n = (a // 2) * KB + c
                    for k in range(KB):
                        kk = KB * (a % 2) + k
                        ins = mm(ps[1][:, n:n + 1], src[:, k, c * P:(c + 1) * P], cs[:, kk:kk + 1],
                                 start=(a == 0 and c == 0 and k == 0), stop=False, skip_group_check=True)
                ins.then_inc(ada_turned, 1)

            def mod_columns(j, m, bank):
                pe.wait_ge(ada_done, ada_count((1, 5, 3, 7)[2 * j + m]))
                for c in range(KB):
                    n = KT * m + KB * j + c
                    ins = mm(ps[bank][:, n:n + 1], acc_a[:, n * P:(n + 1) * P], ones[:, 0:1],
                             start=(j == 1 and m == 0 and c == 0), stop=True, skip_group_check=True)
                if m == 1:
                    event(ins, f"mod_col{j}")

            after(pe, "c_silu")
            ada_pe(0)
            after(pe, "x_norm")
            for k in range(KT):
                for t in range(TT):
                    ins = tr(ps[4 + k // 2][:, (k % 2) * T + t * P:(k % 2) * T + (t + 1) * P],
                             x_in[:, t, k * P:(k + 1) * P], ident[:])
            event(ins, "x_t")
            pe.wait_ge(rows_loaded, 80)
            event(tr(ps[0][:, 0:104], rows[0:104, :], ident[0:104, 0:104]), "vec_t")
            mod_columns(0, 0, 1)
            mod_columns(0, 1, 1)

            for s, (g, k0, first, end) in enumerate(BLOCKS):
                kind, _, channel_major = GROUP_LIST[g]
                if s == 0:
                    after(pe, "u_lo0", "x_up")
                if s == EARLY:
                    after(pe, "u_lo1")
                if first and g >= EARLY:
                    evacuated(pe, g - EARLY if g < EARLY + 2 else g - 2)
                if g == 21:
                    after(pe, f"hm_lo{k0 // KB}")
                if g == 23:
                    after(pe, "ha_lo")
                if g == 25:
                    after(pe, f"y_lo{k0 // KB}")
                x_hi, x_lo = {"bm": (hm_hi, hm_lo), "ba": (ha_hi, ha_lo), "wo": (y_hi, y_lo)}.get(kind, (u_hi, u_lo))
                pe.wait_ge(lo_ready, s + 1)
                w_hi, w_lo = hi[s % RING], lo[s % RING]
                banks = banks_of(g)
                if channel_major:
                    for c in range(4):
                        dst = ps[banks[c // 2]][:, (c % 2) * T:(c % 2 + 1) * T]
                        cols = slice(c * P, (c + 1) * P)
                        for k in range(KB):
                            for n, (w, x) in enumerate(((w_hi, x_hi), (w_hi, x_lo), (w_lo, x_hi))):
                                ins = mm(dst, w[:, k, cols], x[:, k0 + k, :],
                                         start=(first and c % 2 == 0 and k == 0 and n == 0),
                                         stop=(end and k == KB - 1 and n == 2), skip_group_check=True)
                else:
                    for t in range(TT):
                        rows_t = slice(t * P, (t + 1) * P)
                        for k in range(KB):
                            for n, (w, x) in enumerate(((w_hi, x_hi), (w_hi, x_lo), (w_lo, x_hi))):
                                ins = mm(ps[banks[t]][:], x[:, k0 + k, rows_t], w[:, k, :],
                                         start=(first and k == 0 and n == 0), stop=(end and k == KB - 1 and n == 2))
                        if s == NBLK - 1 and t == 0:
                            event(ins, "wo_t0")
                ins.then_inc(block_done, 1)

                if s == EARLY - 2:
                    mod_columns(1, 0, 7)
                if s == EARLY - 1:
                    mod_columns(1, 1, 7)
                if s in (GATES_AT - 1, GATES_AT):
                    after(pe, "wif_lo")
                    t = s - (GATES_AT - 1)
                    at_t = t * 2 * IF_N
                    for k in range(KT):
                        mm(ps[6][:, at_t:at_t + 2 * IF_N], u_hi[:, k, t * P:(t + 1) * P], wif[:, k, :],
                           start=(k == 0), stop=(k == KT - 1), skip_group_check=True)
                        ins = mm(ps[6][:, at_t:at_t + IF_N], u_lo[:, k, t * P:(t + 1) * P], wif[:, k, 0:IF_N],
                                 start=False, stop=(k == KT - 1), skip_group_check=True)
                    if t == TT - 1:
                        event(ins, "gates")
                if s == CUMSUM_AT:
                    after(pe, "lf")
                    mm(ps[6][:, 0:MH], tri_le[:], gm[:, m_lf, 0, :], start=True, stop=True)
                    mm(ps[6][:, MH:2 * MH], ones[:], gm[:, m_lf, 0, :], start=True, stop=False)
                    event(mm(ps[6][:, MH:2 * MH], tri_le[:], gm[:, m_lf, 1, :], start=False, stop=True), "cumsum")
                if s == GATE_T_AT:
                    after(pe, "neg_g")
                    for t in range(TT):
                        ins = tr(ps[7][0:MH, t * P:(t + 1) * P], gm[:, m_ng, t, :], ident[:])
                    event(ins, "gate_t")
                if s == GATE_BACK_AT:
                    after(pe, "run_min")
                    for t in range(TT):
                        ins = tr(ps[6][:, t * MH:(t + 1) * MH], run_row[:, t * P:(t + 1) * P], ident[0:MH, 0:MH])
                    event(ins, "gate_back")
                if s in SCORE_M_AT:
                    h = SCORE_M_AT.index(s)
                    if h == 0:
                        pe.wait_ge(qk_ready, 4)
                        after(pe, "m_neg")
                        evacuated(pe, 2)
                    else:
                        after(pe, f"m_p{h - 1}")
                    mm(ps[4][:, 0:T], ident[0:MH, h:h + 1].broadcast_to([MH, P]), run_row[:], start=True, stop=True)
                    for k in range(2):
                        mm(ps[5][:, 0:T], qk_m[:, KT + 2 * h + k, 0:P], qk_m[:, 2 * h + k, :], start=(k == 0), stop=(k == 1))
                    for k in range(2):
                        ins = mm(ps[5][:, T:T + P], qk_m[:, KT + 2 * h + k, P:T], qk_m[:, 2 * h + k, P:T],
                                 start=(k == 0), stop=(k == 1))
                    event(ins, f"m_score{h}")
                if s in VALUE_M_AT:
                    h = VALUE_M_AT.index(s)
                    after(pe, f"m_p{h}")
                    if h == 0:
                        evacuated(pe, 5)
                    else:
                        after(pe, f"m_num{h - 1}")
                    for t, parts in ((0, ((0, 0),)), (1, ((P, 0), (2 * P, 1)))):
                        for n, (at_p, sk) in enumerate(parts):
                            mm(ps[6 + t][:, 0:MD], p_m[:, at_p:at_p + P], v_m[:, sk, h * MD:(h + 1) * MD],
                               start=(n == 0), stop=(n == len(parts) - 1))
                        for n, (at_p, sk) in enumerate(parts):
                            ins = mm(ps[6 + t][:, MD:MD + 1], p_m[:, at_p:at_p + P], ones[:, 0:1],
                                     start=(n == 0), stop=(n == len(parts) - 1))
                    event(ins, f"m_val{h}")
                if s in TURN_A_AT:
                    h = TURN_A_AT.index(s)
                    after(pe, f"a_prob{h}")
                    for n in range(AG):
                        for m, src in enumerate((prob[:, n * P:(n + 1) * P], prob[:, 384 + n * T:384 + n * T + P],
                                                 prob[:, 384 + n * T + P:384 + (n + 1) * T])):
                            ins = tr(ps[4 + n][:, m * P:(m + 1) * P], src, ident[:])
                    event(ins, f"a_turn{h}")
                if s in VALUE_A_AT:
                    h = VALUE_A_AT.index(s)
                    after(pe, f"a_turned{h}")
                    if h:
                        after(pe, f"a_out{h - 1}")
                    else:
                        evacuated(pe, 14)
                        after(pe, "m_num3")
                    for n in range(AG):
                        cols = slice((n * AM + h) * AD, (n * AM + h + 1) * AD)
                        mm(ps[7][:, 0:T], v_a[:, 0, cols], turned[:, n, 0:T], start=(n == 0), stop=False, skip_group_check=True)
                        ins = mm(ps[7][:, P:T], v_a[:, 1, cols], turned[:, n, T:384], start=False, stop=(n == AG - 1),
                                 skip_group_check=True)
                    event(ins, f"a_val{h}")
                if s in SCORE_A_AT:
                    h = SCORE_A_AT.index(s)
                    if h == 0:
                        evacuated(pe, 11)
                        after(pe, "m_p3", "masks")
                    else:
                        after(pe, f"a_turned{h - 1}")
                    for n in range(AG):
                        head = n * AM + h
                        mm(ps[4][:, n * P:(n + 1) * P], q_a[:, head, 0:P], k_a[:, head, 0:P], start=True, stop=True)
                        dst = ps[5][:, n * T:(n + 1) * T] if n < 2 else ps[6][:, 0:T]
                        ins = mm(dst, q_a[:, head, P:T], k_a[:, head, :], start=True, stop=True)
                    event(ins, f"a_score{h}")
                if s in M_TURN_AT:
                    h = M_TURN_AT.index(s)
                    if h == 0:
                        after(pe, "h_m")
                        evacuated(pe, 19)
                    else:
                        after(pe, "a_turned3")
                    for k in range(KB):
                        for t in range(TT):
                            ins = tr(hm_bank(h, k)[:, t * P:(t + 1) * P],
                                     h_m[:, t, (KB * h + k) * P:(KB * h + k + 1) * P], ident[:])
                    event(ins, f"hm_t{h}")
                if s in FFN_COL_AT:
                    pe.wait_ge(ada_done, ada_count(ADA_FIRST + ADA_REST - 1))
                    after(pe, "a_turned3")
                    m = FFN_COL_AT.index(s)
                    for k in range(KT):
                        ins = mm(ps[6][:, KT * m + k:KT * m + k + 1], mod[:, 1 + m, k * P:(k + 1) * P], ones[:, 0:1],
                                 start=True, stop=True)
                    if m == 1:
                        event(ins, "ffn_col")
                if s == SHIFT_LOGIT_AT:
                    after(pe, "rw_scaled", "a_out3")
                    for k in range(KT):
                        ins = mm(ps[7][:, 0:NE], ffn_col[:, 0, k:k + 1].broadcast_to([P, P]), rw[:, k, :],
                                 start=(k == 0), stop=(k == KT - 1))
                    event(ins, "shift_logit")
                if s in BCAST_AT:
                    i = BCAST_AT[s]
                    after(pe, *(("hm_lo1",) if i == 0 else ("logit_shift",)))
                    for n in range(2):
                        ins = mm(ps[4 + 2 * (i % 2) + n][:], ones[:], mod[:, i, n * NB:(n + 1) * NB], start=True, stop=True)
                    event(ins, f"bcast{i}")
                if s == LAST_BLOCK[25] + 1:
                    after(pe, "x1_0", "mod0")
                    for t in range(TT):
                        for k in range(KB):
                            ins = tr(ps[4 + t][:, k * P:(k + 1) * P], x_res[:, t, k * P:(k + 1) * P], ident[:])
                    event(ins, "x1_turn0")

            def logits(t, h):
                for k in range(KB):
                    ins = mm(ps[0][:, t * NE:(t + 1) * NE], x_res_t[h][:, k, t * P:(t + 1) * P], rw_scaled[:, KB * h + k, :],
                             start=(t == 0 and h == 0 and k == 0), stop=(h == 1 and k == KB - 1), skip_group_check=True)
                return ins

            evacuated(pe, 25)
            after(pe, "x1_turned0", "mod3")
            for t in range(TT):
                logits(t, 0)
            for t in range(TT):
                after(pe, f"x1_1_t{t}")
                for k in range(KB):
                    ins = tr(ps[6 + t][:, k * P:(k + 1) * P], x_res[:, t, NB + k * P:NB + (k + 1) * P], ident[:])
                event(ins, f"x1_turn1_t{t}")
            for t in range(TT):
                after(pe, f"x1_turned1_t{t}")
                ins = logits(t, 1)
            event(ins, "logits")
            after(pe, "zero", "logits_all")
            evacuated(pe, 26)
            for b in range(3):
                mm(ps[b][:], zeros[:, 0:P], zeros[:], start=True, stop=False, skip_group_check=True)
            after(pe, "picked")
            pe.wait_ge(consts_ready, 6)
            pick = rt[:, 9]
            mm(ps[4][:, 0:NE], tri_lt, pick[:, 0, :], start=True, stop=True)
            mm(ps[4][:, NE:2 * NE], ones[:], pick[:, 0, :], start=True, stop=False)
            mm(ps[4][:, NE:2 * NE], tri_lt, pick[:, 1, :], start=False, stop=True)
            mm(ps[4][:, 2 * NE:3 * NE], ones[:], pick[:, 0, :], start=True, stop=False)
            event(mm(ps[4][:, 2 * NE:3 * NE], ones[:], pick[:, 1, :], start=False, stop=True), "rank_sums")
            mm(ps[3][:], zeros[:, 0:P], zeros[:], start=True, stop=False, skip_group_check=True)

            def turn_slots():
                for t in range(TT):
                    tr(ps[6][:, t * P:(t + 1) * P], onehot[:, t, :], ident[:])
                for t in range(TT):
                    ins = mm(ps[6][:, T:T + 2], onehot[:, t, :], w_pair[:, t, :], start=(t == 0), stop=(t == TT - 1))
                ins.then_inc(slots_turned, 1)

            def gather(j):
                for k in range(KB):
                    for t in range(TT):
                        ins = mm(ps[5 + 2 * j][:, k * P:(k + 1) * P], x_hat[:, t, (KB * j + k) * P:(KB * j + k + 1) * P],
                                 onehot[:, t, :], start=(t == 0), stop=(t == TT - 1))
                ins.then_inc(gathered, 1)

            def scatter(side, t):
                for h in range(2):
                    ins = mm(ps[2 * t + h][:], scat[side][:, t * P:(t + 1) * P], y_e[:, h * NB:(h + 1) * NB],
                             start=False, stop=False, skip_group_check=True)
                return ins

            def chunk(i, q, matrix, m, k):
                c = len(PAIR_CHUNKS) * q + PAIR_CHUNKS.index((matrix, m))
                pe.wait_ge(ring_loaded[c % CHUNKS], 32 * (3 * BODY // CHUNKS) * i + 32 * (c // CHUNKS + 1))
                return ring[c % CHUNKS][:].rearrange("p (k n) -> p k n", k=k)

            def gate_up(i, q, s):
                w_gate, w_up = chunk(i, q, "gate", s, KT), chunk(i, q, "up", s, KT)
                up, gate = ps[4 + s][64 * s:64 * s + 64, :], ps[4 + s][64 * (1 - s):64 * (1 - s) + 64, :]
                for k in range(KT):
                    x = xe_t[:, k, s * SLOTS:(s + 1) * SLOTS]
                    mm(gate, x, w_gate[:, k, :], start=(k == 0), stop=(k == KT - 1))
                    ins = mm(up, x, w_up[:, k, :], start=(k == 0), stop=(k == KT - 1))
                    if k == KT // 2 - 1:
                        ins.then_inc(gate_up_half, 1)
                ins.then_inc(gate_up_done, 1)

            def turn_he(n, s):
                pe.wait_ge(he_ready, n + (s + 1))
                half = slice(64 * s, 64 * s + 64)
                for k in range(FF // P):
                    ins = mm(ps[6 - s][:, k * SLOTS:(k + 1) * SLOTS], he[half, k * P:(k + 1) * P], ident[half, half],
                             start=True, stop=True)
                ins.then_inc(he_turned, 1)

            def down(i, q, n, s):
                pe.wait_ge(he_t_ready, n + (s + 1))
                w_down = chunk(i, q, "down", s, FF // P)
                for k in range(FF // P):
                    for h in range(2):
                        ins = mm(ps[7 if s == 0 else 4][64 * h:64 * h + 64, :], he_t[:, s, k, :], w_down[:, k, h * NB:(h + 1) * NB],
                                 start=(k == 0), stop=(k == FF // P - 1))
                ins.then_inc(down_done, 1)

            def work_pair(i, q):
                p, n = BODY // 2 * i + q, BODY * i + 2 * q
                pe.wait_ge(onehot_ready, p + 1)
                gather(0)
                pe.wait_ge(y_ready, n + 1)
                gather(1)
                turn_slots()
                scatter((q + 1) % 2, 0)
                pe.wait_ge(xe_ready, 2 * p + 2)
                gate_up(i, q, 0)
                gate_up(i, q, 1)
                turn_he(n, 0)
                scatter((q + 1) % 2, 1)
                turn_he(n, 1)
                down(i, q, n, 0)
                down(i, q, n, 1)

            after(pe, "x_hat")
            with pe.Fori(0, NE // BODY) as i:
                for q in range(BODY // 2):
                    work_pair(i, q)
            after(pe, "many")
            again = pe.value_load(many_i[0:1, 0:1], min_val=0, max_val=1)
            with pe.If(again == 1):
                with pe.Fori(NE // BODY, VISITS * NE // BODY) as i:
                    for q in range(BODY // 2):
                        work_pair(i, q)
                pe.wait_ge(y_ready, VISITS * NE + 1)
            pe.wait_ge(y_ready, NE + 1)
            for t in range(TT):
                scatter(1, t).then_inc(moe_done, 1)


_INS = ["x", "c", "ada_w", "ada_b", "w_in", "mlstm_conv", "mlstm_gate_b", "mlstm_norm_g", "w_branch_m", "w_branch_a",
        "w_out", "router_w", "router_b", "w_gate_e", "w_up_e", "w_down_e", "norm_mix_g", "norm_ffn_g", "final_norm_g"]
_OUTS = [((1, 256, 1024), "float32")]


def kernel(**inputs):
    import numpy as _np
    import concourse.bacc as _bacc
    from concourse import mybir as _mybir
    from concourse.bass_utils import run_bass_kernel_spmd as _run

    nc = _bacc.Bacc("TRN2", target_bir_lowering=False, num_devices=1)
    arrays, aps = {}, {}
    for name in _INS:
        a = _np.ascontiguousarray(inputs[name])
        arrays[f"in_{name}_dram"] = a
        aps[name] = nc.dram_tensor(f"in_{name}_dram", a.shape, _mybir.dt.from_np(a.dtype), kind="ExternalInput").ap()
    shape, dtype = _OUTS[0]
    out = nc.dram_tensor("out_0_dram", shape, _mybir.dt.from_np(_np.dtype(dtype)), kind="ExternalOutput").ap()
    build(nc, aps, out)
    r = _run(nc, [arrays], core_ids=[0])
    return r.results[0]["out_0_dram"]
```
